# Optimizing a Trainium2 kernel written in Bass

```python
import math
import jax, jax.numpy as jnp
from jax import lax
import numpy as np

D_MODEL = 1024
BATCH = 1
SEQ = 512
DEPTH = 2

N_MIXERS = 2
EXPAND = 2
D_INNER = EXPAND * D_MODEL
EPS = 1e-6
GLA_HEADS = 4
GLA_KEY_DIM = D_MODEL // 2
GLA_DK = GLA_KEY_DIM // GLA_HEADS
GLA_DV = D_INNER // GLA_HEADS
GLA_GATE_RANK = 16
GLA_GATE_TAU = 16.0
GLA_CHUNK = 64
GLA_IN = 2 * GLA_KEY_DIM + 2 * D_INNER + GLA_GATE_RANK
S5_GROUP = 16
S5_GROUPS = D_INNER // S5_GROUP
S5_STATE = 64
S5_DT_MIN = 1e-3
S5_DT_MAX = 1e-1
S5_IN = 2 * D_INNER
N_GLA = (DEPTH + 1) // 2
N_S5 = DEPTH // 2


def _rmsnorm(x, g):
    x32 = x.astype(jnp.float32)
    y = x32 * lax.rsqrt(jnp.mean(x32 * x32, axis=-1, keepdims=True) + EPS) * g.astype(jnp.float32)
    return y.astype(x.dtype)

def _gla_mixer(h, w_in, w_gate_up, b_gate, head_gain, w_out):
    bsz, seqlen, _ = h.shape
    n_chunks = seqlen // GLA_CHUNK
    f32 = jnp.float32
    proj = h @ w_in
    q, k, v, z, r = jnp.split(
        proj,
        [GLA_KEY_DIM, 2 * GLA_KEY_DIM, 2 * GLA_KEY_DIM + D_INNER, 2 * GLA_KEY_DIM + 2 * D_INNER],
        axis=-1)
    log_a = jax.nn.log_sigmoid((r @ w_gate_up + b_gate).astype(f32)) / GLA_GATE_TAU

    def to_chunks(t, d):
        return t.astype(f32).reshape(bsz, n_chunks, GLA_CHUNK, GLA_HEADS, d).transpose(0, 3, 1, 2, 4)

    qc = to_chunks(q, GLA_DK) * (GLA_DK ** -0.5)
    kc = to_chunks(k, GLA_DK)
    vc = to_chunks(v, GLA_DV)
    bcum = jnp.cumsum(to_chunks(log_a, GLA_DK), axis=3)
    b_last = bcum[:, :, :, -1:, :]

    q_g = qc * jnp.exp(bcum)
    k_g = kc * jnp.exp(-bcum)
    k_end = kc * jnp.exp(b_last - bcum)

    causal = jnp.tril(jnp.ones((GLA_CHUNK, GLA_CHUNK), dtype=bool))
    att = jnp.einsum('bhncd,bhnsd->bhncs', q_g, k_g)
    att = jnp.where(causal, att, 0.0)
    o_intra = jnp.einsum('bhncs,bhnse->bhnce', att, vc)

    kv_chunk = jnp.einsum('bhnsd,bhnse->bhnde', k_end, vc)
    decay_chunk = jnp.exp(b_last[:, :, :, 0, :])

    def step(state, inp):
        dec, kv = inp
        return dec[..., None] * state + kv, state

    s0 = jnp.zeros((bsz, GLA_HEADS, GLA_DK, GLA_DV), f32)
    _, s_prev = lax.scan(step, s0, (jnp.moveaxis(decay_chunk, 2, 0), jnp.moveaxis(kv_chunk, 2, 0)))
    s_prev = jnp.moveaxis(s_prev, 0, 2)
    o = o_intra + jnp.einsum('bhncd,bhnde->bhnce', q_g, s_prev)

    o = o.transpose(0, 2, 3, 1, 4).reshape(bsz, seqlen, GLA_HEADS, GLA_DV)
    o = o * lax.rsqrt(jnp.mean(o * o, axis=-1, keepdims=True) + EPS) * head_gain.astype(f32)
    o = o.reshape(bsz, seqlen, D_INNER) * jax.nn.silu(z.astype(f32))
    return o.astype(h.dtype) @ w_out

def _s5_mixer(h, w_in, lam_re, lam_im, log_dt, b_re, b_im, c_re, c_im, d_skip, w_glu, b_glu, w_out):
    bsz, seqlen, _ = h.shape
    f32 = jnp.float32
    proj = h @ w_in
    u, z = jnp.split(proj, [D_INNER], axis=-1)
    u32 = u.astype(f32).reshape(bsz, seqlen, S5_GROUPS, S5_GROUP)

    lam = lax.complex(lam_re.astype(f32), lam_im.astype(f32))
    dt = jnp.exp(log_dt.astype(f32))[:, None]
    lam_bar = jnp.exp(lam * dt)
    b_coef = (lam_bar - 1.0) / lam
    b_cplx = lax.complex(b_re.astype(f32), b_im.astype(f32))
    b_bar = b_coef[..., None] * b_cplx
    bu = lax.complex(jnp.einsum('blgi,gpi->blgp', u32, jnp.real(b_bar)),
                     jnp.einsum('blgi,gpi->blgp', u32, jnp.imag(b_bar)))
    a = jnp.broadcast_to(lam_bar[None, None], (1, seqlen, S5_GROUPS, S5_STATE))

    def combine(left, right):
        a_l, b_l = left
        a_r, b_r = right
        return a_l * a_r, a_r * b_l + b_r

    _, states = lax.associative_scan(combine, (a, bu), axis=1)
    y = (jnp.einsum('blgp,gip->blgi', jnp.real(states), c_re.astype(f32))
         - jnp.einsum('blgp,gip->blgi', jnp.imag(states), c_im.astype(f32)))
    y = y + d_skip.astype(f32) * u32
    y = jax.nn.gelu(y.reshape(bsz, seqlen, D_INNER))
    y = y * jax.nn.sigmoid(y @ w_glu.astype(f32) + b_glu.astype(f32))
    y = y * jax.nn.silu(z.astype(f32))
    return y.astype(h.dtype) @ w_out

def first_inputs(seed: int = 0) -> dict:
    key = jax.random.key(seed)
    ks = jax.random.split(key, 24)
    nrm = jax.random.normal
    f32 = jnp.float32
    x = nrm(ks[0], (BATCH, SEQ, D_MODEL), f32)
    gla_norm = 1.0 + 0.01 * nrm(ks[1], (N_GLA, D_MODEL), f32)
    gla_w_in = nrm(ks[2], (N_GLA, D_MODEL, GLA_IN), f32) * D_MODEL ** -0.5
    gla_w_gate_up = nrm(ks[3], (N_GLA, GLA_GATE_RANK, GLA_KEY_DIM), f32) * GLA_GATE_RANK ** -0.5
    gla_b_gate = 0.1 * nrm(ks[4], (N_GLA, GLA_KEY_DIM), f32)
    gla_head_gain = 1.0 + 0.01 * nrm(ks[5], (N_GLA, GLA_DV), f32)
    gla_w_out = nrm(ks[6], (N_GLA, D_INNER, D_MODEL), f32) * D_INNER ** -0.5
    s5_norm = 1.0 + 0.01 * nrm(ks[7], (N_S5, D_MODEL), f32)
    s5_w_in = nrm(ks[8], (N_S5, D_MODEL, S5_IN), f32) * D_MODEL ** -0.5
    s5_lam_re = -0.5 + 1e-3 * nrm(ks[9], (N_S5, S5_GROUPS, S5_STATE), f32)
    s5_lam_im = (math.pi * jnp.arange(S5_STATE, dtype=f32))[None, None, :] \
        + 1e-3 * nrm(ks[10], (N_S5, S5_GROUPS, S5_STATE), f32)
    s5_log_dt = jax.random.uniform(ks[11], (N_S5, S5_GROUPS), f32,
                                   minval=math.log(S5_DT_MIN), maxval=math.log(S5_DT_MAX))
    s5_b_re = nrm(ks[12], (N_S5, S5_GROUPS, S5_STATE, S5_GROUP), f32) * (2 * S5_GROUP) ** -0.5
    s5_b_im = nrm(ks[13], (N_S5, S5_GROUPS, S5_STATE, S5_GROUP), f32) * (2 * S5_GROUP) ** -0.5
    s5_c_re = nrm(ks[14], (N_S5, S5_GROUPS, S5_GROUP, S5_STATE), f32) * S5_STATE ** -0.5
    s5_c_im = nrm(ks[15], (N_S5, S5_GROUPS, S5_GROUP, S5_STATE), f32) * S5_STATE ** -0.5
    s5_d = nrm(ks[16], (N_S5, S5_GROUPS, S5_GROUP), f32)
    s5_w_glu = nrm(ks[17], (N_S5, D_INNER, D_INNER), f32) * D_INNER ** -0.5
    s5_b_glu = 0.01 * nrm(ks[18], (N_S5, D_INNER), f32)
    s5_w_out = nrm(ks[19], (N_S5, D_INNER, D_MODEL), f32) * D_INNER ** -0.5
    final_norm = 1.0 + 0.01 * nrm(ks[20], (D_MODEL,), f32)
    return {
        "x": x,
        "gla_norm": gla_norm, "gla_w_in": gla_w_in, "gla_w_gate_up": gla_w_gate_up,
        "gla_b_gate": gla_b_gate, "gla_head_gain": gla_head_gain, "gla_w_out": gla_w_out,
        "s5_norm": s5_norm, "s5_w_in": s5_w_in, "s5_lam_re": s5_lam_re, "s5_lam_im": s5_lam_im,
        "s5_log_dt": s5_log_dt, "s5_b_re": s5_b_re, "s5_b_im": s5_b_im,
        "s5_c_re": s5_c_re, "s5_c_im": s5_c_im, "s5_d": s5_d,
        "s5_w_glu": s5_w_glu, "s5_b_glu": s5_b_glu, "s5_w_out": s5_w_out,
        "final_norm": final_norm,
    }

def first_block(x, gla_norm, gla_w_in, gla_w_gate_up, gla_b_gate, gla_head_gain, gla_w_out,
              s5_norm, s5_w_in, s5_lam_re, s5_lam_im, s5_log_dt, s5_b_re, s5_b_im,
              s5_c_re, s5_c_im, s5_d, s5_w_glu, s5_b_glu, s5_w_out, final_norm):
    for i in range(DEPTH):
        j = i // N_MIXERS
        if i % N_MIXERS == 0:
            h = _rmsnorm(x, gla_norm[j])
            out = _gla_mixer(h, gla_w_in[j], gla_w_gate_up[j], gla_b_gate[j],
                             gla_head_gain[j], gla_w_out[j])
        else:
            h = _rmsnorm(x, s5_norm[j])
            out = _s5_mixer(h, s5_w_in[j], s5_lam_re[j], s5_lam_im[j], s5_log_dt[j],
                            s5_b_re[j], s5_b_im[j], s5_c_re[j], s5_c_im[j], s5_d[j],
                            s5_w_glu[j], s5_b_glu[j], s5_w_out[j])
        x = x + out.astype(x.dtype)
    return _rmsnorm(x, final_norm)


DEPTH_2 = 1

N_META = 16
ROPE_THETA = 10000.0
BLOCK_Q = 128
MLA_HEADS = 8
MLA_Q_RANK = 256
MLA_KV_RANK = 128
MLA_NOPE_DIM = 64
MLA_ROPE_DIM = 32
MLA_QK_DIM = MLA_NOPE_DIM + MLA_ROPE_DIM
MLA_V_DIM = 64
DSA_HEADS = 8
DSA_HEAD_DIM = 64
IDX_HEADS = 8
IDX_DIM = 64
TOPK_MAX = 256
MIX_WIDTH = MLA_HEADS * MLA_V_DIM + DSA_HEADS * DSA_HEAD_DIM
IN_SIZES = (MLA_Q_RANK, MLA_KV_RANK, MLA_ROPE_DIM,
            DSA_HEADS * DSA_HEAD_DIM, DSA_HEADS * DSA_HEAD_DIM, DSA_HEADS * DSA_HEAD_DIM,
            IDX_HEADS * IDX_DIM, IDX_DIM, IDX_HEADS)
C_IN = sum(IN_SIZES)
D_FF_RAW = -(-8 * D_MODEL // 3)
D_FF = -(-D_FF_RAW // 256) * 256


def rmsnorm(x, g):
    x32 = x.astype(jnp.float32)
    y = x32 * lax.rsqrt(jnp.mean(x32 * x32, axis=-1, keepdims=True) + EPS)
    return (y * g.astype(jnp.float32)).astype(x.dtype)

def rope(x, pos):
    half = x.shape[-1] // 2
    inv = jnp.power(ROPE_THETA, -jnp.arange(half, dtype=jnp.float32) / half)
    ang = pos.astype(jnp.float32)[:, None] * inv[None, :]
    cos = jnp.cos(ang)[:, None, :]
    sin = jnp.sin(ang)[:, None, :]
    x32 = x.astype(jnp.float32)
    x1, x2 = x32[..., :half], x32[..., half:]
    return jnp.concatenate([x1 * cos - x2 * sin, x2 * cos + x1 * sin], axis=-1).astype(x.dtype)

def to_blocks(a):
    b, tp = a.shape[0], a.shape[1]
    return a.reshape((b, tp // BLOCK_Q, BLOCK_Q) + a.shape[2:]).swapaxes(0, 1)

def from_blocks(a):
    a = a.swapaxes(0, 1)
    return a.reshape((a.shape[0], a.shape[1] * a.shape[2]) + a.shape[3:])

def causal_block_attention(q, k, v):
    tp = q.shape[1]
    scale = q.shape[-1] ** -0.5
    kpos = jnp.arange(tp)

    def one_block(args):
        qb, blk = args
        qpos = blk * BLOCK_Q + jnp.arange(BLOCK_Q)
        s = jnp.einsum('bqhd,bkhd->bhqk', qb, k, preferred_element_type=jnp.float32) * scale
        s = jnp.where((kpos[None, :] <= qpos[:, None])[None, None], s, -jnp.inf)
        p = jax.nn.softmax(s, axis=-1).astype(v.dtype)
        return jnp.einsum('bhqk,bkhd->bqhd', p, v)

    out = lax.map(one_block, (to_blocks(q), jnp.arange(tp // BLOCK_Q)))
    return from_blocks(out)

def indexed_sparse_attention(q, k, v, q_idx, k_idx, w_idx, topk):
    tp = q.shape[1]
    scale = q.shape[-1] ** -0.5
    idx_scale = IDX_DIM ** -0.5
    kpos = jnp.arange(tp)

    def one_block(args):
        qb, qib, wib, blk = args
        qpos = blk * BLOCK_Q + jnp.arange(BLOCK_Q)
        causal = kpos[None, :] <= qpos[:, None]
        logits = jnp.einsum('bqhd,bkd->bqhk', qib, k_idx, preferred_element_type=jnp.float32) * idx_scale
        score = jnp.einsum('bqh,bqhk->bqk', wib.astype(jnp.float32), jax.nn.relu(logits))
        score = jnp.where(causal[None], score, -jnp.inf)
        _, sel = lax.top_k(score, topk)
        valid = sel <= qpos[None, :, None]
        k_sel = jax.vmap(lambda kb, ib: kb[ib])(k, sel)
        v_sel = jax.vmap(lambda vb, ib: vb[ib])(v, sel)
        s = jnp.einsum('bqhd,bqkhd->bhqk', qb, k_sel, preferred_element_type=jnp.float32) * scale
        s = jnp.where(valid[:, None], s, -jnp.inf)
        p = jax.nn.softmax(s, axis=-1).astype(v.dtype)
        return jnp.einsum('bhqk,bqkhd->bqhd', p, v_sel)

    out = lax.map(one_block, (to_blocks(q), to_blocks(q_idx), to_blocks(w_idx), jnp.arange(tp // BLOCK_Q)))
    return from_blocks(out)

def hybrid_mixer(u, pos, topk, w_in, q_norm_g, w_uq, kv_norm_g, w_ukv, w_o):
    b, tp, _ = u.shape
    proj = u @ w_in
    splits = [int(v) for v in np.cumsum(IN_SIZES)[:-1]]
    c_q, c_kv, k_r, q_s, k_s, v_s, q_i, k_i, w_i = jnp.split(proj, splits, axis=-1)

    q = (rmsnorm(c_q, q_norm_g) @ w_uq).reshape(b, tp, MLA_HEADS, MLA_QK_DIM)
    q_mla = jnp.concatenate([q[..., :MLA_NOPE_DIM], rope(q[..., MLA_NOPE_DIM:], pos)], axis=-1)
    kv = (rmsnorm(c_kv, kv_norm_g) @ w_ukv).reshape(b, tp, MLA_HEADS, MLA_NOPE_DIM + MLA_V_DIM)
    k_rope = rope(k_r[:, :, None, :], pos)
    k_mla = jnp.concatenate([kv[..., :MLA_NOPE_DIM],
                             jnp.broadcast_to(k_rope, (b, tp, MLA_HEADS, MLA_ROPE_DIM))], axis=-1)
    v_mla = kv[..., MLA_NOPE_DIM:]
    o_mla = causal_block_attention(q_mla, k_mla, v_mla)

    q_s = rope(q_s.reshape(b, tp, DSA_HEADS, DSA_HEAD_DIM), pos)
    k_s = rope(k_s.reshape(b, tp, DSA_HEADS, DSA_HEAD_DIM), pos)
    v_s = v_s.reshape(b, tp, DSA_HEADS, DSA_HEAD_DIM)
    q_i = rope(q_i.reshape(b, tp, IDX_HEADS, IDX_DIM), pos)
    k_i = rope(k_i[:, :, None, :], pos)[:, :, 0, :]
    w_i = w_i * (IDX_HEADS ** -0.5)
    o_dsa = indexed_sparse_attention(q_s, k_s, v_s, q_i, k_i, w_i, topk)

    o = jnp.concatenate([o_mla.reshape(b, tp, MLA_HEADS * MLA_V_DIM),
                         o_dsa.reshape(b, tp, DSA_HEADS * DSA_HEAD_DIM)], axis=-1)
    return o @ w_o

def swiglu(u, w_gate, w_up, w_down):
    return (jax.nn.silu(u @ w_gate) * (u @ w_up)) @ w_down

def second_inputs(seed: int = 0) -> dict:
    key = jax.random.key(seed)
    ks = jax.random.split(key, 16)
    f32 = jnp.float32

    def w(k, shape, fan_in):
        return jax.random.normal(k, shape, f32) * (fan_in ** -0.5)

    def g(k, shape):
        return 1.0 + 0.02 * jax.random.normal(k, shape, f32)

    return {
        'x': jax.random.normal(ks[0], (BATCH, SEQ, D_MODEL), f32),
        'meta_tokens': jax.random.normal(ks[1], (N_META, D_MODEL), f32),
        'attn_norm_g': g(ks[2], (DEPTH_2, D_MODEL)),
        'w_in': w(ks[3], (DEPTH_2, D_MODEL, C_IN), D_MODEL),
        'mla_q_norm_g': g(ks[4], (DEPTH_2, MLA_Q_RANK)),
        'w_uq': w(ks[5], (DEPTH_2, MLA_Q_RANK, MLA_HEADS * MLA_QK_DIM), MLA_Q_RANK),
        'mla_kv_norm_g': g(ks[6], (DEPTH_2, MLA_KV_RANK)),
        'w_ukv': w(ks[7], (DEPTH_2, MLA_KV_RANK, MLA_HEADS * (MLA_NOPE_DIM + MLA_V_DIM)), MLA_KV_RANK),
        'w_o': w(ks[8], (DEPTH_2, MIX_WIDTH, D_MODEL), MIX_WIDTH),
        'ffn_norm_g': g(ks[9], (DEPTH_2, D_MODEL)),
        'w_gate': w(ks[10], (DEPTH_2, D_MODEL, D_FF), D_MODEL),
        'w_up': w(ks[11], (DEPTH_2, D_MODEL, D_FF), D_MODEL),
        'w_down': w(ks[12], (DEPTH_2, D_FF, D_MODEL), D_FF),
        'final_norm_g': g(ks[13], (D_MODEL,)),
    }

def second_block(x, meta_tokens, attn_norm_g, w_in, mla_q_norm_g, w_uq, mla_kv_norm_g, w_ukv, w_o,
              ffn_norm_g, w_gate, w_up, w_down, final_norm_g):
    b, seq, _ = x.shape
    topk = min(TOPK_MAX, seq // 4)
    meta = jnp.broadcast_to(meta_tokens[None].astype(x.dtype), (b, N_META, D_MODEL))
    h = jnp.concatenate([meta, x], axis=1)
    t = h.shape[1]
    tp = -(-t // BLOCK_Q) * BLOCK_Q
    h = jnp.pad(h, ((0, 0), (0, tp - t), (0, 0)))
    pos = jnp.arange(tp, dtype=jnp.int32)
    for l in range(DEPTH_2):
        h = h + hybrid_mixer(rmsnorm(h, attn_norm_g[l]), pos, topk, w_in[l], mla_q_norm_g[l], w_uq[l],
                             mla_kv_norm_g[l], w_ukv[l], w_o[l])
        h = h + swiglu(rmsnorm(h, ffn_norm_g[l]), w_gate[l], w_up[l], w_down[l])
    h = rmsnorm(h, final_norm_g)
    return h[:, N_META:t]


def setup_inputs(seed=0):
    out = dict(first_inputs(seed))
    for name, value in second_inputs(seed + 1).items():
        if name != "x":
            out[name + "_2"] = value
    return out


def reference(
    x, gla_norm, gla_w_in, gla_w_gate_up, gla_b_gate, gla_head_gain, gla_w_out, s5_norm,
    s5_w_in, s5_lam_re, s5_lam_im, s5_log_dt, s5_b_re, s5_b_im, s5_c_re, s5_c_im, s5_d,
    s5_w_glu, s5_b_glu, s5_w_out, final_norm, meta_tokens_2, attn_norm_g_2, w_in_2,
    mla_q_norm_g_2, w_uq_2, mla_kv_norm_g_2, w_ukv_2, w_o_2, ffn_norm_g_2, w_gate_2, w_up_2,
    w_down_2, final_norm_g_2,
):
    x = first_block(
        x, gla_norm, gla_w_in, gla_w_gate_up, gla_b_gate, gla_head_gain, gla_w_out, s5_norm,
        s5_w_in, s5_lam_re, s5_lam_im, s5_log_dt, s5_b_re, s5_b_im, s5_c_re, s5_c_im, s5_d,
        s5_w_glu, s5_b_glu, s5_w_out, final_norm,
    )
    return second_block(
        x, meta_tokens_2, attn_norm_g_2, w_in_2, mla_q_norm_g_2, w_uq_2, mla_kv_norm_g_2,
        w_ukv_2, w_o_2, ffn_norm_g_2, w_gate_2, w_up_2, w_down_2, final_norm_g_2,
    )


_drawn_inputs = setup_inputs


def setup_inputs(seed=0):
    import zlib

    import numpy as np

    out = dict(_drawn_inputs(seed))
    spreads = {}
    factors = {'gla_norm': 3.199,
     'gla_head_gain': 5.782,
     's5_norm': 8.0,
     's5_lam_re': 8.0,
     's5_log_dt': 2.708,
     's5_b_re': 3.427,
     's5_b_im': 3.424,
     's5_c_re': 3.442,
     's5_c_im': 3.415,
     's5_b_glu': 8.0,
     'final_norm': 3.691,
     'attn_norm_g_2': 3.568,
     'mla_q_norm_g_2': 8.0,
     'mla_kv_norm_g_2': 8.0,
     'ffn_norm_g_2': 3.735,
     'final_norm_g_2': 2.783}
    for name, (base, spread) in spreads.items():
        noise = np.random.default_rng([zlib.crc32(name.encode()), seed]).standard_normal(out[name].shape)
        drawn = base * np.exp(spread * noise) if base else spread * noise
        out[name] = __import__('jax').numpy.asarray(drawn.astype(out[name].dtype))
    for name, factor in factors.items():
        out[name] = (out[name] * factor).astype(out[name].dtype)
    return out
```

```python
import math
from contextlib import ExitStack

import numpy as np

import concourse.bass as bass
from concourse import mybir

F32 = mybir.dt.float32
I32 = mybir.dt.int32
U32 = mybir.dt.uint32
ALU = mybir.AluOpType
ACT = mybir.ActivationFunctionType
AX_X = mybir.AxisListType.X

P = 128
T = 512
D = 1024
KD = D // P
EPS = 1e-6
GH, GDK, GDV, GCH, GRANK, GTAU = 4, 128, 512, 64, 16, 16.0
DI = 2 * D
KI = DI // P
G_Q, G_K, G_V, G_Z, G_R = 0, 512, 1024, 3072, 5120
NPAIR = T // P
NCH = T // GCH
SG, SGRP, SP_ = 128, 16, 64
TB = 8
NB = T // TB
BG = 8
NBATCH = SG // BG
NM = 16
T2 = T + NM
HALF = T2 // 2
TPAD = 640
MH, MQR, MKR, MNOPE, MROPE, MV = 8, 256, 128, 64, 32, 64
MQK = MNOPE + MROPE
DH, DHD = 8, 64
TOPK = 128
FF = 2816
KF = FF // P
A_CQ, A_CKV, A_KR, A_QS, A_KS, A_VS, A_QI, A_KI, A_WI, A_END = 0, 256, 384, 416, 928, 1440, 1952, 2464, 2528, 2536
LOW = -1e30
TAKEN = -3e38
ROUND = 12582912.0
A_MIN = -9.0

SLOT = 2048
NSLOT = 4

C_ID, C_ONE, C_SM, C_NM, C_NI, C_SG, C_NSG, C_EPS, C_HPI, C_N = 0, 128, 256, 768, 832, 896, 897, 898, 899, 900
C_GM, C_RST = 0, 512
R_C, R_S, R_MC, R_MS, R_P, R_MP, C_CB, R_N = 0, 528, 1056, 1584, 2112, 2240, 2368, 2896
PV_GLA, PV_BG, PV_HG, PV_S5, PV_BGLU, PV_DS, PV_FIN, PV_ATT, PV_GQ, PV_GKV, PV_FFN, PV_FIN2, PV_N = \
    0, 8, 12, 16, 24, 40, 56, 64, 72, 74, 75, 83, 91


def shape_constants():
    c = np.zeros((P, C_N), np.float32)
    r = np.arange(P)
    c[:, C_ID:C_ID + P] = np.eye(P)
    c[:, C_ONE:C_ONE + P] = 1.0
    m = (r[:, None] // SGRP) <= (r[None, :] // SGRP)
    c[:, C_SM:C_SM + T] = np.tile(m, (1, 4))
    c[:, C_NM:C_NM + NB] = (np.arange(NB) != 0)[None, :]
    c[:, C_NI:C_NI + NB] = np.arange(NB)[None, :]
    c[:, C_SG] = np.where(r < SP_, 1.0, -1.0)
    c[:, C_NSG] = -c[:, C_SG]
    c[:, C_EPS] = EPS
    c[:, C_HPI] = math.pi / 2
    return c


def chunk_constants():
    c = np.zeros((P, 2 * T), np.float32)
    r = np.arange(P)
    m = (r[:, None] <= r[None, :]) & (r[:, None] // GCH == r[None, :] // GCH)
    c[:, C_GM:C_GM + T] = np.tile(m, (1, NPAIR))
    c[:, C_RST:C_RST + T] = (np.arange(T) % GCH != 0)[None, :]
    return c


def rotary_constants():
    c = np.zeros((P, R_N), np.float32)
    r = np.arange(P)
    c[:, C_CB + T2 - P:C_CB + T2] = np.where(r[None, :] <= r[:, None], 0.0, LOW)
    pos = np.arange(T2, dtype=np.float32)
    for width, rows, oc, os, op in ((DHD, range(P), R_C, R_S, R_P), (MROPE, range(MNOPE, MQK), R_MC, R_MS, R_MP)):
        half = width // 2
        inv = np.power(np.float32(10000.0), -np.arange(half, dtype=np.float32) / np.float32(half)).astype(np.float32)
        for r in rows:
            d = r % width if width == DHD else r - MNOPE
            ang = pos * inv[d % half]
            c[r, oc:oc + T2] = np.cos(ang)
            c[r, os:os + T2] = np.sin(ang) * (-1.0 if d < half else 1.0)
            c[r - d + (d + half) % width, op + r] = 1.0
    return c


class Tile:

    def __init__(self, t, loads):
        self.t, self.loads, self.slot = t, loads, t % 2


class Plan:

    def __init__(self):
        self.loads, self.tiles, self.last_use, self.value = [], {}, [], []
        self.n, self.count = 0, [0] * NSLOT

    def load(self, *parts):
        n = len(self.loads)
        self.loads.append(parts)
        self.count[n % NSLOT] += 16 * len(parts)
        self.value.append(self.count[n % NSLOT])
        self.last_use.append(None)
        return n

    def tile(self, stage, *loads):
        t = Tile(self.n, loads)
        self.n += 1
        self.tiles.setdefault(stage, []).append(t)
        for n in loads:
            self.last_use[n] = t.t
        return t


def build(nc, a, out):
    w1 = a["gla_w_in"][0].rearrange("(k p) m -> p k m", p=P)
    wo1 = a["gla_w_out"][0].rearrange("(k p) m -> p k m", p=P)
    w2 = a["s5_w_in"][0].rearrange("(k p) m -> p k m", p=P)
    wg2 = a["s5_w_glu"][0].rearrange("(k p) m -> p k m", p=P)
    wo2 = a["s5_w_out"][0].rearrange("(k p) m -> p k m", p=P)
    w3 = a["w_in_2"][0].rearrange("(k p) m -> p k m", p=P)
    wuq = a["w_uq_2"][0].rearrange("(k p) m -> p k m", p=P)
    wukv = a["w_ukv_2"][0]
    wo3 = a["w_o_2"][0].rearrange("(k p) m -> p k m", p=P)
    wga = a["w_gate_2"][0].rearrange("(k p) m -> p k m", p=P)
    wup = a["w_up_2"][0].rearrange("(k p) m -> p k m", p=P)
    wdn = a["w_down_2"][0].rearrange("(k p) m -> p k m", p=P)

    plan = Plan()

    def pairs(stage, w, c0, n):
        for m in range(0, n, 2):
            ld = plan.load((w[:, :, c0 + m * P:c0 + (m + 2) * P], 0, (KD, 2 * P)))
            plan.tile(stage, ld)
            plan.tile(stage, ld)

    def singles(stage, w, n):
        for m in range(n):
            plan.tile(stage, plan.load((w[:, :, m * P:(m + 1) * P], 0, (KI, P))))

    def token_major(stage, w, c0, n, tiles):
        for m in range(n):
            lds = [plan.load((w[:, 4 * j:4 * j + 4, c0 + m * T:c0 + (m + 1) * T], 0, (4, T))) for j in range(2)]
            for _ in range(tiles):
                plan.tile(stage, *lds)

    pairs("gla_q", w1, G_Q, 4)
    pairs("gla_k", w1, G_K, 4)
    plan.tile("gla_r", plan.load((w1[:, :, G_R + GRANK - P:G_R + GRANK], 0, (KD, P))))
    token_major("gla_v", w1, G_V, 4, 2)
    pairs("gla_z", w1, G_Z, KI)
    singles("gla_out", wo1, KD)
    pairs("s5_u", w2, 0, KI)
    pairs("s5_z", w2, DI, KI)
    singles("s5_glu", wg2, KI)
    singles("s5_out", wo2, KD)
    pairs("cq", w3, A_CQ, 2)
    ld = plan.load((w3[:, :, A_CKV:A_QS], 0, (KD, A_QS - A_CKV)))
    plan.tile("ckv", ld)
    plan.tile("kr", ld)
    pairs("qs", w3, A_QS, 4)
    pairs("ks", w3, A_KS, 4)
    pairs("qi", w3, A_QI, 4)
    ld = plan.load((w3[:, :, A_KI:A_WI], 0, (KD, P), slice(0, 64)), (w3[:, :, A_KI:A_WI], 0, (KD, P), slice(64, P)),
                   (w3[:, :, A_WI:A_END], KD * P, (KD, 8)))
    plan.tile("ki", ld)
    plan.tile("wi", ld)
    token_major("vs", w3, A_VS, 1, 3)
    ld = plan.load((wuq, 0, (2, MH * MQK)))
    for _ in range(MH):
        plan.tile("uq", ld)
    ld = plan.load((wukv, 0, (MH * P,)))
    for _ in range(MH):
        plan.tile("ukn", ld)
    for _ in range(3):
        plan.tile("ukvv", ld)
    pairs("attn_out", wo3, 0, KD)
    for m in range(KF):
        ld = plan.load((wga[:, :, m * P:(m + 1) * P], 0, (KD, P)), (wup[:, :, m * P:(m + 1) * P], KD * P, (KD, P)))
        plan.tile("ffn_up", ld)
    for m in range(KD):
        plan.tile("ffn_down", *[plan.load((wdn[:, 11 * j:11 * j + 11, m * P:(m + 1) * P], 0, (11, P))) for j in range(2)])
    tiles = plan.tiles

    NORMS = {}
    norm_at = [0, 0]
    for name, k in (("gla", KD), *[(f"head{h}", 4) for h in range(GH)], ("s5", KD), ("fin", KD), ("attn", KD),
                    ("cq", 2), ("ckv", 1), ("ffn", KD), ("fin2", KD)):
        NORMS[name] = (norm_at[0], norm_at[1], k)
        norm_at[0] += k
        norm_at[1] += 1

    with ExitStack() as ctx:
        base = nc.sbuf_base
        base = base() if callable(base) else base
        base = (base + 63) // 64 * 64
        top = [base]
        ends = []

        def place(name, shape, at=None, dt=F32):
            size = int(np.prod(shape[1:])) * 4
            off = (top[0] if at is None else at) + 31 & -32
            t = nc.alloc_sbuf_tensor_at(name, list(shape), dt, offset=off)
            if at is None:
                top[0] = off + size
            ends.append(off + size)
            return t, off + size

        def keep(name, shape, dt=F32):
            return place(name, shape, None, dt)[0]

        ring = keep("ring", [P, NSLOT, SLOT])
        con = keep("con", [P, C_N])
        pv = keep("pv", [P, PV_N])
        pvr_off = top[0] + 31 & -32
        pvr = keep("pvr", [P, 2 * P])
        sq = keep("sq", [P, 2, T2])
        rs = keep("rs", [P, T2])
        sg2pi = keep("sg2pi", [P, 8])
        xt_off = top[0] + 31 & -32
        XT = keep("XT", [P, KD, T])
        lo = top[0]

        o = lo
        HT, o = place("HT", [P, KD, T], o)
        QG, o = place("QG", [P, GH, T], o)
        KG, o = place("KG", [P, GH, T], o)
        LA, o = place("LA", [P, GH, T], o)
        KE, o = place("KE", [P, NPAIR, GH * GDK], o)
        V, o = place("V", [P, NPAIR, DI], o)
        O, o_end = place("O", [P, KI, T], o)
        xtok, _ = place("xtok", [P, NPAIR, D], o)
        dec, o = place("dec", [P, GH, NCH], o_end)
        gcon, o = place("gcon", [P, 2 * T], o)
        SZ, o = place("SZ", [P, 2, T], o)
        o_tmp = o
        WG, o = place("WG", [P, T], o)
        R16, o = place("R16", [P, T], o)
        la_e, o = place("la_e", [P, T], o)
        ex_p, o = place("ex_p", [P, T], o)
        ex_n, o = place("ex_n", [P, T], o)
        kend, o = place("kend", [P, GH, T], o)
        S, o = place("S", [P, 3, GH * GDV], o_tmp)
        ATT = LA

        o = lo
        _, o = place("HT_", [P, KD, T], o)
        U, o = place("U", [P, KI, T], o)
        Z, o = place("Z", [P, KI, T], o)
        s5_lo = o
        PW, o = place("PW", [P, 6, TB, SG], o)
        Bt, o = place("Bt", [P, BG, TB * SGRP], o)
        Bn, o = place("Bn", [P, BG, TB * SGRP], o)
        KM = Bn
        W1, o = place("W1", [P, BG, TB * SGRP], o)
        W2, o = place("W2", [P, BG, TB * SGRP], o)
        w_tmp, o = place("w_tmp", [P, BG, TB * SGRP], o)
        M12, o = place("M12", [P, 2, T], o)
        b_tmp = M12[:].rearrange("p a b -> p (a b)").rearrange("p (g m) -> p g m", g=BG)
        rot_c, o = place("rot_c", [P, T], o)
        rot_s, o = place("rot_s", [P, T], o)
        dk, o = place("dk", [P, T], o)
        UB, o = place("UB", [P, BG, NB], o)
        CN, o = place("CN", [P, 2, 3 * SP_], o)
        BZ, o = place("BZ", [P, 2, 2, BG, SGRP], o)
        CZ, o = place("CZ", [P, 2, P], o)
        WB, o = place("WB", [P, BG, 3 * SP_], o)
        o = s5_lo + 4 * 6 * TB * SG
        glr, o = place("glr", [P, SP_], o)
        gli, o = place("gli", [P, SP_], o)
        gdt, o = place("gdt", [P, 8], o)
        gt, o = place("gt", [P, 16, SP_], o)
        gi, o = place("gi", [P, SP_], o, I32)
        TPg, o = place("TPg", [P, 8, P], o)
        PT, o = place("PT", [P, 8, P], o)
        ctmp, o = place("ctmp", [P, 2, P], o)
        r8f8, _ = place("r8f8", [P, 2, P], pvr_off)
        YB, YIN = sq[:, 0, 0:T], sq[:, 1, 0:T]

        o = lo
        X2, o = place("X2", [P, KD, T2], o)
        U2, o = place("U2", [P, KD, TPAD], o)
        att_lo = o
        Km, o = place("Km", [P, MH, T2], o)
        Qm, o = place("Qm", [P, MH, T], o)
        Vm, o = place("Vm", [P, 5, MH * MV], o)
        QS, o = place("QS", [P, 4, T], o)
        KS, o = place("KS", [P, 4, T2], o)
        VS, o = place("VS", [P, 5, DH * DHD], o)
        KI_, o = place("KI_", [P, T2], o)
        WI, o = place("WI", [P, NPAIR, 8], o)
        rt, o = place("rt", [P, R_N], o)
        OA, _ = place("OA", [P, KD, T], o)
        CQ, o = place("CQ", [P, 2, T], o)
        CK, o = place("CK", [P, TPAD], o)
        KR, o = place("KR", [P, T2], o)
        ro, o = place("ro", [P, 2, T2], o)
        MT, o = place("MT", [P, D], lo + 4 * KD * (T2 + TPAD))
        o = xt_off
        QI, o = place("QI", [P, 4, T], o)
        RL, o = place("RL", [P, 2, T2], o)
        acc, o = place("acc", [P, T2], o)
        top8, o = place("top8", [P, 8], o)
        o = lo + 4 * KD * T2
        PB, o = place("PB", [P, 2, TPAD], o)
        PT2, o = place("PT2", [P, 2, TPAD], o)
        selb, o = place("selb", [P, T2], o)
        mx, o = place("mx", [P, 2, 8], o)
        HF, o = place("HF", [P, KF, T], att_lo)
        SF, o = place("SF", [P, 2, T], o)
        OT, o = place("OT", [P, NPAIR, D], o)

        PS = ctx.enter_context(nc.psum_tensor("PS", [P, 4, 512], F32))
        PA = ctx.enter_context(nc.psum_tensor("PA", [P, 4, 512], F32))

        def sem(name):
            return ctx.enter_context(nc.semaphore(name))

        landed = [sem(f"landed{i}") for i in range(NSLOT)]
        tile_done = sem("tile_done")
        slot_free = [sem("slot_free0"), sem("slot_free1")]
        con_in, pv_in, x_in, wg_in, out_done = sem("con_in"), sem("pv_in"), sem("x_in"), sem("wg_in"), sem("out_done")
        pv_ps, pv_sb = sem("pv_ps"), sem("pv_sb")
        xT_ps, xT_sb = sem("xT_ps"), sem("xT_sb")
        sq_ready, sq_used, sum_ready, std_ready, rstd_ready, normed = (
            sem("sq_ready"), sem("sq_used"), sem("sum_ready"), sem("std_ready"), sem("rstd_ready"), sem("normed"))
        act_chain, dve_chain, pool_chain = sem("act_chain"), sem("dve_chain"), sem("pool_chain")
        wg_zero, gate_ps, gate_ev, gl_ready, la_ready, ex_ready, de_ready, kx_ready, qkg_ready, ke_ready = (
            sem("wg_zero"), sem("gate_ps"), sem("gate_ev"), sem("gl_ready"), sem("la_ready"), sem("ex_ready"),
            sem("de_ready"), sem("kx_ready"), sem("qkg_ready"), sem("ke_ready"))
        keT_ps, keT_sb, att_ps, att_sb, kv_ps, S_ready, o_ps, o_sb = (
            sem("keT_ps"), sem("keT_sb"), sem("att_ps"), sem("att_sb"), sem("kv_ps"), sem("S_ready"), sem("o_ps"), sem("o_sb"))
        oz_ready = sem("oz_ready")
        par_in, gx_ready, tp_ready, pt_ps, pt_sb, pw_ready, sin_ready = (
            sem("par_in"), sem("gx_ready"), sem("tp_ready"), sem("pt_ps"), sem("pt_sb"), sem("pw_ready"), sem("sin_ready"))
        u_out, ub_in, y_out, y_in = sem("u_out"), sem("ub_in"), sem("y_out"), sem("y_in")
        small_in = [sem("small_in0"), sem("small_in1")]
        c_ps, cz_sb, bt_ready, b_ps, wb_sb, w_ready, k_ps, km_ready, v_ps, m_ready, y_ps, y_sb = (
            sem("c_ps"), sem("cz_sb"), sem("bt_ready"), sem("b_ps"), sem("wb_sb"), sem("w_ready"), sem("k_ps"),
            sem("km_ready"), sem("v_ps"), sem("m_ready"), sem("y_ps"), sem("y_sb"))
        frac_ready, rot_ready, dk_ready, rot_used, yd_ready, gelu_done = (
            sem("frac_ready"), sem("rot_ready"), sem("dk_ready"), sem("rot_used"), sem("yd_ready"), sem("gelu_done"))

        ident = con[:, C_ID:C_ID + P]
        ones = con[:, C_ONE:C_ONE + P]

        def read_out(eng, tile):
            eng.wait_ge(slot_free[tile.slot], tile.t // 2 + 1)

        mt_in, mt_ps, mt_sb, rt_in, pad_zero = sem("mt_in"), sem("mt_ps"), sem("mt_sb"), sem("rt_in"), sem("pad_zero")
        ro_ps, ro_read, roped, kr_copied, pb_zero = sem("ro_ps"), sem("ro_read"), sem("roped"), sem("kr_copied"), sem("pb_zero")
        score_ps, score_free, relu_ready, acc_used, max_ready, exp_ready, rsum_ready, p_ready = (
            sem("score_ps"), [sem("score_free0"), sem("score_free1")], sem("relu_ready"), sem("acc_used"), sem("max_ready"),
            sem("exp_ready"), sem("rsum_ready"), sem("p_ready"))
        pT_ps, pT_sb, pv_out_ps, oa_ready = sem("pT_ps"), sem("pT_sb"), sem("pv_out_ps"), sem("oa_ready")
        silu_ready, ot_ps, ot_sb = sem("silu_ready"), sem("ot_ps"), sem("ot_sb")

        def keys(i):
            return NM + (i + 1) * P

        def scores(pair, i):
            n = keys(i)
            return PA[:, 2 * pair:2 * pair + 1, 0:n] if n <= 512 else PA[:, 2 * pair:2 * pair + 2, 0:n // 2]

        def split(ap, i):
            n = keys(i)
            return ap.rearrange("p (h n) -> p h n", h=1 if n <= 512 else 2)

        def rotations(stage):
            if stage == "qs":
                return [(QS[:, j, :], 0, P, NM, R_C, tiles["qs"][j]) for j in range(4)]
            if stage == "ks":
                return [(KS[:, j, :], 0, P, 0, R_C, tiles["ks"][j]) for j in range(4)]
            if stage == "qi":
                return [(QI[:, j, :], 0, P, NM, R_C, tiles["qi"][j]) for j in range(4)]
            if stage == "k1":
                return [(KI_[:], 0, P, 0, R_C, tiles["ki"][0]), (KR[:], MNOPE, MQK, 0, R_MC, tiles["kr"][0])]
            return [(Qm[:, h, :], MNOPE, MQK, NM, R_MC, tiles["uq"][h]) for h in range(MH)]

        ROT_STAGES = ("qs", "ks", "qi", "k1", "qm")
        ROT_AT = {"qs": 0, "ks": 4, "qi": 8, "k1": 12, "qm": 14}

        UNITS = []
        for i in range(NPAIR):
            UNITS += [("idx", i, h) for h in range(8)] + [("mla", i, h) for h in range(MH)] + [("dsa", i, h) for h in range(DH)]

        u_dram = nc.dram_tensor("u_by_block", (DI, T), F32, kind="Internal").ap()
        y_dram = nc.dram_tensor("y_by_block", (DI, T), F32, kind="Internal").ap()
        TWO_PI = 6.283185

        def by_block(ap):
            return ap.rearrange("p (n s) -> p s n", s=TB)

        def sn(ap):
            return ap.rearrange("p (s n) -> p s n", s=TB)

        def slot_view(n, shape, at=0):
            size = int(np.prod(shape))
            v = ring[:, n % NSLOT, at:at + size]
            return v.rearrange("p (k m) -> p k m", k=shape[0]) if len(shape) == 2 else v

        def halves(ap, width):
            return ap.rearrange("p (h n) -> p h n", h=2)

        def pe_program(pe):
            def open_tile(tile, kth=0):
                n = tile.loads[kth]
                pe.wait_ge(landed[n % NSLOT], plan.value[n])
                if kth == 0 and tile.t >= 2:
                    pe.wait_ge(slot_free[tile.slot], tile.t // 2)

            def feature_tile(tile, weights, rhs, nk, width=T, rows=P):
                open_tile(tile)
                for k in range(nk):
                    if width == T:
                        m = pe.matmul(PS[0:rows, 2 * tile.slot, 0:T], weights(k), rhs(k), start=k == 0, stop=k == nk - 1)
                    else:
                        for h in range(2):
                            m = pe.matmul(PS[0:rows, 2 * tile.slot + h, 0:HALF], weights(k), rhs(k)[:, h * HALF:(h + 1) * HALF],
                                          start=k == 0, stop=k == nk - 1)
                m.then_inc(tile_done, 1)

            def pair_stage(stage, rhs, width=T):
                for i, tile in enumerate(tiles[stage]):
                    w = slot_view(tile.loads[0], (KD, 2 * P))
                    feature_tile(tile, lambda k: w[:, k, (i % 2) * P:(i % 2 + 1) * P], rhs, KD, width)

            def single_stage(stage, rhs, before=None):
                for i, tile in enumerate(tiles[stage]):
                    w = slot_view(tile.loads[0], (KI, P))
                    feature_tile(tile, lambda k: w[:, k, :], rhs, KI)

            def norm(name, width):
                s0, n0, k = NORMS[name]
                if n0 > 0:
                    pe.wait_ge(std_ready, n0)
                for i in range(k):
                    pe.wait_ge(sq_ready, s0 + i + 1)
                    for h in range(2):
                        m = pe.matmul(PA[:, h, 0:width // 2], ones, sq[:, (s0 + i) % 2, h * (width // 2):(h + 1) * (width // 2)],
                                      start=i == 0, stop=i == k - 1)
                    m.then_inc(sq_used, 1)
                m_last = m
                return m_last

            pe.wait_ge(con_in, 32)
            pe.wait_ge(pv_in, 16 * 12)
            pe.transpose(PS[:, 0, 0:PV_N], pvr[0:PV_N, 0:P], con[0:PV_N, C_ID:C_ID + PV_N]).then_inc(pv_ps, 1)
            pe.wait_ge(x_in, 16)
            for k in range(KD):
                if k >= 4:
                    pe.wait_ge(xT_sb, k - 3)
                for tt in range(NPAIR):
                    m = pe.transpose(PA[:, k % 4, tt * P:(tt + 1) * P], xtok[:, tt, k * P:(k + 1) * P], ident)
                m.then_inc(xT_ps, 1)
            pe.wait_ge(xT_sb, KD)
            norm("gla", T)
            pe.wait_ge(normed, NORMS["gla"][0] + KD)
            pair_stage("gla_q", lambda k: HT[:, k, :])
            pair_stage("gla_k", lambda k: HT[:, k, :])
            w = slot_view(tiles["gla_r"][0].loads[0], (KD, P))
            feature_tile(tiles["gla_r"][0], lambda k: w[:, k, :], lambda k: HT[:, k, :], KD)
            pe.wait_ge(wg_in, 16)
            read_out(pe, tiles["gla_r"][0])
            for h in range(GH):
                pe.matmul(PA[:, h, :], WG[:, h * P:(h + 1) * P], R16[:], start=True, stop=True).then_inc(gate_ps, 1)
            for i, tile in enumerate(tiles["gla_v"]):
                for j in range(2):
                    open_tile(tile, j) if j == 0 else pe.wait_ge(landed[tile.loads[1] % NSLOT], plan.value[tile.loads[1]])
                    w = slot_view(tile.loads[j], (4, T))
                    for b in range(2):
                        tt = (i % 2) * 2 + b
                        for k in range(4):
                            m = pe.matmul(PS[:, 2 * tile.slot + b, :], HT[:, 4 * j + k, tt * P:(tt + 1) * P], w[:, k, :],
                                          start=j == 0 and k == 0, stop=j == 1 and k == 3)
                m.then_inc(tile_done, 1)
            for h in range(GH):
                pe.wait_ge(gate_ev, h + 1)
                pe.wait_ge(ke_ready, h + 1)
                for tt in range(NPAIR):
                    m = pe.transpose(PA[:, h, tt * P:(tt + 1) * P], kend[:, h, tt * P:(tt + 1) * P], ident)
                m.then_inc(keT_ps, 1)
            for h in range(GH):
                pe.wait_ge(qkg_ready, h + 1)
                pe.wait_ge(keT_sb, h + 1)
                for tt in range(NPAIR):
                    s = slice(tt * P, (tt + 1) * P)
                    m = pe.matmul(PA[:, h, s], KG[:, h, s], QG[:, h, s], start=True, stop=True)
                m.then_inc(att_ps, 1)
            read_out(pe, tiles["gla_v"][-1])
            read_out(pe, tiles["gla_v"][-2])
            pe.wait_ge(att_sb, GH)
            nkv = no = 0
            for tt in range(NPAIR):
                for c in (2 * tt, 2 * tt + 1):
                    if c == NCH - 1:
                        continue
                    for h in range(GH):
                        if nkv >= 2:
                            pe.wait_ge(S_ready, nkv - 1)
                        r = slice((c % 2) * GCH, (c % 2) * GCH + GCH)
                        pe.matmul(PA[:, nkv % 2, :], KE[r, tt, h * P:(h + 1) * P], V[r, tt, h * GDV:(h + 1) * GDV],
                                  start=True, stop=True).then_inc(kv_ps, 1)
                        nkv += 1
                for h in range(GH):
                    if no >= 2:
                        pe.wait_ge(o_sb, no - 1)
                    pe.wait_ge(S_ready, GH * 2 * tt + h + 1)
                    for e in range(4):
                        dst = PA[:, 2 + no % 2, e * P:(e + 1) * P]
                        es = slice(h * GDV + e * P, h * GDV + (e + 1) * P)
                        for c in (2 * tt, 2 * tt + 1):
                            r = slice((c % 2) * GCH, (c % 2) * GCH + GCH)
                            m = pe.matmul(dst[:, r], V[:, tt, es], ATT[:, h, c * GCH:(c + 1) * GCH], start=True, stop=c == 0)
                            if c > 0:
                                m = pe.matmul(dst[:, r], S[:, (c - 1) % 3, es], QG[:, h, c * GCH:(c + 1) * GCH],
                                              start=False, stop=True)
                    m.then_inc(o_ps, 1)
                    no += 1
            for h in range(GH):
                norm(f"head{h}", T)
            pair_stage("gla_z", lambda k: HT[:, k, :])
            pe.wait_ge(oz_ready, KI)
            single_stage("gla_out", lambda k: O[:, k, :])
            norm("s5", T)
            pe.wait_ge(tp_ready, 1)
            for i in range(8):
                m = pe.transpose(PA[:, 2 + i // 4, (i % 4) * P:(i % 4 + 1) * P], TPg[:, i, :], ident)
            m.then_inc(pt_ps, 1)
            pe.wait_ge(normed, NORMS["s5"][0] + KD)
            pair_stage("s5_u", lambda k: HT[:, k, :])
            pe.wait_ge(std_ready, NORMS["s5"][1] + 1)
            pe.wait_ge(pt_sb, 1)
            for b in range(NBATCH):
                pe.wait_ge(small_in[b % 2], 16 * 7 * (b // 2 + 1))
                if b > 0:
                    pe.wait_ge(y_sb, b)
                pe.transpose(PA[:, 0, 0:P], CN[:, b % 2, 0:P], ident)
                pe.transpose(PA[:, 0, P:2 * P], CN[:, b % 2, SP_:SP_ + P], ident).then_inc(c_ps, 1)
                tile = tiles["s5_z"][b]
                w = slot_view(tile.loads[0], (KD, 2 * P))
                feature_tile(tile, lambda k: w[:, k, (b % 2) * P:(b % 2 + 1) * P], lambda k: HT[:, k, :], KD)
                pe.wait_ge(bt_ready, 2 * b + 1)
                if b > 0:
                    pe.wait_ge(rot_used, b)
                for g in range(BG):
                    m = pe.transpose(PA[:, 1 + g // 4, (g % 4) * P:(g % 4 + 1) * P], Bt[:, g, :], ident)
                m.then_inc(b_ps, 1)
                pe.wait_ge(bt_ready, 2 * b + 2)
                pe.wait_ge(w_ready, 2 * b + 1)
                pe.wait_ge(cz_sb, b + 1)
                if b > 0:
                    pe.wait_ge(km_ready, 2 * b)
                for g in range(BG):
                    m = pe.matmul(PA[:, 3 * (g // 4), (g % 4) * P:(g % 4 + 1) * P], Bn[:, g, :], W1[:, g, :], start=True, stop=True)
                    if g % 4 == 3:
                        m.then_inc(k_ps, 1)
                pe.wait_ge(wb_sb, b + 1)
                pe.wait_ge(ub_in, 16 * TB * (b + 1))
                for h in range(2):
                    for g in range(BG):
                        m = pe.matmul(PA[:, 1 + h, g * NB:(g + 1) * NB], WB[:, g, h * SP_:h * SP_ + P], UB[:, g, :],
                                      start=True, stop=True)
                m.then_inc(v_ps, 1)
                pe.wait_ge(km_ready, 2 * b + 2)
                pe.wait_ge(w_ready, 2 * b + 2)
                pe.wait_ge(m_ready, 2 * b + 2)
                for g in range(BG):
                    n0 = g * NB
                    pe.matmul(PA[:, 0, n0:n0 + NB], KM[:, g, :], UB[:, g, :], start=True, stop=False)
                    pe.matmul(PA[:, 0, n0 + 1:n0 + NB], W1[:, g, :], M12[:, 0, n0:n0 + NB - 1], start=False, stop=False)
                    m = pe.matmul(PA[:, 0, n0 + 1:n0 + NB], W2[:, g, :], M12[:, 1, n0:n0 + NB - 1], start=False, stop=True)
                m.then_inc(y_ps, 1)
            pe.wait_ge(gelu_done, KI)
            single_stage("s5_glu", lambda k: U[:, k, :])
            for tile in tiles["s5_glu"][-2:]:
                read_out(pe, tile)
            pe.wait_ge(oz_ready, 2 * KI)
            single_stage("s5_out", lambda k: Z[:, k, :])
            norm("fin", T)
            pe.wait_ge(mt_in, 16)
            for k in range(KD):
                m = pe.transpose(PA[:, 2, k * NM:(k + 1) * NM], MT[0:NM, k * P:(k + 1) * P], con[0:NM, C_ID:C_ID + NM])
            m.then_inc(mt_ps, 1)
            norm("attn", T2)
            pe.wait_ge(normed, NORMS["attn"][0] + KD)
            pe.wait_ge(std_ready, NORMS["attn"][1] + 1)
            pair_stage("cq", lambda k: U2[:, k, NM:T2])
            w = slot_view(tiles["ckv"][0].loads[0], (KD, A_QS - A_CKV))
            feature_tile(tiles["ckv"][0], lambda k: w[:, k, 0:P], lambda k: U2[:, k, 0:T2], KD, T2)
            feature_tile(tiles["kr"][0], lambda k: w[:, k, A_KR - A_CKV - MNOPE:A_KR - A_CKV + MROPE], lambda k: U2[:, k, 0:T2], KD, T2, MQK)
            pair_stage("qs", lambda k: U2[:, k, NM:T2])
            norm("cq", T)
            norm("ckv", T2)
            pe.wait_ge(std_ready, NORMS["ckv"][1] + 1)
            pe.wait_ge(rt_in, 16)

            def rotate(stage):
                for j, (x, lo_row, hi_row, t0, c, tile) in enumerate(rotations(stage)):
                    n = ROT_AT[stage] + j
                    read_out(pe, tile)
                    if n >= 2:
                        pe.wait_ge(ro_read, n - 1)
                    width = T2 - t0
                    rows = P if hi_row == P else MQK
                    perm = rt[0:rows, (R_P if hi_row == P else R_MP):(R_P if hi_row == P else R_MP) + rows]
                    for h in range(2):
                        m = pe.matmul(PA[0:rows, 2 * (n % 2) + h, 0:width // 2], perm, x[0:rows, h * (width // 2):(h + 1) * (width // 2)],
                                      start=True, stop=True)
                    m.then_inc(ro_ps, 1)

            pair_stage("ks", lambda k: U2[:, k, 0:T2], T2)
            rotate("qs")
            pair_stage("qi", lambda k: U2[:, k, NM:T2])
            rotate("ks")
            w = slot_view(tiles["ki"][0].loads[0], (KD, P))
            feature_tile(tiles["ki"][0], lambda k: w[:, k, :], lambda k: U2[:, k, 0:T2], KD, T2)
            tile = tiles["wi"][0]
            open_tile(tile)
            wi = ring[:, tile.loads[0] % NSLOT, KD * P:KD * (P + 8)].rearrange("p (k m) -> p k m", k=KD)
            for i in range(NPAIR):
                for k in range(KD):
                    m = pe.matmul(PS[:, 2 * tile.slot, i * 8:(i + 1) * 8], U2[:, k, NM + i * P:NM + (i + 1) * P], wi[:, k, :],
                                  start=k == 0, stop=k == KD - 1)
            m.then_inc(tile_done, 1)
            rotate("qi")
            for i, tile in enumerate(tiles["vs"]):
                for j in range(2):
                    open_tile(tile) if j == 0 else pe.wait_ge(landed[tile.loads[1] % NSLOT], plan.value[tile.loads[1]])
                    w = slot_view(tile.loads[j], (4, T))
                    for b in range(2 if i < 2 else 1):
                        t0 = (2 * i + b) * P
                        for k in range(4):
                            m = pe.matmul(PS[:, 2 * tile.slot + b, :], U2[:, 4 * j + k, t0:t0 + P], w[:, k, :],
                                          start=j == 0 and k == 0, stop=j == 1 and k == 3)
                m.then_inc(tile_done, 1)
            pe.wait_ge(normed, NORMS["ckv"][0] + 1)
            w = slot_view(tiles["uq"][0].loads[0], (2, MH * MQK))
            for h, tile in enumerate(tiles["uq"]):
                feature_tile(tile, lambda k: w[:, k, h * MQK:(h + 1) * MQK], lambda k: CQ[:, k, :], 2, T, MQK)
            rotate("k1")
            w = slot_view(tiles["ukn"][0].loads[0], (MH * P,))
            for h, tile in enumerate(tiles["ukn"]):
                feature_tile(tile, lambda k: w[:, h * P:(h + 1) * P], lambda k: CK[:, 0:T2], 1, T2)
            wv = w.rearrange("p (h m) -> p h m", h=MH)[:, :, MNOPE:P]
            for i, tile in enumerate(tiles["ukvv"]):
                open_tile(tile)
                for b in range(2 if i < 2 else 1):
                    t0 = (2 * i + b) * P
                    m = pe.matmul(PS[:, 2 * tile.slot + b, :], CK[:, t0:t0 + P], wv, start=True, stop=True)
                m.then_inc(tile_done, 1)
            rotate("qm")

            pe.wait_ge(roped, 22)
            pe.wait_ge(kr_copied, MH)
            for tile in tiles["ukvv"][-2:]:
                read_out(pe, tile)
            att_n = 0
            pending = []

            def close_unit():
                n, kind, i, h = pending.pop(0)
                pair = n % 2
                pe.wait_ge(p_ready, n + 1)
                if n >= 2:
                    pe.wait_ge(oa_ready, n - 1)
                for j in range(i + 2):
                    m = pe.transpose(PS[:, 2 * pair + j // 4, (j % 4) * P:(j % 4 + 1) * P], PB[:, pair, j * P:(j + 1) * P], ident)
                m.then_inc(pT_ps, 1)
                pe.wait_ge(pT_sb, n + 1)
                vals = Vm if kind == "mla" else VS
                for j in range(i + 2):
                    m = pe.matmul(PS[:, 2 * pair + 1, 2 * P:3 * P], vals[:, j, (h // 2) * P:(h // 2 + 1) * P],
                                  PT2[:, pair, j * P:(j + 1) * P], start=j == 0, stop=j == i + 1)
                m.then_inc(pv_out_ps, 1)

            for n, (kind, i, h) in enumerate(UNITS):
                if n >= 2:
                    pe.wait_ge(score_free[n % 2], n // 2)
                nk = keys(i)
                dst = scores(n % 2, i)
                r = slice((h % 2) * 64, (h % 2) * 64 + 64)
                qs = slice(i * P, (i + 1) * P)
                for b in range(dst.shape[1]):
                    w = nk // dst.shape[1]
                    ks = slice(b * w, (b + 1) * w)
                    if kind == "idx":
                        m = pe.matmul(dst[:, b, :], QI[r, h // 2, qs], KI_[r, ks], start=True, stop=True)
                    elif kind == "mla":
                        m = pe.matmul(dst[:, b, :], Qm[0:MQK, h, qs], Km[0:MQK, h, ks], start=True, stop=True)
                    else:
                        m = pe.matmul(dst[:, b, :], QS[r, h // 2, qs], KS[r, h // 2, ks], start=True, stop=True)
                m.then_inc(score_ps, 1)
                if kind != "idx":
                    pending.append((att_n, kind, i, h))
                    att_n += 1
                    if len(pending) == 2:
                        close_unit()
                    if n + 1 == len(UNITS) or UNITS[n + 1][0] == "idx":
                        while pending:
                            close_unit()
            pe.wait_ge(oa_ready, att_n)
            pair_stage("attn_out", lambda k: OA[:, k, :])
            norm("ffn", T)
            pe.wait_ge(normed, NORMS["ffn"][0] + KD)
            for i, tile in enumerate(tiles["ffn_up"]):
                open_tile(tile)
                w = slot_view(tile.loads[0], (2 * KD, P))
                for b in range(2):
                    for k in range(KD):
                        m = pe.matmul(PS[:, 2 * tile.slot + b, :], w[:, b * KD + k, :], U2[:, k, 0:T], start=k == 0, stop=k == KD - 1)
                m.then_inc(tile_done, 1)
            for tile in tiles["ffn_up"][-2:]:
                read_out(pe, tile)
            for tile in tiles["ffn_down"]:
                for j in range(2):
                    open_tile(tile) if j == 0 else pe.wait_ge(landed[tile.loads[1] % NSLOT], plan.value[tile.loads[1]])
                    w = slot_view(tile.loads[j], (11, P))
                    for k in range(11):
                        m = pe.matmul(PS[:, 2 * tile.slot, :], w[:, k, :], HF[:, 11 * j + k, :], start=j + k == 0, stop=j == 1 and k == 10)
                m.then_inc(tile_done, 1)
            norm("fin2", T)
            pe.wait_ge(normed, NORMS["fin2"][0] + KD)
            pe.wait_ge(std_ready, NORMS["fin2"][1] + 1)
            for tt in range(NPAIR):
                if tt >= 2:
                    pe.wait_ge(ot_sb, tt - 1)
                for k in range(KD):
                    m = pe.transpose(PA[:, 2 * (tt % 2) + k // 4, (k % 4) * P:(k % 4 + 1) * P], U2[:, k, tt * P:(tt + 1) * P], ident)
                m.then_inc(ot_ps, 1)

        def act_program(act):
            chain = [0]

            def link(ins):
                chain[0] += 1
                ins.then_inc(act_chain, 1)
                act.wait_ge(act_chain, chain[0])

            def norm(name, src, width, dim):
                s0, n0, k = NORMS[name]
                for i in range(k):
                    if s0 + i >= 2:
                        act.wait_ge(sq_used, s0 + i - 1)
                    act.activation(sq[:, (s0 + i) % 2, 0:width], src(i), ACT.Square).then_inc(sq_ready, 1)
                act.wait_ge(sq_used, s0 + k)
                if n0 > 0:
                    act.wait_ge(normed, s0)
                act.activation(rs[:, 0:width].rearrange("p (h n) -> p h n", h=2), PA[:, 0:2, 0:width // 2], ACT.Sqrt,
                               scale=1.0 / dim, bias=con[:, C_EPS:C_EPS + 1]).then_inc(std_ready, 1)

            def evac(tile, dst, func=ACT.Copy, ready=None, rows=P, **kw):
                act.wait_ge(tile_done, tile.t + 1)
                return act.activation(dst, PS[0:rows, 2 * tile.slot, 0:T], func, **kw).then_inc(slot_free[tile.slot], 1)

            act.dma_start(con[:], a["shape_constants"]).then_inc(con_in, 16)
            act.dma_start(gcon[:], a["chunk_constants"]).then_inc(con_in, 16)
            act.wait_ge(pv_ps, 1)
            act.activation(pv[:], PS[:, 0, 0:PV_N], ACT.Copy).then_inc(pv_sb, 1)
            for k in range(KD):
                act.wait_ge(xT_ps, k + 1)
                act.activation(XT[:, k, :], PA[:, k % 4, :], ACT.Copy).then_inc(xT_sb, 1)
            act.wait_ge(xT_sb, KD)
            norm("gla", lambda k: XT[:, k, :], T, D)
            for i, tile in enumerate(tiles["gla_q"]):
                evac(tile, QG[:, i, :])
            for i, tile in enumerate(tiles["gla_k"]):
                evac(tile, KG[:, i, :])
            tile = tiles["gla_r"][0]
            evac(tile, R16[:])
            act.wait_ge(pv_sb, 1)
            for h in range(GH):
                act.wait_ge(gate_ps, h + 1)
                link(act.activation(LA[:, h, :], PA[:, h, :], ACT.Identity, bias=pv[:, PV_BG + h:PV_BG + h + 1]))
                act.nop().then_inc(gate_ev, 1)
                if h > 0:
                    act.wait_ge(la_ready, h)
                link(act.activation(la_e[:], LA[:, h, :], ACT.Abs))
                link(act.activation(la_e[:], la_e[:], ACT.Exp, scale=-1.0))
                act.activation(la_e[:], la_e[:], ACT.Ln, bias=con[:, C_ONE:C_ONE + 1]).then_inc(gl_ready, 1)
                act.wait_ge(la_ready, h + 1)
                if h > 0:
                    act.wait_ge(qkg_ready, h)
                act.activation(ex_p[:], LA[:, h, :], ACT.Exp, scale=1.0 / GTAU).then_inc(ex_ready, 1)
                act.activation(ex_n[:], LA[:, h, :], ACT.Exp, scale=-1.0 / GTAU).then_inc(ex_ready, 1)
                act.wait_ge(de_ready, h + 1)
                act.activation(kend[:, h, :], kend[:, h, :], ACT.Exp, scale=1.0 / GTAU).then_inc(kx_ready, 1)
            for i, tile in enumerate(tiles["gla_v"]):
                act.wait_ge(tile_done, tile.t + 1)
                tt = (i % 2) * 2
                act.activation(V[:, tt:tt + 2, (i // 2) * T:(i // 2 + 1) * T], PS[:, 2 * tile.slot:2 * tile.slot + 2, :], ACT.Copy)\
                    .then_inc(slot_free[tile.slot], 1)
            for h in range(GH):
                act.wait_ge(keT_ps, h + 1)
                act.activation(KE[:, :, h * P:(h + 1) * P], PA[:, h, :].rearrange("p (t d) -> p t d", t=NPAIR), ACT.Copy)\
                    .then_inc(keT_sb, 1)
            n = 0
            for tt in range(NPAIR):
                for h in range(GH):
                    act.wait_ge(o_ps, n + 1)
                    act.activation(O[:, 4 * h:4 * h + 4, tt * P:(tt + 1) * P],
                                   PA[:, 2 + n % 2, :].rearrange("p (e c) -> p e c", e=4), ACT.Copy).then_inc(o_sb, 1)
                    n += 1
            act.wait_ge(o_sb, n)
            for h in range(GH):
                norm(f"head{h}", lambda k: O[:, 4 * h + k, :], T, GDV)
            for i, tile in enumerate(tiles["gla_z"]):
                if i >= 2:
                    act.wait_ge(oz_ready, i - 1)
                act.wait_ge(tile_done, tile.t + 1)
                act.activation(SZ[:, i % 2, :], PS[:, 2 * tile.slot, :], ACT.Silu).then_inc(slot_free[tile.slot], 1)
            for tile in tiles["gla_out"][-2:]:
                read_out(act, tile)
            norm("s5", lambda k: XT[:, k, :], T, D)
            act.wait_ge(gx_ready, 1)
            act.activation(gt[:, 8, :], gt[:, 7, :], ACT.Sin, scale=TWO_PI).then_inc(sin_ready, 1)
            act.activation(gt[:, 9, :], gt[:, 7, :], ACT.Sin, scale=TWO_PI / 2).then_inc(sin_ready, 1)
            act.wait_ge(pt_ps, 1)
            act.activation(PT[:].rearrange("p a b -> p (a b)").rearrange("p (a b) -> p a b", a=2), PA[:, 2:4, :], ACT.Copy).then_inc(pt_sb, 1)
            for i, tile in enumerate(tiles["s5_u"]):
                act.wait_ge(tile_done, tile.t + 1)
                act.activation(U[:, i, :], PS[:, 2 * tile.slot, :], ACT.Copy).then_inc(slot_free[tile.slot], 1)
                read_out(act, tile)
                act.dma_start(u_dram[i * P:(i + 1) * P, :], U[:, i, :]).then_inc(u_out, 16)
            for b in range(NBATCH):
                act.wait_ge(c_ps, b + 1)
                if b > 0:
                    act.wait_ge(w_ready, 2 * b)
                act.activation(CZ[:].rearrange("p a b -> p (a b)"), PA[:, 0, 0:2 * P], ACT.Copy).then_inc(cz_sb, 1)
                act.wait_ge(frac_ready, b + 1)
                act.activation(rot_s[:], rot_c[:], ACT.Sin, scale=sg2pi[:, 0:1]).then_inc(rot_ready, 1)
                link(act.activation(rot_c[:], rot_c[:], ACT.Abs))
                act.activation(rot_c[:], rot_c[:], ACT.Sin, scale=-TWO_PI, bias=con[:, C_HPI:C_HPI + 1]).then_inc(rot_ready, 1)
                act.wait_ge(b_ps, b + 1)
                if b > 0:
                    act.wait_ge(v_ps, b)
                bt4 = PA[:, 1:3, :].rearrange("p a (g m) -> p a g m", g=4)
                act.activation(WB[:, :, 0:P].rearrange("p (a g) m -> p a g m", a=2), bt4, ACT.Copy)
                for h in range(2):
                    m = act.activation(WB[:, 4 * h:4 * h + 4, P:P + SP_], bt4[:, h, :, 0:SP_], ACT.Copy)
                m.then_inc(wb_sb, 1)
                tile = tiles["s5_z"][b]
                act.wait_ge(tile_done, tile.t + 1)
                act.activation(Z[:, b, :], PS[:, 2 * tile.slot, :], ACT.Silu).then_inc(slot_free[tile.slot], 1)
                act.wait_ge(y_ps, b + 1)
                if b > 0:
                    act.wait_ge(y_out, 16 * TB * b)
                act.activation(YB, PA[:, 0, :], ACT.Copy).then_inc(y_sb, 1)
                act.wait_ge(y_sb, b + 1)
                dst = y_dram[b * P:(b + 1) * P, :].rearrange("(g i) (t n) -> t i g n", g=BG, t=TB)
                for t in range(TB):
                    act.dma_start(dst[t], YB[t * SGRP:(t + 1) * SGRP, :].rearrange("p (g n) -> p g n", g=BG)).then_inc(y_out, 16)
            for i in range(KI):
                act.wait_ge(yd_ready, i + 1)
                act.activation(U[:, i, :], U[:, i, :], ACT.Gelu_apprx_tanh).then_inc(gelu_done, 1)
            for i, tile in enumerate(tiles["s5_glu"]):
                if i >= 2:
                    act.wait_ge(oz_ready, KI + i - 1)
                act.wait_ge(tile_done, tile.t + 1)
                act.activation(M12[:, i % 2, :], PS[:, 2 * tile.slot, :], ACT.Sigmoid, bias=pv[:, PV_BGLU + i:PV_BGLU + i + 1])\
                    .then_inc(slot_free[tile.slot], 1)
            for tile in tiles["s5_out"][-2:]:
                read_out(act, tile)
            norm("fin", lambda k: XT[:, k, :], T, D)
            act.wait_ge(mt_ps, 1)
            act.activation(X2[:, :, 0:NM], PA[:, 2, 0:KD * NM].rearrange("p (k m) -> p k m", k=KD), ACT.Copy).then_inc(mt_sb, 1)
            act.wait_ge(mt_sb, 1)
            act.wait_ge(normed, NORMS["fin"][0] + KD)
            norm("attn", lambda k: X2[:, k, :], T2, D)
            act.wait_ge(normed, NORMS["attn"][0] + KD)

            def wide(tile, dst, rows=slice(0, P)):
                act.wait_ge(tile_done, tile.t + 1)
                act.activation(dst.rearrange("p (h n) -> p h n", h=2), PS[rows, 2 * tile.slot:2 * tile.slot + 2, 0:HALF], ACT.Copy)\
                    .then_inc(slot_free[tile.slot], 1)

            for i, tile in enumerate(tiles["cq"]):
                evac(tile, CQ[:, i, :])
            wide(tiles["ckv"][0], CK[:, 0:T2])
            wide(tiles["kr"][0], KR[0:MQK, :], slice(0, MQK))
            for i, tile in enumerate(tiles["qs"]):
                evac(tile, QS[:, i, :])
            for tile in (*tiles["cq"], *tiles["ckv"]):
                read_out(act, tile)
            norm("cq", lambda k: CQ[:, k, :], T, MQR)
            norm("ckv", lambda k: CK[:, 0:T2], T2, MKR)
            for i, tile in enumerate(tiles["ks"]):
                wide(tile, KS[:, i, :])
            for i, tile in enumerate(tiles["qi"]):
                evac(tile, QI[:, i, :])
            wide(tiles["ki"][0], KI_[:])
            tile = tiles["wi"][0]
            act.wait_ge(tile_done, tile.t + 1)
            act.activation(WI[:], PS[:, 2 * tile.slot, 0:NPAIR * 8].rearrange("p (i h) -> p i h", i=NPAIR), ACT.Copy, scale=8 ** -0.5)\
                .then_inc(slot_free[tile.slot], 1)

            def values(stage, dst):
                for i, tile in enumerate(tiles[stage]):
                    act.wait_ge(tile_done, tile.t + 1)
                    nb = 2 if i < 2 else 1
                    act.activation(dst[:, 2 * i:2 * i + nb, :], PS[:, 2 * tile.slot:2 * tile.slot + nb, :], ACT.Copy)\
                        .then_inc(slot_free[tile.slot], 1)

            values("vs", VS)
            for h, tile in enumerate(tiles["uq"]):
                evac(tile, Qm[0:MQK, h, :], rows=MQK)
            for h, tile in enumerate(tiles["ukn"]):
                wide(tile, Km[0:MNOPE, h, :], slice(0, MNOPE))
            values("ukvv", Vm)

            n_idx = n_att = 0
            for n, (kind, i, h) in enumerate(UNITS):
                nk = keys(i)
                if kind == "idx":
                    act.wait_ge(score_ps, n + 1)
                    if n_idx >= 2:
                        act.wait_ge(acc_used, n_idx - 1)
                    act.activation(split(RL[:, n_idx % 2, 0:nk], i), scores(n % 2, i), ACT.Relu, scale=64 ** -0.5)\
                        .then_inc(score_free[n % 2], 1)
                    act.nop().then_inc(relu_ready, 1)
                    n_idx += 1
                    continue
                scale = (MQK if kind == "mla" else DHD) ** -0.5
                pair = n_att % 2
                act.wait_ge(max_ready, n_att + 1)
                act.activation(PB[:, pair, 0:nk], PB[:, pair, 0:nk], ACT.Exp, scale=scale, bias=mx[:, pair, 1:2],
                               accum_out=mx[:, pair, 2:3]).then_inc(exp_ready, 1)
                n_att += 1

                def copy_pT(m, i):
                    act.wait_ge(pT_ps, m + 1)
                    p = m % 2
                    if m >= 2:
                        act.wait_ge(pv_out_ps, m - 1)
                    act.activation(PT2[:, p, 0:(i + 2) * P], PS[:, 2 * p:2 * p + 2, :].rearrange("p a b -> p (a b)")[:, 0:(i + 2) * P],
                                   ACT.Copy).then_inc(pT_sb, 1)

                if h > 0 or kind == "dsa":
                    copy_pT(n_att - 2, i)
                if kind == "dsa" and h == DH - 1:
                    copy_pT(n_att - 1, i)
            for tile in tiles["attn_out"][-2:]:
                read_out(act, tile)
            norm("ffn", lambda k: X2[:, k, NM:T2], T, D)
            for i, tile in enumerate(tiles["ffn_up"]):
                act.wait_ge(tile_done, tile.t + 1)
                if i >= 2:
                    read_out(act, tiles["ffn_up"][i - 2])
                act.activation(SF[:, i % 2, :], PS[:, 2 * tile.slot, :], ACT.Silu).then_inc(silu_ready, 1)
            for tile in tiles["ffn_down"][-2:]:
                read_out(act, tile)
            norm("fin2", lambda k: X2[:, k, NM:T2], T, D)
            for tt in range(NPAIR):
                act.wait_ge(ot_ps, tt + 1)
                act.activation(OT[:, tt, :], PA[:, 2 * (tt % 2):2 * (tt % 2) + 2, :].rearrange("p a b -> p (a b)"), ACT.Copy)\
                    .then_inc(ot_sb, 1)

        def dve_program(dve):
            chain = [0]

            def link(ins):
                chain[0] += 1
                ins.then_inc(dve_chain, 1)
                dve.wait_ge(dve_chain, chain[0])

            def norm(name, src, dst, gain, width):
                s0, n0, k = NORMS[name]
                dve.wait_ge(std_ready, n0 + 1)
                dve.reciprocal(rs[:, 0:width], rs[:, 0:width]).then_inc(rstd_ready, 1)
                dve.wait_ge(rstd_ready, n0 + 1)
                for i in range(k):
                    dve.scalar_tensor_tensor(out=dst(i), in0=src(i), scalar=pv[:, gain + i:gain + i + 1], in1=rs[:, 0:width],
                                             op0=ALU.mult, op1=ALU.mult).then_inc(normed, 1)

            dve.memset(WG[:], 0.0).then_inc(wg_zero, 1)
            dve.wait_ge(con_in, 32)
            dve.wait_ge(pv_sb, 1)
            dve.wait_ge(xT_sb, KD)
            norm("gla", lambda k: XT[:, k, :], lambda k: HT[:, k, :], PV_GLA, T)
            for i in (-2, -1):
                read_out(dve, tiles["gla_k"][i])
            for h in range(GH):
                dve.wait_ge(gl_ready, h + 1)
                link(dve.scalar_tensor_tensor(out=LA[:, h, :], in0=LA[:, h, :], scalar=0.0, in1=la_e[:],
                                              op0=ALU.min, op1=ALU.subtract))
                dve.tensor_tensor_scan(LA[:, h, :], gcon[:, C_RST:C_RST + T], LA[:, h, :], 0.0, ALU.mult, ALU.add)\
                    .then_inc(la_ready, 1)
                dve.wait_ge(la_ready, h + 1)
                la3 = LA[:, h, :].rearrange("p (c t) -> p c t", t=GCH)
                last = la3[:, :, GCH - 1:GCH]
                dve.tensor_tensor(kend[:, h, :].rearrange("p (c t) -> p c t", t=GCH), last.broadcast_to([P, NCH, GCH]), la3,
                                  ALU.subtract).then_inc(de_ready, 1)
                dve.wait_ge(ex_ready, 2 * h + 2)
                link(dve.tensor_copy(dec[:, h, :], ex_p[:].rearrange("p (c t) -> p c t", t=GCH)[:, :, GCH - 1]))
                link(dve.scalar_tensor_tensor(out=QG[:, h, :], in0=QG[:, h, :], scalar=GDK ** -0.5, in1=ex_p[:],
                                              op0=ALU.mult, op1=ALU.mult))
                dve.wait_ge(kx_ready, h + 1)
                dve.tensor_tensor(kend[:, h, :], kend[:, h, :], KG[:, h, :], ALU.mult).then_inc(ke_ready, 1)
                dve.wait_ge(ke_ready, h + 1)
                dve.tensor_tensor(KG[:, h, :], KG[:, h, :], ex_n[:], ALU.mult).then_inc(qkg_ready, 1)
            dve.wait_ge(qkg_ready, GH)
            link(dve.memset(ATT[:].rearrange("p a b -> p (a b)"), 0.0))
            for h in range(GH):
                dve.wait_ge(att_ps, h + 1)
                dve.copy_predicated(ATT[:, h, :], gcon[:, C_GM:C_GM + T].bitcast(U32), PA[:, h, :]).then_inc(att_sb, 1)
            dve.wait_ge(keT_ps, GH)
            n = 0
            for c in range(NCH - 1):
                for h in range(GH):
                    dve.wait_ge(kv_ps, n + 1)
                    if c >= 3:
                        dve.wait_ge(o_ps, GH * ((c - 2) // 2) + h + 1)
                    if c > 0:
                        dve.wait_ge(S_ready, n - GH + 1)
                    hs = slice(h * GDV, (h + 1) * GDV)
                    if c == 0:
                        dve.tensor_copy(S[:, 0, hs], PA[:, n % 2, :]).then_inc(S_ready, 1)
                    else:
                        dve.scalar_tensor_tensor(out=S[:, c % 3, hs], in0=S[:, (c - 1) % 3, hs], scalar=dec[:, h, c:c + 1],
                                                 in1=PA[:, n % 2, :], op0=ALU.mult, op1=ALU.add).then_inc(S_ready, 1)
                    n += 1
            dve.wait_ge(o_sb, GH * NPAIR)
            for h in range(GH):
                norm(f"head{h}", lambda k: O[:, 4 * h + k, :], lambda k: O[:, 4 * h + k, :], PV_HG, T)
            dve.wait_ge(normed, NORMS["head3"][0] + 4)
            for i, tile in enumerate(tiles["gla_z"]):
                read_out(dve, tile)
                dve.tensor_tensor(O[:, i, :], O[:, i, :], SZ[:, i % 2, :], ALU.mult).then_inc(oz_ready, 1)
            for i, tile in enumerate(tiles["gla_out"]):
                dve.wait_ge(tile_done, tile.t + 1)
                dve.tensor_tensor(XT[:, i, :], XT[:, i, :], PS[:, 2 * tile.slot, :], ALU.add).then_inc(slot_free[tile.slot], 1)

            for tile in tiles["gla_out"][-2:]:
                read_out(dve, tile)
            dve.wait_ge(par_in, 16 * 3)
            tt, ts, stt = dve.tensor_tensor, dve.tensor_scalar, dve.scalar_tensor_tensor

            def mul(o, x, y):
                link(tt(o, x, y, ALU.mult))

            def round_to(o, x):
                link(ts(o, x, ROUND, ROUND, ALU.add, ALU.subtract))

            def expm1(x, n, r, t, p2, ni):
                link(ts(n, x, 1 / math.log(2), None, ALU.mult))
                round_to(n, n)
                ln2_hi = 0.693359375
                link(stt(out=r, in0=n, scalar=-ln2_hi, in1=x, op0=ALU.mult, op1=ALU.add))
                link(stt(out=r, in0=n, scalar=ln2_hi - math.log(2), in1=r, op0=ALU.mult, op1=ALU.add))
                link(ts(t, r, 1 / 8, 1.0, ALU.mult, ALU.add))
                for m in range(7, 1, -1):
                    mul(t, t, r)
                    link(ts(t, t, 1 / m, 1.0, ALU.mult, ALU.add))
                mul(t, t, r)
                link(ts(n, n, 127.0, None, ALU.add))
                link(dve.tensor_copy(ni, n))
                link(dve.tensor_single_scalar(p2.bitcast(I32), ni, 23, ALU.logical_shift_left))

            g = [gt[:, i, :] for i in range(16)]
            d = [gdt[:, i:i + 1] for i in range(8)]
            link(ts(d[1], d[0], -80.0, 80.0, ALU.max, ALU.min))
            expm1(d[1], d[2], d[3], d[4], d[5], gi[:, 0:1])
            mul(d[4], d[4], d[5])
            link(tt(d[6], d[4], d[5], ALU.add))
            link(ts(g[0], glr[:], d[6], A_MIN, ALU.mult, ALU.max))
            link(ts(g[6], gli[:], d[6], 1 / (2 * math.pi), ALU.mult, ALU.mult))
            round_to(g[7], g[6])
            tt(g[7], g[6], g[7], ALU.subtract).then_inc(gx_ready, 1)
            dve.wait_ge(gx_ready, 1)
            expm1(g[0], g[1], g[2], g[3], g[4], gi[:])
            mul(g[3], g[3], g[4])
            link(stt(out=g[5], in0=g[4], scalar=-1.0, in1=g[3], op0=ALU.add, op1=ALU.add))
            link(tt(g[4], g[3], g[4], ALU.add))
            dve.wait_ge(sin_ready, 2)
            mul(g[9], g[9], g[9])
            link(ts(g[9], g[9], 2.0, None, ALU.mult))
            link(ts(g[10], g[9], -1.0, 1.0, ALU.mult, ALU.add))
            tp = [TPg[:, i, 0:SP_] for i in range(8)]
            mul(tp[0], g[4], g[10])
            mul(tp[1], g[4], g[8])
            mul(g[11], g[5], g[10])
            link(tt(g[11], g[11], g[9], ALU.subtract))
            link(dve.reciprocal(g[12], g[4]))
            mul(tp[2], g[12], g[10])
            link(stt(out=tp[3], in0=g[12], scalar=-1.0, in1=g[8], op0=ALU.mult, op1=ALU.mult))
            mul(g[12], glr[:], glr[:])
            mul(g[13], gli[:], gli[:])
            link(tt(g[12], g[12], g[13], ALU.add))
            link(dve.reciprocal(g[12], g[12]))
            mul(g[13], g[11], glr[:])
            mul(g[14], tp[1], gli[:])
            link(tt(g[13], g[13], g[14], ALU.add))
            mul(tp[4], g[13], g[12])
            mul(g[13], tp[1], glr[:])
            mul(g[14], g[11], gli[:])
            link(tt(g[13], g[13], g[14], ALU.subtract))
            mul(tp[5], g[13], g[12])
            mul(g[13], g[4], g[4])
            mul(g[13], g[13], g[13])
            mul(tp[6], g[13], g[13])
            link(ts(g[13], g[7], float(TB), None, ALU.mult))
            round_to(g[14], g[13])
            link(tt(tp[7], g[13], g[14], ALU.subtract))
            dve.tensor_copy(TPg[:, :, SP_:P], TPg[:, :, 0:SP_]).then_inc(tp_ready, 1)

            s0, n0, k = NORMS["s5"]
            dve.wait_ge(std_ready, n0 + 1)
            dve.reciprocal(rs[:, 0:T], rs[:, 0:T]).then_inc(rstd_ready, 1)
            dve.wait_ge(rstd_ready, n0 + 1)
            for i in range(k):
                stt(out=sn(HT[:, i, :]), in0=by_block(XT[:, i, :]), scalar=pv[:, PV_S5 + i:PV_S5 + i + 1], in1=by_block(rs[:, 0:T]),
                    op0=ALU.mult, op1=ALU.mult).then_inc(normed, 1)

            dve.wait_ge(pt_sb, 1)
            L, LI, CO = (PT[:, 0, :], PT[:, 1, :]), (PT[:, 2, :], PT[:, 3, :]), (PT[:, 4, :], PT[:, 5, :])

            def cmul(dst, x, y):
                link(tt(ctmp[:, 0, :], x[1], y[1], ALU.mult))
                link(tt(ctmp[:, 1, :], x[1], y[0], ALU.mult))
                link(tt(dst[0], x[0], y[0], ALU.mult))
                link(tt(dst[1], x[0], y[1], ALU.mult))
                link(tt(dst[0], dst[0], ctmp[:, 0, :], ALU.subtract))
                link(tt(dst[1], dst[1], ctmp[:, 1, :], ALU.add))

            def pw(i, k):
                return PW[:, 2 * i, k, :], PW[:, 2 * i + 1, k, :]

            for c in range(2):
                link(dve.tensor_copy(pw(0, 0)[c], L[c]))
                link(dve.tensor_copy(pw(1, TB - 1)[c], CO[c]))
            cmul(pw(2, 0), CO, LI)
            for k in range(1, TB):
                cmul(pw(0, k), pw(0, k - 1), L)
                cmul(pw(1, TB - 1 - k), pw(1, TB - k), L)
                cmul(pw(2, k), pw(2, k - 1), LI)
            link(dve.tensor_copy(r8f8[:], PT[:, 6:8, :]))
            link(ts(sg2pi[:, 0:1], con[:, C_SG:C_SG + 1], TWO_PI, None, ALU.mult))
            sg, nsg = con[:, C_SG:C_SG + 1], con[:, C_NSG:C_NSG + 1]
            for i, scale in ((0, sg), (1, -1.0), (3, nsg), (5, nsg)):
                v = PW[:, i, :, :].rearrange("p a b -> p (a b)")
                link(ts(v, v, scale, None, ALU.mult))
            dve.nop().then_inc(pw_ready, 1)

            def factor(i, b):
                return PW[:, i, :, b * BG:(b + 1) * BG].rearrange("p k g -> p g k").unsqueeze(3).broadcast_to([P, BG, TB, SGRP])

            def rows(ap):
                return ap.rearrange("p g j -> p g j").unsqueeze(2).broadcast_to([P, BG, TB, SGRP])

            def four(ap):
                return ap.rearrange("p g (s j) -> p g s j", s=TB)

            def add_skip(b):
                dve.wait_ge(y_in, 16 * (b + 1))
                stt(out=U[:, b, :], in0=U[:, b, :], scalar=pv[:, PV_DS + b:PV_DS + b + 1], in1=YIN, op0=ALU.mult, op1=ALU.add)\
                    .then_inc(yd_ready, 1)

            for b in range(NBATCH):
                gs = slice(b * BG, (b + 1) * BG)
                if b > 0:
                    dve.wait_ge(y_ps, b)
                rc, rk = rot_c[:].rearrange("p (g n) -> p g n", g=BG), rot_s[:]
                link(tt(rc, r8f8[:, 1, gs].unsqueeze(2).broadcast_to([P, BG, NB]),
                        con[:, C_NI:C_NI + NB].unsqueeze(1).broadcast_to([P, BG, NB]), ALU.mult))
                round_to(rk, rot_c[:])
                tt(rot_c[:], rot_c[:], rk, ALU.subtract).then_inc(frac_ready, 1)
                dve.wait_ge(small_in[b % 2], 16 * 7 * (b // 2 + 1))
                for dst, i in ((Bt, 2), (Bn, 4)):
                    link(tt(four(dst[:]), factor(i, b), rows(BZ[:, b % 2, 0]), ALU.mult))
                    link(tt(four(b_tmp), factor(i + 1, b), rows(BZ[:, b % 2, 1]), ALU.mult))
                    tt(dst[:], dst[:], b_tmp, ALU.add).then_inc(bt_ready, 1)
                    dve.wait_ge(bt_ready, 2 * b + (1 if i == 2 else 2))
                if b > 0:
                    add_skip(b - 1)
                for h in range(2):
                    dve.wait_ge(k_ps, 2 * b + 2)
                    tt(KM[:, 4 * h:4 * h + 4, :].rearrange("p g m -> p (g m)"), PA[:, 3 * h, :], con[:, C_SM:C_SM + T], ALU.mult)\
                        .then_inc(km_ready, 1)
                dve.wait_ge(v_ps, b + 1)
                dve.wait_ge(rot_ready, 2 * b + 2)
                link(tt(M12[:, 0, :], PA[:, 1, :], rot_c[:], ALU.mult))
                tt(M12[:, 1, :], PA[:, 2, :], rot_s[:], ALU.mult).then_inc(rot_used, 1)
                dve.wait_ge(rot_used, b + 1)
                link(tt(M12[:, 0, :], M12[:, 0, :], M12[:, 1, :], ALU.add))
                dve.wait_ge(dk_ready, b + 1)
                link(dve.tensor_tensor_scan(M12[:, 1, :], dk[:], M12[:, 0, :], 0.0, ALU.mult, ALU.add))
                tt(M12[:, 0, :], M12[:, 1, :], rot_c[:], ALU.mult).then_inc(m_ready, 1)
                dve.wait_ge(m_ready, 2 * b + 1)
                tt(M12[:, 1, :], M12[:, 1, :], rot_s[:], ALU.mult).then_inc(m_ready, 1)
            add_skip(NBATCH - 1)
            for i in range(KI):
                dve.wait_ge(gelu_done, i + 1)
                read_out(dve, tiles["s5_z"][i])
                link(tt(Z[:, i, :], Z[:, i, :], U[:, i, :], ALU.mult))
            for i, tile in enumerate(tiles["s5_glu"]):
                read_out(dve, tile)
                tt(Z[:, i, :], Z[:, i, :], M12[:, i % 2, :], ALU.mult).then_inc(oz_ready, 1)
            for i, tile in enumerate(tiles["s5_out"]):
                dve.wait_ge(tile_done, tile.t + 1)
                tt(by_block(XT[:, i, :]), by_block(XT[:, i, :]), sn(PS[:, 2 * tile.slot, :]), ALU.add).then_inc(slot_free[tile.slot], 1)
            for tile in tiles["s5_out"][-2:]:
                read_out(dve, tile)
            norm("fin", lambda k: XT[:, k, :], lambda k: X2[:, k, NM:T2], PV_FIN, T)
            dve.memset(U2[:, :, T2:TPAD], 0.0).then_inc(pad_zero, 1)
            dve.wait_ge(mt_sb, 1)
            dve.wait_ge(normed, NORMS["fin"][0] + KD)
            norm("attn", lambda k: X2[:, k, :], lambda k: U2[:, k, 0:T2], PV_ATT, T2)
            dve.memset(CK[:, T2:TPAD], 0.0).then_inc(pad_zero, 1)
            norm("cq", lambda k: CQ[:, k, :], lambda k: CQ[:, k, :], PV_GQ, T)
            norm("ckv", lambda k: CK[:, 0:T2], lambda k: CK[:, 0:T2], PV_GKV, T2)
            dve.wait_ge(rt_in, 16)
            for stage in ROT_STAGES:
                for j, (x, lo_row, hi_row, t0, c, tile) in enumerate(rotations(stage)):
                    n = ROT_AT[stage] + j
                    width = T2 - t0
                    r = slice(lo_row, hi_row)
                    sin = c + T2
                    dve.wait_ge(ro_ps, n + 1)
                    tt(halves(ro[r, n % 2, 0:width], 2), PA[r, 2 * (n % 2):2 * (n % 2) + 2, 0:width // 2],
                       halves(rt[r, sin + t0:sin + T2], 2), ALU.mult).then_inc(ro_read, 1)
                    link(tt(x[r, :], x[r, :], rt[r, c + t0:c + T2], ALU.mult))
                    dve.wait_ge(ro_read, n + 1)
                    tt(x[r, :], x[r, :], ro[r, n % 2, 0:width], ALU.add).then_inc(roped, 1)

            n_idx = n_att = 0

            def finish(m, kind, i, h):
                p = m % 2
                dve.wait_ge(exp_ready, m + 1)
                dve.reciprocal(mx[:, p, 3:4], mx[:, p, 2:3]).then_inc(rsum_ready, 1)

            def output(m, kind, i, h):
                p = m % 2
                dve.wait_ge(pv_out_ps, m + 1)
                r = slice((h % 2) * 64, (h % 2) * 64 + 64)
                dve.tensor_copy(OA[r, (0 if kind == "mla" else 4) + h // 2, i * P:(i + 1) * P], PS[r, 2 * p + 1, 2 * P:3 * P])\
                    .then_inc(oa_ready, 1)

            todo = []
            dve.wait_ge(pb_zero, 1)
            dve.wait_ge(roped, 22)
            for n, (kind, i, h) in enumerate(UNITS):
                nk = keys(i)
                cb = rt[:, C_CB + T2 - nk:C_CB + T2]
                if kind == "idx":
                    dve.wait_ge(relu_ready, n_idx + 1)
                    dve.wait_ge(score_free[n % 2], n // 2 + 1)
                    if n_idx > 0:
                        dve.wait_ge(acc_used, n_idx)
                    wih = WI[:, i, h:h + 1]
                    if h == 0:
                        ts(acc[:, 0:nk], RL[:, n_idx % 2, 0:nk], wih, None, ALU.mult).then_inc(acc_used, 1)
                    else:
                        stt(out=acc[:, 0:nk], in0=RL[:, n_idx % 2, 0:nk], scalar=wih, in1=acc[:, 0:nk], op0=ALU.mult, op1=ALU.add)\
                            .then_inc(acc_used, 1)
                    n_idx += 1
                    if h == 7:
                        dve.wait_ge(acc_used, n_idx)
                        link(tt(acc[:, 0:nk], acc[:, 0:nk], cb, ALU.add))
                        for _ in range(TOPK // 8):
                            link(dve.max(top8[:], acc[:, 0:nk]))
                            link(dve.match_replace(out=acc[:, 0:nk], in_to_replace=top8[:], in_values=acc[:, 0:nk], imm_value=TAKEN))
                        link(ts(selb[:, 0:nk], acc[:, 0:nk], TAKEN, 1.0, ALU.is_equal, ALU.subtract))
                        link(stt(out=selb[:, 0:nk], in0=selb[:, 0:nk], scalar=-LOW, in1=cb, op0=ALU.mult, op1=ALU.add))
                    continue
                scale = (MQK if kind == "mla" else DHD) ** -0.5
                p = n_att % 2
                dve.wait_ge(score_ps, n + 1)
                if n_att >= 2:
                    dve.wait_ge(pT_ps, n_att - 1)
                bias = cb if kind == "mla" else selb[:, 0:nk]
                dve.tensor_tensor_reduce(split(PB[:, p, 0:nk], i), scores(n % 2, i), split(bias, i), 1.0, TAKEN, ALU.add, ALU.max,
                                         mx[:, p, 0:1]).then_inc(score_free[n % 2], 1)
                dve.wait_ge(score_free[n % 2], n // 2 + 1)
                ts(mx[:, p, 1:2], mx[:, p, 0:1], -scale, None, ALU.mult).then_inc(max_ready, 1)
                todo.append((n_att, kind, i, h))
                n_att += 1
                if len(todo) >= 2:
                    finish(*todo[-2])
                    if len(todo) >= 3:
                        output(*todo.pop(0))
                if kind == "dsa" and h == DH - 1:
                    finish(*todo[-1])
                    while todo:
                        output(*todo.pop(0))
            for i, tile in enumerate(tiles["attn_out"]):
                dve.wait_ge(tile_done, tile.t + 1)
                tt(X2[:, i, NM:T2], X2[:, i, NM:T2], PS[:, 2 * tile.slot, :], ALU.add).then_inc(slot_free[tile.slot], 1)
            for tile in tiles["attn_out"][-2:]:
                read_out(dve, tile)
            norm("ffn", lambda k: X2[:, k, NM:T2], lambda k: U2[:, k, 0:T], PV_FFN, T)
            for i, tile in enumerate(tiles["ffn_up"]):
                dve.wait_ge(silu_ready, i + 1)
                dve.wait_ge(tile_done, tile.t + 1)
                tt(HF[:, i, :], SF[:, i % 2, :], PS[:, 2 * tile.slot + 1, :], ALU.mult).then_inc(slot_free[tile.slot], 1)
            for i, tile in enumerate(tiles["ffn_down"]):
                dve.wait_ge(tile_done, tile.t + 1)
                tt(X2[:, i, NM:T2], X2[:, i, NM:T2], PS[:, 2 * tile.slot, :], ALU.add).then_inc(slot_free[tile.slot], 1)
            for tile in tiles["ffn_down"][-2:]:
                read_out(dve, tile)
            norm("fin2", lambda k: X2[:, k, NM:T2], lambda k: U2[:, k, 0:T], PV_FIN2, T)

        def pool_program(pool):
            def vec(name, row, n, src):
                pool.dma_start(pvr[row:row + n, 0:P], src).then_inc(pv_in, 16)

            def col(x):
                return x.rearrange("(k p) -> k p", p=P)

            pool.dma_start(xtok[:], a["x"][0].rearrange("(t p) d -> p t d", p=P)).then_inc(x_in, 16)
            vec("gla_norm", PV_GLA, KD, col(a["gla_norm"][0]))
            vec("b_gate", PV_BG, 4, col(a["gla_b_gate"][0]))
            vec("head_gain", PV_HG, 4, col(a["gla_head_gain"][0]))
            vec("s5_norm", PV_S5, KD, col(a["s5_norm"][0]))
            vec("b_glu", PV_BGLU, KI, col(a["s5_b_glu"][0]))
            vec("d", PV_DS, KI, col(a["s5_d"][0].rearrange("g i -> (g i)")))
            vec("final_norm", PV_FIN, KD, col(a["final_norm"]))
            vec("attn_norm", PV_ATT, KD, col(a["attn_norm_g_2"][0]))
            vec("q_norm", PV_GQ, 2, col(a["mla_q_norm_g_2"][0]))
            vec("kv_norm", PV_GKV, 1, col(a["mla_kv_norm_g_2"][0]))
            vec("ffn_norm", PV_FFN, KD, col(a["ffn_norm_g_2"][0]))
            vec("final_norm_2", PV_FIN2, KD, col(a["final_norm_g_2"]))
            pool.wait_ge(wg_zero, 1)
            pool.dma_start(WG[P - GRANK:P, :], a["gla_w_gate_up"][0]).then_inc(wg_in, 16)
            pool.wait_ge(tile_done, tiles["gla_out"][-1].t + 1)
            pool.dma_start(glr[:], a["s5_lam_re"][0]).then_inc(par_in, 16)
            pool.dma_start(gli[:], a["s5_lam_im"][0]).then_inc(par_in, 16)
            pool.dma_start(gdt[:, 0:1], a["s5_log_dt"][0].rearrange("(g o) -> g o", o=1)).then_inc(par_in, 16)
            pool.wait_ge(pw_ready, 1)

            def factor(i, b):
                return PW[:, i, :, b * BG:(b + 1) * BG].rearrange("p k g -> p g k").unsqueeze(3).broadcast_to([P, BG, TB, SGRP])

            def rows(ap):
                return ap.rearrange("p (g j) -> p g j", g=BG).unsqueeze(2).broadcast_to([P, BG, TB, SGRP])

            def four(ap):
                return ap.rearrange("p g (s j) -> p g s j", s=TB)

            chain = [0]

            def link(ins):
                chain[0] += 1
                ins.then_inc(pool_chain, 1)
                pool.wait_ge(pool_chain, chain[0])

            def read_back(b):
                pool.wait_ge(y_out, 16 * TB * (b + 1))
                if b > 0:
                    pool.wait_ge(yd_ready, b)
                pool.dma_start(YIN, y_dram[b * P:(b + 1) * P, :]).then_inc(y_in, 16)

            for b in range(NBATCH):
                gs = slice(b * BG, (b + 1) * BG)
                if b > 0:
                    pool.wait_ge(y_ps, b)
                pool.tensor_tensor(dk[:].rearrange("p (g n) -> p g n", g=BG), r8f8[:, 0, gs].unsqueeze(2).broadcast_to([P, BG, NB]),
                                   con[:, C_NM:C_NM + NB].unsqueeze(1).broadcast_to([P, BG, NB]), ALU.mult).then_inc(dk_ready, 1)
                pool.wait_ge(cz_sb, b + 1)
                for dst, i, j, op in ((W1, 0, 1, ALU.add), (W2, 1, 0, ALU.subtract)):
                    link(pool.tensor_tensor(four(dst[:]), factor(i, b), rows(CZ[:, 0, :]), ALU.mult))
                    link(pool.tensor_tensor(four(w_tmp[:]), factor(j, b), rows(CZ[:, 1, :]), ALU.mult))
                    pool.tensor_tensor(dst[:], dst[:], w_tmp[:], op).then_inc(w_ready, 1)
                    if dst is W1:
                        pool.wait_ge(w_ready, 2 * b + 1)
                    if dst is W1 and b > 0:
                        read_back(b - 1)
            read_back(NBATCH - 1)
            pool.wait_ge(tile_done, tiles["s5_out"][-1].t + 1)
            pool.dma_start(MT[0:NM, :], a["meta_tokens_2"]).then_inc(mt_in, 16)
            pool.dma_start(rt[:], a["rotary_constants"]).then_inc(rt_in, 16)
            pool.wait_ge(roped, ROT_AT["k1"] + 2)
            for h in range(MH):
                pool.tensor_copy(Km[MNOPE:MQK, h, :], KR[MNOPE:MQK, :]).then_inc(kr_copied, 1)
            pool.wait_ge(kr_copied, MH)
            pool.wait_ge(tile_done, tiles["ukvv"][-1].t + 1)
            pool.memset(PB[:], 0.0).then_inc(pb_zero, 1)
            for n in range(2 * MH * NPAIR):
                nk = keys(n // (2 * MH))
                p = n % 2
                pool.wait_ge(rsum_ready, n + 1)
                pool.tensor_scalar(PB[:, p, 0:nk], PB[:, p, 0:nk], mx[:, p, 3:4], None, ALU.mult).then_inc(p_ready, 1)

        def sp_program(sp):
            z_loads = {}
            for b, tile in enumerate(tiles["s5_z"]):
                z_loads.setdefault(tile.loads[0], []).append(b)

            def batch_loads(b):
                gs = slice(b * BG, (b + 1) * BG)
                if b == 0:
                    sp.wait_ge(pw_ready, 1)
                if b >= 2:
                    sp.wait_ge(c_ps, b - 1)
                    sp.wait_ge(bt_ready, 2 * (b - 1))
                here = small_in[b % 2]
                for k, name in enumerate(("s5_c_re", "s5_c_im", "s5_c_re")):
                    sp.dma_start(CN[:, b % 2, k * SP_:(k + 1) * SP_], a[name][0, gs].rearrange("g i p -> (g i) p")).then_inc(here, 16)
                for k in range(2):
                    for r, name in enumerate(("s5_b_re", "s5_b_im")):
                        rows = slice(((r + k) % 2) * SP_, ((r + k) % 2 + 1) * SP_)
                        sp.dma_start(BZ[rows, b % 2, k], a[name][0, gs].rearrange("g p j -> p g j")).then_inc(here, 16)
                if b == 0:
                    sp.wait_ge(u_out, 16 * KI)
                if b > 0:
                    sp.wait_ge(y_ps, b)
                src = u_dram[b * P:(b + 1) * P, :].rearrange("(g j) (s n) -> s j g n", g=BG, s=TB)
                for s in range(TB):
                    sp.dma_start(UB[s * SGRP:(s + 1) * SGRP], src[s]).then_inc(ub_in, 16)

            for n, parts in enumerate(plan.loads):
                if n >= NSLOT:
                    sp.wait_ge(tile_done, plan.last_use[n - NSLOT] + 1)
                for src, at, shape, *cols in parts:
                    dst = slot_view(n, shape, at)
                    sp.dma_start(dst[:, :, cols[0]] if cols else dst, src).then_inc(landed[n % NSLOT], 16)
                if tiles["s5_z"][0].loads[0] <= n <= tiles["s5_z"][-1].loads[0] and n in z_loads:
                    for b in z_loads[n]:
                        batch_loads(b)
            for tt in range(NPAIR):
                sp.wait_ge(ot_sb, tt + 1)
                sp.dma_start(out[0, tt * P:(tt + 1) * P, :], OT[:, tt, :]).then_inc(out_done, 16)
            sp.wait_ge(out_done, 16 * NPAIR)

        block = ctx.enter_context(nc.Block())

        @block.tensor
        def _(pe):
            pe_program(pe)

        @block.scalar
        def _(act):
            act_program(act)

        @block.vector
        def _(dve):
            dve_program(dve)

        @block.gpsimd
        def _(pool):
            pool_program(pool)

        @block.sync
        def _(sp):
            sp_program(sp)


def kernel(**inputs):
    import concourse.bacc as bacc
    from concourse.bass_utils import run_bass_kernel_spmd

    nc = bacc.Bacc("TRN2", target_bir_lowering=False, num_devices=1)
    arrays = {f"in_{name}": np.ascontiguousarray(value) for name, value in inputs.items()}
    arrays["in_shape_constants"] = shape_constants()
    arrays["in_chunk_constants"] = chunk_constants()
    arrays["in_rotary_constants"] = rotary_constants()
    a = {name[3:]: nc.dram_tensor(name, value.shape, mybir.dt.from_np(value.dtype), kind="ExternalInput").ap()
         for name, value in arrays.items()}
    out = nc.dram_tensor("out_0_dram", (1, T, D), F32, kind="ExternalOutput").ap()
    build(nc, a, out)
    r = run_bass_kernel_spmd(nc, [arrays], core_ids=[0])
    return r.results[0]["out_0_dram"]
```

```python
import math
from contextlib import ExitStack

import numpy as np

import concourse.bass as bass
from concourse import mybir

F32 = mybir.dt.float32
I32 = mybir.dt.int32
U32 = mybir.dt.uint32
F32R = mybir.dt.float32r
ALU = mybir.AluOpType
ACT = mybir.ActivationFunctionType
AX_X = mybir.AxisListType.X

P = 128
T = 512
D = 1024
KD = D // P
EPS = 1e-6
GH, GDK, GDV, GCH, GRANK, GTAU = 4, 128, 512, 64, 16, 16.0
DI = 2 * D
KI = DI // P
G_Q, G_K, G_V, G_Z, G_R = 0, 512, 1024, 3072, 5120
NPAIR = T // P
NCH = T // GCH
SG, SGRP, SP_ = 128, 16, 64
TB = 8
NB = T // TB
BG = 8
NBATCH = SG // BG
NM = 16
T2 = T + NM
HALF = T2 // 2
TPAD = 640
MH, MQR, MKR, MNOPE, MROPE, MV = 8, 256, 128, 64, 32, 64
MQK = MNOPE + MROPE
DH, DHD = 8, 64
TOPK = 128
FF = 2816
KF = FF // P
A_CQ, A_CKV, A_KR, A_QS, A_KS, A_VS, A_QI, A_KI, A_WI, A_END = 0, 256, 384, 416, 928, 1440, 1952, 2464, 2528, 2536
LOW = -1e30
TAKEN = -3e38
ROUND = 12582912.0
A_MIN = -9.0

SLOT = 2048
NSLOT = 3

C_ID, C_ONE, C_SM, C_NM, C_NI, C_SG, C_NSG, C_EPS, C_HPI, C_N = 0, 128, 256, 768, 832, 896, 897, 898, 899, 900
C_GM, C_RST = 0, 512
R_C, R_S, R_MC, R_MS, R_P, R_MP, C_CB, R_N = 0, 528, 1056, 1584, 2112, 2240, 2368, 2896
PV_GLA, PV_BG, PV_HG, PV_S5, PV_BGLU, PV_DS, PV_FIN, PV_ATT, PV_GQ, PV_GKV, PV_FFN, PV_FIN2, PV_N = \
    0, 8, 12, 16, 24, 40, 56, 64, 72, 74, 75, 83, 91


def shape_constants():
    c = np.zeros((P, C_N), np.float32)
    r = np.arange(P)
    c[:, C_ID:C_ID + P] = np.eye(P)
    c[:, C_ONE:C_ONE + P] = 1.0
    m = (r[:, None] // SGRP) <= (r[None, :] // SGRP)
    c[:, C_SM:C_SM + T] = np.tile(m, (1, 4))
    c[:, C_NM:C_NM + NB] = (np.arange(NB) != 0)[None, :]
    c[:, C_NI:C_NI + NB] = np.arange(NB)[None, :]
    c[:, C_SG] = np.where(r < SP_, 1.0, -1.0)
    c[:, C_NSG] = -c[:, C_SG]
    c[:, C_EPS] = EPS
    c[:, C_HPI] = math.pi / 2
    return c


def chunk_constants():
    c = np.zeros((P, 2 * T), np.float32)
    r = np.arange(P)
    m = (r[:, None] <= r[None, :]) & (r[:, None] // GCH == r[None, :] // GCH)
    c[:, C_GM:C_GM + T] = np.tile(m, (1, NPAIR))
    c[:, C_RST:C_RST + T] = (np.arange(T) % GCH != 0)[None, :]
    return c


def rotary_constants():
    c = np.zeros((P, R_N), np.float32)
    r = np.arange(P)
    c[:, C_CB + T2 - P:C_CB + T2] = np.where(r[None, :] <= r[:, None], 0.0, LOW)
    pos = np.arange(T2, dtype=np.float32)
    for width, rows, oc, os, op in ((DHD, range(P), R_C, R_S, R_P), (MROPE, range(MNOPE, MQK), R_MC, R_MS, R_MP)):
        half = width // 2
        inv = np.power(np.float32(10000.0), -np.arange(half, dtype=np.float32) / np.float32(half)).astype(np.float32)
        for r in rows:
            d = r % width if width == DHD else r - MNOPE
            ang = pos * inv[d % half]
            c[r, oc:oc + T2] = np.cos(ang)
            c[r, os:os + T2] = np.sin(ang) * (-1.0 if d < half else 1.0)
            c[r - d + (d + half) % width, op + r] = 1.0
    return c


class Tile:

    def __init__(self, t, loads):
        self.t, self.loads, self.slot = t, loads, t % 2


class Plan:

    def __init__(self):
        self.loads, self.tiles, self.last_use, self.value = [], {}, [], []
        self.n, self.count = 0, [0] * NSLOT
        self.size = []

    def load(self, *parts):
        n = len(self.loads)
        self.size.append(max(at + int(np.prod(shape)) for _, at, shape, *_ in parts))
        self.loads.append(parts)
        self.count[n % NSLOT] += 16 * len(parts)
        self.value.append(self.count[n % NSLOT])
        self.last_use.append(None)
        return n

    def tile(self, stage, *loads):
        t = Tile(self.n, loads)
        self.n += 1
        self.tiles.setdefault(stage, []).append(t)
        for n in loads:
            self.last_use[n] = t.t
        return t


def build(nc, a, out):
    w1 = a["gla_w_in"][0].rearrange("(k p) m -> p k m", p=P)
    wo1 = a["gla_w_out"][0].rearrange("(k p) m -> p k m", p=P)
    w2 = a["s5_w_in"][0].rearrange("(k p) m -> p k m", p=P)
    wg2 = a["s5_w_glu"][0].rearrange("(k p) m -> p k m", p=P)
    wo2 = a["s5_w_out"][0].rearrange("(k p) m -> p k m", p=P)
    w3 = a["w_in_2"][0].rearrange("(k p) m -> p k m", p=P)
    wuq = a["w_uq_2"][0].rearrange("(k p) m -> p k m", p=P)
    wukv = a["w_ukv_2"][0]
    wo3 = a["w_o_2"][0].rearrange("(k p) m -> p k m", p=P)
    wga = a["w_gate_2"][0].rearrange("(k p) m -> p k m", p=P)
    wup = a["w_up_2"][0].rearrange("(k p) m -> p k m", p=P)
    wdn = a["w_down_2"][0].rearrange("(k p) m -> p k m", p=P)

    plan = Plan()

    def pairs(stage, w, c0, n):
        for m in range(0, n, 2):
            ld = plan.load((w[:, :, c0 + m * P:c0 + (m + 2) * P], 0, (KD, 2 * P)))
            plan.tile(stage, ld)
            plan.tile(stage, ld)

    def singles(stage, w, n):
        for m in range(n):
            plan.tile(stage, plan.load((w[:, :, m * P:(m + 1) * P], 0, (KI, P))))

    def token_major(stage, w, c0, n, tiles):
        for m in range(n):
            lds = [plan.load((w[:, 4 * j:4 * j + 4, c0 + m * T:c0 + (m + 1) * T], 0, (4, T))) for j in range(2)]
            for _ in range(tiles):
                plan.tile(stage, *lds)

    pairs("gla_q", w1, G_Q, 4)
    pairs("gla_k", w1, G_K, 4)
    plan.tile("gla_r", plan.load((w1[:, :, G_R + GRANK - P:G_R + GRANK], 0, (KD, P))))
    token_major("gla_v", w1, G_V, 4, 2)
    pairs("gla_z", w1, G_Z, KI)
    singles("gla_out", wo1, KD)
    pairs("s5_u", w2, 0, KI)
    pairs("s5_z", w2, DI, KI)
    singles("s5_glu", wg2, KI)
    singles("s5_out", wo2, KD)
    pairs("cq", w3, A_CQ, 2)
    ld = plan.load((w3[:, :, A_CKV:A_QS], 0, (KD, A_QS - A_CKV)))
    plan.tile("ckv", ld)
    plan.tile("kr", ld)
    pairs("qs", w3, A_QS, 4)
    pairs("ks", w3, A_KS, 4)
    pairs("qi", w3, A_QI, 4)
    ld = plan.load((w3[:, :, A_KI:A_WI], 0, (KD, P), slice(0, 64)), (w3[:, :, A_KI:A_WI], 0, (KD, P), slice(64, P)),
                   (w3[:, :, A_WI:A_END], KD * P, (KD, 8)))
    plan.tile("ki", ld)
    plan.tile("wi", ld)
    token_major("vs", w3, A_VS, 1, 3)
    ld = plan.load((wuq, 0, (2, MH * MQK)))
    for _ in range(MH):
        plan.tile("uq", ld)
    ld = plan.load((wukv, 0, (MH * P,)))
    for _ in range(MH):
        plan.tile("ukn", ld)
    for _ in range(3):
        plan.tile("ukvv", ld)
    pairs("attn_out", wo3, 0, KD)
    for m in range(KF):
        ld = plan.load((wga[:, :, m * P:(m + 1) * P], 0, (KD, P)), (wup[:, :, m * P:(m + 1) * P], KD * P, (KD, P)))
        plan.tile("ffn_up", ld)
    for m in range(KD):
        plan.tile("ffn_down", *[plan.load((wdn[:, 11 * j:11 * j + 11, m * P:(m + 1) * P], 0, (11, P))) for j in range(2)])
    tiles = plan.tiles

    NORMS, norm_at = {}, [0, 0]
    for name, k in (("gla", KD), *[(f"head{h}", 4) for h in range(GH)], ("s5", KD), ("fin", KD), ("attn", KD),
                    ("cq", 2), ("ckv", 1), ("ffn", KD), ("fin2", KD)):
        NORMS[name] = (norm_at[0], norm_at[1], k)
        norm_at[0] += k
        norm_at[1] += 1
    SPLITS, VALS, split_at, val_at = {}, {}, 0, 0
    for name, k, counted in (("gla", KD, 1), ("gla2", KD, 1), ("o", KI, 1), ("s5", KD, 1), ("s5z", KD, 0), ("g", KI, 0), ("z", KI, 1),
                             ("attn", KD, 1), ("cq", 2, 1), ("ckv", 1, 1), ("oa", KD, 0), ("ffn", KD, 1), ("h", KF, 0)):
        SPLITS[name] = (split_at, k)
        split_at += k
        if counted:
            VALS[name] = val_at
            val_at += k
    PLAIN, plain_at = {}, 0
    for name in NORMS:
        if name not in SPLITS:
            PLAIN[name] = plain_at
            plain_at += NORMS[name][2]
    BEFORE = dict(zip(list(NORMS)[1:], list(NORMS)))

    with ExitStack() as ctx:
        base = nc.sbuf_base
        base = base() if callable(base) else base
        base = (base + 63) // 64 * 64
        top = [base]
        ends = []

        def place(name, shape, at=None, dt=F32):
            size = int(np.prod(shape[1:])) * 4
            off = (top[0] if at is None else at) + 31 & -32
            t = nc.alloc_sbuf_tensor_at(name, list(shape), dt, offset=off)
            if at is None:
                top[0] = off + size
            ends.append(off + size)
            return t, off + size

        def keep(name, shape, dt=F32):
            return place(name, shape, None, dt)[0]

        ring_off = top[0] + 31 & -32
        ring = keep("ring", [P, NSLOT, SLOT])
        ring_lo, _ = place("ring_lo", [P, NSLOT, SLOT], ring_off, F32R)
        hi_off = top[0] + 31 & -32
        ring_hi = keep("ring_hi", [P, NSLOT, SLOT], F32R)
        con = keep("con", [P, C_N])
        pv = keep("pv", [P, PV_N])
        pvr_off = top[0] + 31 & -32
        pvr = keep("pvr", [P, 2 * P])
        sq = keep("sq", [P, 2, T2])
        rs = keep("rs", [P, T2])
        sg2pi = keep("sg2pi", [P, 8])
        xt_off = top[0] + 31 & -32
        XT = keep("XT", [P, KD, T])
        lo = top[0] + 31 & -32
        K1 = 1024

        HTh, _ = place("HTh", [P, KD, T], lo, F32R)
        HTl, _ = place("HTl", [P, KD, T], lo + 16 * K1, F32R)
        QG, _ = place("QG", [P, GH, T], lo + 32 * K1)
        KG, _ = place("KG", [P, GH, T], lo + 40 * K1)
        LA, _ = place("LA", [P, GH, T], lo + 48 * K1)
        ATT = LA
        KE, _ = place("KE", [P, NPAIR, GH * GDK], lo + 56 * K1)
        V, _ = place("V", [P, NPAIR, DI], lo + 64 * K1)
        xtok, _ = place("xtok", [P, NPAIR, D], lo + 64 * K1)
        o = lo + 96 * K1
        WG, o = place("WG", [P, T], o)
        R16, o = place("R16", [P, T], o)
        la_e, o = place("la_e", [P, T], o)
        ex_p, o = place("ex_p", [P, T], o)
        ex_n, o = place("ex_n", [P, T], o)
        kend, o = place("kend", [P, GH, T], o)
        rst, o = place("rst", [P, T], o)
        S, _ = place("S", [P, 3, GH * GDV], lo)
        rs2, _ = place("rs2", [P, T], lo + 24 * K1)
        O, _ = place("O", [P, KI, T], lo + 96 * K1)
        Ol, _ = place("Ol", [P, KI, T], lo + 96 * K1, F32R)
        Oh, _ = place("Oh", [P, KI, T], lo + 64 * K1, F32R)
        HT2h, _ = place("HT2h", [P, KD, T], lo + 32 * K1, F32R)
        HT2l, _ = place("HT2l", [P, KD, T], lo + 48 * K1, F32R)
        SZ, _ = place("SZ", [P, 2, T], lo)
        gmask, o = place("gmask", [P, T], lo + 128 * K1)
        dec, _ = place("dec", [P, GH, NCH], o)

        o = lo + 116 * K1
        glr, o = place("glr", [P, SP_], o)
        gli, o = place("gli", [P, SP_], o)
        gdt, o = place("gdt", [P, 8], o)
        gt, o = place("gt", [P, 16, SP_], o)
        gi, o = place("gi", [P, SP_], o, I32)
        TPg, o = place("TPg", [P, 8, P], o)
        assert o <= lo + 128 * K1
        PT, o = place("PT", [P, 8, P], lo + 26 * K1)
        ctmp, o = place("ctmp", [P, 2, P], o)
        r8f8, _ = place("r8f8", [P, 2, P], pvr_off)
        PW, o = place("PW", [P, 6, TB, SG], lo + 32 * K1)
        CN, o = place("CN", [P, 2, 3 * SP_], o)
        BZ, o = place("BZ", [P, 2, 2, BG, SGRP], o)
        CZ, o = place("CZ", [P, 2, 2 * P], o)
        assert o <= lo + 64 * K1
        HT, _ = place("HT", [P, KD, T], lo)
        U, _ = place("U", [P, KI, T], lo + 64 * K1)
        HT5h, _ = place("HT5h", [P, KD, T], lo + 96 * K1, F32R)
        HT5l, _ = place("HT5l", [P, KD, T], lo + 112 * K1, F32R)

        def factors(name):
            sets = []
            for p_, off in ((0, lo + 16 * K1), (1, lo + 96 * K1)):
                sets.append(place(f"{name}{p_}", [P, BG, TB * SGRP], off + 4 * K1 * ("Bt", "Bn", "W1", "W2").index(name))[0])
            return sets

        Bt, Bn, W1, W2 = factors("Bt"), factors("Bn"), factors("W1"), factors("W2")
        KM = Bn
        o = lo + 112 * K1
        w_tmp, o = place("w_tmp", [P, BG, TB * SGRP], o)
        b_tmp, o = place("b_tmp", [P, BG, TB * SGRP], o)
        WB, o = place("WB", [P, BG, 3 * SP_], o)
        assert o <= lo + 128 * K1
        o = hi_off
        rot_c, o = place("rot_c", [P, 2, T], o)
        rot_s, o = place("rot_s", [P, 2, T], o)
        M12, o = place("M12", [P, 2, T], o)
        dk, o = place("dk", [P, 2, T], o)
        UB, o = place("UB", [P, 2, BG, NB], o)
        assert o <= hi_off + NSLOT * SLOT * 4
        YB, YIN = sq[:, 0, 0:T], sq[:, 1, 0:T]
        HT6l, _ = place("HT6l", [P, KD, T], lo, F32R)
        HT6h, _ = place("HT6h", [P, KD, T], lo + 16 * K1, F32R)
        Z, _ = place("Z", [P, KI, T], lo + 32 * K1)
        Zl, _ = place("Zl", [P, KI, T], lo + 32 * K1, F32R)
        Ul, _ = place("Ul", [P, KI, T], lo + 64 * K1, F32R)
        Uh, _ = place("Uh", [P, KI, T], lo + 96 * K1, F32R)
        Zh, _ = place("Zh", [P, KI, T], lo, F32R)

        X2, o = place("X2", [P, KD, T2], lo)
        u2_lo = o
        U2h, o = place("U2h", [P, KD, TPAD], o, F32R)
        U2l, att_lo = place("U2l", [P, KD, TPAD], o, F32R)
        o = u2_lo
        Km, o = place("Km", [P, MH, T2], o)
        Qm, o = place("Qm", [P, MH, T], o)
        PB, o = place("PB", [P, 2, TPAD], o)
        selb, o = place("selb", [P, T2], o)
        mx, o = place("mx", [P, 2, 8], o)
        assert o <= att_lo
        OAh, _ = place("OAh", [P, KD, T], u2_lo, F32R)
        o = att_lo
        Vm, o = place("Vm", [P, 5, MH * MV], o)
        MT, _ = place("MT", [P, D], att_lo)
        QS, o = place("QS", [P, 4, T], o)
        KS, o = place("KS", [P, 4, T2], o)
        VS, o = place("VS", [P, 5, DH * DHD], o)
        KI_, o = place("KI_", [P, T2], o)
        WI, o = place("WI", [P, NPAIR, 8], o)
        rt, oa_lo = place("rt", [P, R_N], o)
        CQ, o = place("CQ", [P, 2, T], oa_lo)
        CQh, o = place("CQh", [P, 2, T], o, F32R)
        CQl, o = place("CQl", [P, 2, T], o, F32R)
        CKh, o = place("CKh", [P, TPAD], o, F32R)
        CKl, o = place("CKl", [P, TPAD], o, F32R)
        KR, o = place("KR", [P, T2], o)
        ro, o = place("ro", [P, 2, T2], o)
        OA, o = place("OA", [P, KD, T], oa_lo)
        OAl, _ = place("OAl", [P, KD, T], oa_lo, F32R)
        PT2, o = place("PT2", [P, 2, TPAD], o)
        o = xt_off
        QI, o = place("QI", [P, 4, T], o)
        CK, _ = place("CK", [P, T2], o)
        RL, o = place("RL", [P, 2, T2], o)
        acc, o = place("acc", [P, T2], o)
        top8, o = place("top8", [P, 8], o)
        U3h, _ = place("U3h", [P, KD, T], xt_off, F32R)
        U3l, o = place("U3l", [P, KD, T], u2_lo, F32R)
        HF, _ = place("HF", [P, KF, T], o)
        HFl, o = place("HFl", [P, KF, T], o, F32R)
        HFh, o = place("HFh", [P, KF, T], o, F32R)
        SF, o = place("SF", [P, 2, T], o)
        FO, o = place("FO", [P, KD, T], u2_lo)
        OT, o = place("OT", [P, NPAIR, D], o)

        PS = ctx.enter_context(nc.psum_tensor("PS", [P, 4, 512], F32))
        PA = ctx.enter_context(nc.psum_tensor("PA", [P, 4, 512], F32))

        def sem(name):
            return ctx.enter_context(nc.semaphore(name))

        landed = [sem(f"landed{i}") for i in range(NSLOT)]
        tile_done = sem("tile_done")
        slot_free = [sem("slot_free0"), sem("slot_free1")]
        con_in, pv_in, x_in, wg_in, out_done = sem("con_in"), sem("pv_in"), sem("x_in"), sem("wg_in"), sem("out_done")
        pv_ps, pv_sb = sem("pv_ps"), sem("pv_sb")
        whi_ready, wlo_ready = sem("whi_ready"), sem("wlo_ready")
        val_ready, xhi_ready, xlo_ready = sem("val_ready"), sem("xhi_ready"), sem("xlo_ready")
        xT_ps, xT_sb = sem("xT_ps"), sem("xT_sb")
        sq_ready, sq_used, sum_ready, std_ready, rstd_ready, normed = (
            sem("sq_ready"), sem("sq_used"), sem("sum_ready"), sem("std_ready"), sem("rstd_ready"), sem("normed"))
        act_chain, dve_chain, pool_chain = sem("act_chain"), sem("dve_chain"), sem("pool_chain")
        wg_zero, gate_ps, gate_ev, gl_ready, la_ready, ex_ready, de_ready, kx_ready, qkg_ready, ke_ready = (
            sem("wg_zero"), sem("gate_ps"), sem("gate_ev"), sem("gl_ready"), sem("la_ready"), sem("ex_ready"),
            sem("de_ready"), sem("kx_ready"), sem("qkg_ready"), sem("ke_ready"))
        keT_ps, keT_sb, att_ps, att_sb, kv_ps, S_ready, o_ps, o_sb = (
            sem("keT_ps"), sem("keT_sb"), sem("att_ps"), sem("att_sb"), sem("kv_ps"), sem("S_ready"), sem("o_ps"), sem("o_sb"))
        oz_ready = sem("oz_ready")
        par_in, gx_ready, tp_ready, pt_ps, pt_sb, pw_ready, sin_ready = (
            sem("par_in"), sem("gx_ready"), sem("tp_ready"), sem("pt_ps"), sem("pt_sb"), sem("pw_ready"), sem("sin_ready"))
        u_out, ub_in, y_out, y_in = sem("u_out"), [sem("ub_in_even"), sem("ub_in_odd")], sem("y_out"), sem("y_in")
        small_in = [sem("small_in0"), sem("small_in1")]
        c_ps, cz_sb, bt_ready, b_ps, wb_sb, w_ready, k_ps, km_ready, v_ps, m_ready, y_ps, y_sb = (
            sem("c_ps"), sem("cz_sb"), sem("bt_ready"), sem("b_ps"), sem("wb_sb"), sem("w_ready"), sem("k_ps"),
            sem("km_ready"), sem("v_ps"), sem("m_ready"), sem("y_ps"), sem("y_sb"))
        frac_ready, rot_ready, dk_ready, rot_used, yd_ready, gelu_done = (
            sem("frac_ready"), sem("rot_ready"), sem("dk_ready"), sem("rot_used"), sem("yd_ready"), sem("gelu_done"))

        ident = con[:, C_ID:C_ID + P]
        ones = con[:, C_ONE:C_ONE + P]

        def read_out(eng, tile):
            eng.wait_ge(slot_free[tile.slot], tile.t // 2 + 1)

        mt_in, mt_ps, mt_sb, rt_in, pad_zero = sem("mt_in"), sem("mt_ps"), sem("mt_sb"), sem("rt_in"), sem("pad_zero")
        ro_ps, ro_read, roped, kr_copied, pb_zero = sem("ro_ps"), sem("ro_read"), sem("roped"), sem("kr_copied"), sem("pb_zero")
        score_ps, score_free, relu_ready, acc_used, max_ready, exp_ready, rsum_ready, p_ready = (
            sem("score_ps"), [sem("score_free0"), sem("score_free1")], sem("relu_ready"), sem("acc_used"), sem("max_ready"),
            sem("exp_ready"), sem("rsum_ready"), sem("p_ready"))
        pT_ps, pT_sb, pv_out_ps, oa_ready = sem("pT_ps"), sem("pT_sb"), sem("pv_out_ps"), sem("oa_ready")
        silu_ready, ot_ps, ot_sb = sem("silu_ready"), sem("ot_ps"), sem("ot_sb")

        def keys(i):
            return NM + (i + 1) * P

        def scores(pair, i):
            n = keys(i)
            return PA[:, 2 * pair:2 * pair + 1, 0:n] if n <= 512 else PA[:, 2 * pair:2 * pair + 2, 0:n // 2]

        def split(ap, i):
            n = keys(i)
            return ap.rearrange("p (h n) -> p h n", h=1 if n <= 512 else 2)

        def rotations(stage):
            if stage == "qs":
                return [(QS[:, j, :], 0, P, NM, R_C, tiles["qs"][j]) for j in range(4)]
            if stage == "ks":
                return [(KS[:, j, :], 0, P, 0, R_C, tiles["ks"][j]) for j in range(4)]
            if stage == "qi":
                return [(QI[:, j, :], 0, P, NM, R_C, tiles["qi"][j]) for j in range(4)]
            if stage == "k1":
                return [(KI_[:], 0, P, 0, R_C, tiles["ki"][0]), (KR[:], MNOPE, MQK, 0, R_MC, tiles["kr"][0])]
            return [(Qm[:, h, :], MNOPE, MQK, NM, R_MC, tiles["uq"][h]) for h in range(MH)]

        ROT_STAGES = ("qs", "ks", "qi", "k1", "qm")
        ROT_AT = {"qs": 0, "ks": 4, "qi": 8, "k1": 12, "qm": 14}

        UNITS = [("idx", 0, h) for h in range(8)]
        for i in range(NPAIR):
            UNITS += [("mla", i, h) for h in range(MH)]
            for h in range(DH):
                UNITS += [("dsa", i, h)] + ([("idx", i + 1, h)] if i + 1 < NPAIR else [])
        ATT_UNITS = [u for u in UNITS if u[0] != "idx"]

        u_dram = nc.dram_tensor("u_by_block", (DI, T), F32, kind="Internal").ap()
        y_dram = nc.dram_tensor("y_by_block", (DI, T), F32, kind="Internal").ap()
        TWO_PI = 6.283185

        def by_block(ap):
            return ap.rearrange("p (n s) -> p s n", s=TB)

        def sn(ap):
            return ap.rearrange("p (s n) -> p s n", s=TB)

        def slot_view(n, shape, at=0, of=None):
            size = int(np.prod(shape))
            v = (ring if of is None else of)[:, n % NSLOT, at:at + size]
            return v.rearrange("p (k m) -> p k m", k=shape[0]) if len(shape) == 2 else v

        def parts_view(n, shape, at=0):
            return slot_view(n, shape, at, ring_hi), slot_view(n, shape, at, ring_lo)

        def both(pair, *index):
            return tuple(x[index] for x in pair)

        def norm_applied(eng, name):
            if name in SPLITS:
                eng.wait_ge(xlo_ready, sum(SPLITS[name]))
            else:
                eng.wait_ge(normed, PLAIN[name] + NORMS[name][2])

        def halves(ap, width):
            return ap.rearrange("p (h n) -> p h n", h=2)

        def pe_program(pe):
            def weights_in(n):
                pe.wait_ge(wlo_ready, n + 1)

            def open_tile(tile):
                weights_in(tile.loads[0])
                if tile.t >= 2:
                    pe.wait_ge(slot_free[tile.slot], tile.t // 2)

            def product(dst, w, x, start, stop):
                pe.matmul(dst, w[0], x[0], start=start, stop=False)
                pe.matmul(dst, w[0], x[1], start=False, stop=False)
                return pe.matmul(dst, w[1], x[0], start=False, stop=stop)

            def feature_tile(tile, weights, rhs, nk, width=T, rows=P, split=None):
                open_tile(tile)
                for k in range(nk):
                    if split:
                        pe.wait_ge(xlo_ready, SPLITS[split][0] + k + 1)
                    w, x = weights(k), rhs(k)
                    if width == T:
                        m = product(PS[0:rows, 2 * tile.slot, 0:T], w, x, k == 0, k == nk - 1)
                    else:
                        for h in range(2):
                            m = product(PS[0:rows, 2 * tile.slot + h, 0:HALF], w, tuple(y[:, h * HALF:(h + 1) * HALF] for y in x),
                                        k == 0, k == nk - 1)
                m.then_inc(tile_done, 1)

            def pair_stage(stage, rhs, width=T, split=None):
                for i, tile in enumerate(tiles[stage]):
                    w = parts_view(tile.loads[0], (KD, 2 * P))
                    feature_tile(tile, lambda k: both(w, slice(None), k, slice((i % 2) * P, (i % 2 + 1) * P)), rhs, KD, width,
                                 split=split if i == 0 else None)

            def single_stage(stage, rhs, split=None):
                for i, tile in enumerate(tiles[stage]):
                    w = parts_view(tile.loads[0], (KI, P))
                    feature_tile(tile, lambda k: both(w, slice(None), k), rhs, KI, split=split if i == 0 else None)

            def token_stage(stage, x, ntiles):
                for i, tile in enumerate(tiles[stage]):
                    first = 2 * (i % ((ntiles + 1) // 2))
                    count = min(2, ntiles - first)
                    for j in range(2):
                        open_tile(tile) if j == 0 else weights_in(tile.loads[1])
                        w = parts_view(tile.loads[j], (4, T))
                        for b in range(count):
                            ts_ = slice((first + b) * P, (first + b + 1) * P)
                            for k in range(4):
                                m = product(PS[:, 2 * tile.slot + b, :], both(x, slice(None), 4 * j + k, ts_), both(w, slice(None), k),
                                            j == 0 and k == 0, j == 1 and k == 3)
                    m.then_inc(tile_done, 1)

            def norm(name, width):
                s0, n0, k = NORMS[name]
                if n0 > 0:
                    pe.wait_ge(std_ready, n0)
                for i in range(k):
                    pe.wait_ge(sq_ready, s0 + i + 1)
                    for h in range(2):
                        m = pe.matmul(PA[:, h, 0:width // 2], ones, sq[:, (s0 + i) % 2, h * (width // 2):(h + 1) * (width // 2)],
                                      start=i == 0, stop=i == k - 1)
                    m.then_inc(sq_used, 1)

            pe.wait_ge(con_in, 48)
            pe.wait_ge(pv_in, 16 * 12)
            pe.transpose(PS[:, 0, 0:PV_N], pvr[0:PV_N, 0:P], con[0:PV_N, C_ID:C_ID + PV_N]).then_inc(pv_ps, 1)
            pe.wait_ge(x_in, 16)
            for k in range(KD):
                if k >= 4:
                    pe.wait_ge(xT_sb, k - 3)
                for tt in range(NPAIR):
                    m = pe.transpose(PA[:, k % 4, tt * P:(tt + 1) * P], xtok[:, tt, k * P:(k + 1) * P], ident)
                m.then_inc(xT_ps, 1)
            pe.wait_ge(xT_sb, KD)
            norm("gla", T)
            HTp = (HTh, HTl)
            pair_stage("gla_q", lambda k: both(HTp, slice(None), k), split="gla")
            pair_stage("gla_k", lambda k: both(HTp, slice(None), k))
            w = parts_view(tiles["gla_r"][0].loads[0], (KD, P))
            feature_tile(tiles["gla_r"][0], lambda k: both(w, slice(None), k), lambda k: both(HTp, slice(None), k), KD)
            pe.wait_ge(wg_in, 16)
            read_out(pe, tiles["gla_r"][0])
            for h in range(GH):
                pe.matmul(PA[:, h, :], WG[:, h * P:(h + 1) * P], R16[:], start=True, stop=True).then_inc(gate_ps, 1)
            token_stage("gla_v", HTp, NPAIR)
            for h in range(GH):
                pe.wait_ge(gate_ev, h + 1)
                pe.wait_ge(ke_ready, h + 1)
                for tt in range(NPAIR):
                    m = pe.transpose(PA[:, h, tt * P:(tt + 1) * P], kend[:, h, tt * P:(tt + 1) * P], ident)
                m.then_inc(keT_ps, 1)
            for h in range(GH):
                pe.wait_ge(qkg_ready, h + 1)
                pe.wait_ge(keT_sb, h + 1)
                for tt in range(NPAIR):
                    s = slice(tt * P, (tt + 1) * P)
                    m = pe.matmul(PA[:, h, s], KG[:, h, s], QG[:, h, s], start=True, stop=True)
                m.then_inc(att_ps, 1)
            read_out(pe, tiles["gla_v"][-1])
            read_out(pe, tiles["gla_v"][-2])
            pe.wait_ge(att_sb, GH)
            pe.wait_ge(tp_ready, 1)
            for i in range(8):
                m = pe.transpose(PA[:, 2 + i // 4, (i % 4) * P:(i % 4 + 1) * P], TPg[:, i, :], ident)
            m.then_inc(pt_ps, 1)
            nkv = no = 0
            for tt in range(NPAIR):
                for c in (2 * tt, 2 * tt + 1):
                    if c == NCH - 1:
                        continue
                    for h in range(GH):
                        if nkv >= 2:
                            pe.wait_ge(S_ready, nkv - 1)
                        r = slice((c % 2) * GCH, (c % 2) * GCH + GCH)
                        pe.matmul(PA[:, nkv % 2, :], KE[r, tt, h * P:(h + 1) * P], V[r, tt, h * GDV:(h + 1) * GDV],
                                  start=True, stop=True).then_inc(kv_ps, 1)
                        nkv += 1
                for h in range(GH):
                    if no >= 2:
                        pe.wait_ge(o_sb, no - 1)
                    if no == 0:
                        pe.wait_ge(pt_sb, 1)
                    pe.wait_ge(S_ready, GH * 2 * tt + h + 1)
                    for e in range(4):
                        dst = PA[:, 2 + no % 2, e * P:(e + 1) * P]
                        es = slice(h * GDV + e * P, h * GDV + (e + 1) * P)
                        for c in (2 * tt, 2 * tt + 1):
                            r = slice((c % 2) * GCH, (c % 2) * GCH + GCH)
                            m = pe.matmul(dst[:, r], V[:, tt, es], ATT[:, h, c * GCH:(c + 1) * GCH], start=True, stop=c == 0)
                            if c > 0:
                                m = pe.matmul(dst[:, r], S[:, (c - 1) % 3, es], QG[:, h, c * GCH:(c + 1) * GCH],
                                              start=False, stop=True)
                    m.then_inc(o_ps, 1)
                    no += 1
            for h in range(GH):
                norm(f"head{h}", T)
            pair_stage("gla_z", lambda k: both((HT2h, HT2l), slice(None), k), split="gla2")
            single_stage("gla_out", lambda k: both((Oh, Ol), slice(None), k), split="o")
            norm("s5", T)
            pair_stage("s5_u", lambda k: both((HT5h, HT5l), slice(None), k), split="s5")
            for tile in tiles["s5_u"][-2:]:
                read_out(pe, tile)

            def c_to_columns(b):
                pe.wait_ge(small_in[b % 2], 16 * 7 * (b // 2 + 1))
                if b > 0:
                    pe.wait_ge(cz_sb, b)
                pe.transpose(PA[:, 3, 0:P], CN[:, b % 2, 0:P], ident)
                pe.transpose(PA[:, 3, P:2 * P], CN[:, b % 2, SP_:SP_ + P], ident).then_inc(c_ps, 1)

            def b_to_rows(b):
                pe.wait_ge(bt_ready, 2 * b + 1)
                if b > 0:
                    pe.wait_ge(wb_sb, b)
                for g in range(BG):
                    m = pe.transpose(PS[:, g // 4, (g % 4) * P:(g % 4 + 1) * P], Bt[b % 2][:, g, :], ident)
                m.then_inc(b_ps, 1)

            def inside(b):
                pe.wait_ge(bt_ready, 2 * b + 2)
                pe.wait_ge(w_ready, 2 * b + 1)
                if b > 0:
                    pe.wait_ge(km_ready, 2 * b)
                for g in range(BG):
                    m = pe.matmul(PS[:, 2 + g // 4, (g % 4) * P:(g % 4 + 1) * P], Bn[b % 2][:, g, :], W1[b % 2][:, g, :],
                                  start=True, stop=True)
                m.then_inc(k_ps, 1)

            def additions(b):
                pe.wait_ge(wb_sb, b + 1)
                pe.wait_ge(ub_in[b % 2], 16 * TB * (b // 2 + 1))
                if b > 0:
                    pe.wait_ge(rot_used, b)
                for h in range(2):
                    for g in range(BG):
                        m = pe.matmul(PA[:, 1 + h, g * NB:(g + 1) * NB], WB[:, g, h * SP_:h * SP_ + P], UB[:, b % 2, g, :],
                                      start=True, stop=True)
                m.then_inc(v_ps, 1)

            def outputs(b):
                pe.wait_ge(km_ready, 2 * b + 2)
                pe.wait_ge(w_ready, 2 * b + 2)
                pe.wait_ge(m_ready, 2 * b + 2)
                if b > 0:
                    pe.wait_ge(y_sb, b)
                for g in range(BG):
                    n0 = g * NB
                    pe.matmul(PA[:, 0, n0:n0 + NB], KM[b % 2][:, g, :], UB[:, b % 2, g, :], start=True, stop=False)
                    pe.matmul(PA[:, 0, n0 + 1:n0 + NB], W1[b % 2][:, g, :], M12[:, 0, n0:n0 + NB - 1], start=False, stop=False)
                    m = pe.matmul(PA[:, 0, n0 + 1:n0 + NB], W2[b % 2][:, g, :], M12[:, 1, n0:n0 + NB - 1], start=False, stop=True)
                m.then_inc(y_ps, 1)

            pe.wait_ge(std_ready, NORMS["s5"][1] + 1)
            c_to_columns(0)
            c_to_columns(1)
            b_to_rows(0)
            inside(0)
            for b in range(NBATCH):
                additions(b)
                if b + 2 < NBATCH:
                    c_to_columns(b + 2)
                if b + 1 < NBATCH:
                    b_to_rows(b + 1)
                    inside(b + 1)
                outputs(b)
            pair_stage("s5_z", lambda k: both((HT6h, HT6l), slice(None), k), split="s5z")
            single_stage("s5_glu", lambda k: both((Uh, Ul), slice(None), k), split="g")
            single_stage("s5_out", lambda k: both((Zh, Zl), slice(None), k), split="z")
            norm("fin", T)
            pe.wait_ge(mt_in, 16)
            for k in range(KD):
                m = pe.transpose(PA[:, 2, k * NM:(k + 1) * NM], MT[0:NM, k * P:(k + 1) * P], con[0:NM, C_ID:C_ID + NM])
            m.then_inc(mt_ps, 1)
            norm("attn", T2)
            U2 = (U2h, U2l)

            def queries(k):
                return both(U2, slice(None), k, slice(NM, T2))

            def keyed(k):
                return both(U2, slice(None), k, slice(0, T2))

            pair_stage("cq", queries, split="attn")
            w = parts_view(tiles["ckv"][0].loads[0], (KD, A_QS - A_CKV))
            feature_tile(tiles["ckv"][0], lambda k: both(w, slice(None), k, slice(0, P)), keyed, KD, T2)
            feature_tile(tiles["kr"][0], lambda k: both(w, slice(None), k, slice(A_KR - A_CKV - MNOPE, A_KR - A_CKV + MROPE)),
                         keyed, KD, T2, MQK)
            pair_stage("qs", queries)
            norm("cq", T)
            norm("ckv", T2)
            pe.wait_ge(std_ready, NORMS["ckv"][1] + 1)
            pe.wait_ge(rt_in, 16)

            def rotate(stage):
                for j, (x, lo_row, hi_row, t0, c, tile) in enumerate(rotations(stage)):
                    n = ROT_AT[stage] + j
                    read_out(pe, tile)
                    if n >= 2:
                        pe.wait_ge(ro_read, n - 1)
                    width = T2 - t0
                    rows = P if hi_row == P else MQK
                    perm = rt[0:rows, (R_P if hi_row == P else R_MP):(R_P if hi_row == P else R_MP) + rows]
                    for h in range(2):
                        m = pe.matmul(PA[0:rows, 2 * (n % 2) + h, 0:width // 2], perm, x[0:rows, h * (width // 2):(h + 1) * (width // 2)],
                                      start=True, stop=True)
                    m.then_inc(ro_ps, 1)

            pair_stage("ks", keyed, T2)
            rotate("qs")
            pair_stage("qi", queries)
            rotate("ks")
            w = parts_view(tiles["ki"][0].loads[0], (KD, P))
            feature_tile(tiles["ki"][0], lambda k: both(w, slice(None), k), keyed, KD, T2)
            tile = tiles["wi"][0]
            open_tile(tile)
            wi = parts_view(tile.loads[0], (KD, 8), KD * P)
            for i in range(NPAIR):
                for k in range(KD):
                    m = product(PS[:, 2 * tile.slot, i * 8:(i + 1) * 8], both(U2, slice(None), k, slice(NM + i * P, NM + (i + 1) * P)),
                                both(wi, slice(None), k), k == 0, k == KD - 1)
            m.then_inc(tile_done, 1)
            rotate("qi")
            pe.wait_ge(pad_zero, 2)
            token_stage("vs", U2, 5)
            pe.wait_ge(xlo_ready, sum(SPLITS["cq"]))
            w = parts_view(tiles["uq"][0].loads[0], (2, MH * MQK))
            for h, tile in enumerate(tiles["uq"]):
                feature_tile(tile, lambda k: both(w, slice(None), k, slice(h * MQK, (h + 1) * MQK)),
                             lambda k: both((CQh, CQl), slice(None), k), 2, T, MQK)
            rotate("k1")
            w = parts_view(tiles["ukn"][0].loads[0], (MH * P,))
            pe.wait_ge(xlo_ready, sum(SPLITS["ckv"]))
            pe.wait_ge(pad_zero, 4)
            for h, tile in enumerate(tiles["ukn"]):
                feature_tile(tile, lambda k: both(w, slice(None), slice(h * P, (h + 1) * P)),
                             lambda k: (CKh[:, 0:T2], CKl[:, 0:T2]), 1, T2)
            wv = tuple(x.rearrange("p (h m) -> p h m", h=MH)[:, :, MNOPE:P] for x in w)
            for i, tile in enumerate(tiles["ukvv"]):
                open_tile(tile)
                for b in range(2 if i < 2 else 1):
                    t0 = (2 * i + b) * P
                    m = product(PS[:, 2 * tile.slot + b, :], (CKh[:, t0:t0 + P], CKl[:, t0:t0 + P]), wv, True, True)
                m.then_inc(tile_done, 1)
            rotate("qm")

            pe.wait_ge(roped, 22)
            pe.wait_ge(kr_copied, MH)
            for tile in tiles["ukvv"][-2:]:
                read_out(pe, tile)
            att_n = 0

            def transposed(m):
                i = ATT_UNITS[m][1]
                pe.wait_ge(p_ready, m + 1)
                if m >= 2:
                    pe.wait_ge(oa_ready, m - 1)
                for j in range(i + 2):
                    ins = pe.transpose(PS[:, 2 * (m % 2) + j // 4, (j % 4) * P:(j % 4 + 1) * P], PB[:, m % 2, j * P:(j + 1) * P], ident)
                ins.then_inc(pT_ps, 1)

            def with_values(m):
                kind, i, h = ATT_UNITS[m]
                pe.wait_ge(pT_sb, m + 1)
                vals = Vm if kind == "mla" else VS
                for j in range(i + 2):
                    ins = pe.matmul(PS[:, 2 * (m % 2) + 1, 2 * P:3 * P], vals[:, j, (h // 2) * P:(h // 2 + 1) * P],
                                    PT2[:, m % 2, j * P:(j + 1) * P], start=j == 0, stop=j == i + 1)
                ins.then_inc(pv_out_ps, 1)

            for n, (kind, i, h) in enumerate(UNITS):
                if n >= 2:
                    pe.wait_ge(score_free[n % 2], n // 2)
                nk = keys(i)
                dst = scores(n % 2, i)
                r = slice((h % 2) * 64, (h % 2) * 64 + 64)
                qs = slice(i * P, (i + 1) * P)
                for b in range(dst.shape[1]):
                    w = nk // dst.shape[1]
                    ks = slice(b * w, (b + 1) * w)
                    if kind == "idx":
                        m = pe.matmul(dst[:, b, :], QI[r, h // 2, qs], KI_[r, ks], start=True, stop=True)
                    elif kind == "mla":
                        m = pe.matmul(dst[:, b, :], Qm[0:MQK, h, qs], Km[0:MQK, h, ks], start=True, stop=True)
                    else:
                        m = pe.matmul(dst[:, b, :], QS[r, h // 2, qs], KS[r, h // 2, ks], start=True, stop=True)
                m.then_inc(score_ps, 1)
                if kind != "idx":
                    if att_n >= 1:
                        transposed(att_n - 1)
                    if att_n >= 2:
                        with_values(att_n - 2)
                    att_n += 1
            transposed(att_n - 1)
            with_values(att_n - 2)
            with_values(att_n - 1)
            pair_stage("attn_out", lambda k: both((OAh, OAl), slice(None), k), split="oa")
            norm("ffn", T)
            for i, tile in enumerate(tiles["ffn_up"]):
                open_tile(tile)
                w = parts_view(tile.loads[0], (2 * KD, P))
                for b in range(2):
                    for k in range(KD):
                        if i == b == 0:
                            pe.wait_ge(xlo_ready, SPLITS["ffn"][0] + k + 1)
                        m = product(PS[:, 2 * tile.slot + b, :], both(w, slice(None), b * KD + k), both((U3h, U3l), slice(None), k),
                                    k == 0, k == KD - 1)
                m.then_inc(tile_done, 1)
            for i, tile in enumerate(tiles["ffn_down"]):
                for j in range(2):
                    open_tile(tile) if j == 0 else weights_in(tile.loads[1])
                    w = parts_view(tile.loads[j], (11, P))
                    for k in range(11 * j, 11 * j + 11):
                        if i == 0:
                            pe.wait_ge(xlo_ready, SPLITS["h"][0] + k + 1)
                        m = product(PS[:, 2 * tile.slot, :], both(w, slice(None), k - 11 * j), both((HFh, HFl), slice(None), k),
                                    k == 0, k == KF - 1)
                m.then_inc(tile_done, 1)
            norm("fin2", T)
            norm_applied(pe, "fin2")
            pe.wait_ge(std_ready, NORMS["fin2"][1] + 1)
            for tt in range(NPAIR):
                if tt >= 2:
                    pe.wait_ge(ot_sb, tt - 1)
                for k in range(KD):
                    m = pe.transpose(PA[:, 2 * (tt % 2) + k // 4, (k % 4) * P:(k % 4 + 1) * P], FO[:, k, tt * P:(tt + 1) * P], ident)
                m.then_inc(ot_ps, 1)

        def act_program(act):
            chain = [0]

            def link(ins):
                chain[0] += 1
                ins.then_inc(act_chain, 1)
                act.wait_ge(act_chain, chain[0])

            def norm(name, src, width, dim):
                s0, n0, k = NORMS[name]
                if name in BEFORE:
                    norm_applied(act, BEFORE[name])
                for i in range(k):
                    if s0 + i >= 2:
                        act.wait_ge(sq_used, s0 + i - 1)
                    act.activation(sq[:, (s0 + i) % 2, 0:width], src(i), ACT.Square).then_inc(sq_ready, 1)
                act.wait_ge(sq_used, s0 + k)
                act.activation(rs[:, 0:width].rearrange("p (h n) -> p h n", h=2), PA[:, 0:2, 0:width // 2], ACT.Sqrt,
                               scale=1.0 / dim, bias=con[:, C_EPS:C_EPS + 1]).then_inc(std_ready, 1)

            done = [0]

            def split_weights(upto):
                while done[0] <= min(upto, len(plan.loads) - 1):
                    n = done[0]
                    done[0] += 1
                    act.wait_ge(landed[n % NSLOT], plan.value[n])
                    act.activation(ring_hi[:, n % NSLOT, 0:plan.size[n]], ring[:, n % NSLOT, 0:plan.size[n]], ACT.Copy)\
                        .then_inc(whi_ready, 1)

            def high(name, i, src, dst):
                if name in VALS:
                    act.wait_ge(val_ready, VALS[name] + i + 1)
                act.activation(dst, src, ACT.Copy).then_inc(xhi_ready, 1)

            def high_normed(name, dst, width=T):
                for i in range(SPLITS[name][1]):
                    high(name, i, sq[:, i % 2, 0:width], dst(i))

            def evac(tile, dst, func=ACT.Copy, rows=P, **kw):
                split_weights(tile.loads[-1] + 1)
                act.wait_ge(tile_done, tile.t + 1)
                return act.activation(dst, PS[0:rows, 2 * tile.slot, 0:T], func, **kw).then_inc(slot_free[tile.slot], 1)

            act.dma_start(con[:], a["shape_constants"]).then_inc(con_in, 16)
            act.dma_start(gmask[:], a["chunk_constants"][:, C_GM:C_GM + T]).then_inc(con_in, 16)
            act.dma_start(rst[:], a["chunk_constants"][:, C_RST:C_RST + T]).then_inc(con_in, 16)
            act.wait_ge(pv_ps, 1)
            act.activation(pv[:], PS[:, 0, 0:PV_N], ACT.Copy).then_inc(pv_sb, 1)
            for k in range(KD):
                act.wait_ge(xT_ps, k + 1)
                act.activation(XT[:, k, :], PA[:, k % 4, :], ACT.Copy).then_inc(xT_sb, 1)
            act.wait_ge(xT_sb, KD)
            norm("gla", lambda k: XT[:, k, :], T, D)
            split_weights(0)
            high_normed("gla", lambda i: HTh[:, i, :])
            for i, tile in enumerate(tiles["gla_q"]):
                evac(tile, QG[:, i, :])
            for i, tile in enumerate(tiles["gla_k"]):
                evac(tile, KG[:, i, :])
            tile = tiles["gla_r"][0]
            evac(tile, R16[:])
            act.wait_ge(pv_sb, 1)
            split_weights(tiles["gla_v"][0].loads[1])
            for h in range(GH):
                act.wait_ge(gate_ps, h + 1)
                link(act.activation(LA[:, h, :], PA[:, h, :], ACT.Identity, bias=pv[:, PV_BG + h:PV_BG + h + 1]))
                act.nop().then_inc(gate_ev, 1)
                if h > 0:
                    act.wait_ge(la_ready, h)
                link(act.activation(la_e[:], LA[:, h, :], ACT.Abs))
                link(act.activation(la_e[:], la_e[:], ACT.Exp, scale=-1.0))
                act.activation(la_e[:], la_e[:], ACT.Ln, bias=con[:, C_ONE:C_ONE + 1]).then_inc(gl_ready, 1)
                act.wait_ge(la_ready, h + 1)
                if h > 0:
                    act.wait_ge(qkg_ready, h)
                act.activation(ex_p[:], LA[:, h, :], ACT.Exp, scale=1.0 / GTAU).then_inc(ex_ready, 1)
                act.activation(ex_n[:], LA[:, h, :], ACT.Exp, scale=-1.0 / GTAU).then_inc(ex_ready, 1)
                act.wait_ge(de_ready, h + 1)
                act.activation(kend[:, h, :], kend[:, h, :], ACT.Exp, scale=1.0 / GTAU).then_inc(kx_ready, 1)
            for i, tile in enumerate(tiles["gla_v"]):
                split_weights(tile.loads[-1] + 1)
                act.wait_ge(tile_done, tile.t + 1)
                tt = (i % 2) * 2
                act.activation(V[:, tt:tt + 2, (i // 2) * T:(i // 2 + 1) * T], PS[:, 2 * tile.slot:2 * tile.slot + 2, :], ACT.Copy)\
                    .then_inc(slot_free[tile.slot], 1)
                if i == 4:
                    act.wait_ge(gx_ready, 1)
                    act.activation(gt[:, 8, :], gt[:, 7, :], ACT.Sin, scale=TWO_PI).then_inc(sin_ready, 1)
                    act.activation(gt[:, 9, :], gt[:, 7, :], ACT.Sin, scale=TWO_PI / 2).then_inc(sin_ready, 1)
            for h in range(GH):
                act.wait_ge(keT_ps, h + 1)
                act.activation(KE[:, :, h * P:(h + 1) * P], PA[:, h, :].rearrange("p (t d) -> p t d", t=NPAIR), ACT.Copy)\
                    .then_inc(keT_sb, 1)
            act.wait_ge(pt_ps, 1)
            act.activation(PT[:].rearrange("p a b -> p (a b)").rearrange("p (a b) -> p a b", a=2), PA[:, 2:4, :], ACT.Copy)\
                .then_inc(pt_sb, 1)
            n = 0
            for tt in range(NPAIR):
                for h in range(GH):
                    act.wait_ge(o_ps, n + 1)
                    act.activation(O[:, 4 * h:4 * h + 4, tt * P:(tt + 1) * P],
                                   PA[:, 2 + n % 2, :].rearrange("p (e c) -> p e c", e=4), ACT.Copy).then_inc(o_sb, 1)
                    n += 1
            act.wait_ge(o_sb, n)
            high_normed("gla2", lambda i: HT2h[:, i, :])
            norm_applied(act, "gla2")
            for h in range(GH):
                norm(f"head{h}", lambda k: O[:, 4 * h + k, :], T, GDV)
            for i, tile in enumerate(tiles["gla_z"]):
                split_weights(tile.loads[-1] + 1)
                if i >= 2:
                    act.wait_ge(val_ready, VALS["o"] + i - 1)
                act.wait_ge(tile_done, tile.t + 1)
                act.activation(SZ[:, i % 2, :], PS[:, 2 * tile.slot, :], ACT.Silu).then_inc(slot_free[tile.slot], 1)
                if i > 0:
                    high("o", i - 1, O[:, i - 1, :], Oh[:, i - 1, :])
            high("o", KI - 1, O[:, KI - 1, :], Oh[:, KI - 1, :])
            for tile in tiles["gla_out"]:
                split_weights(tile.loads[-1] + 1)
                act.wait_ge(tile_done, tile.t + 1)
            for tile in tiles["gla_out"][-2:]:
                read_out(act, tile)
            norm("s5", lambda k: XT[:, k, :], T, D)
            for i in range(KD):
                high("s5", i, HT[:, i, :], HT5h[:, i, :])
            for i, tile in enumerate(tiles["s5_u"]):
                split_weights(min(tile.loads[-1] + 1, tiles["s5_u"][-1].loads[0]))
                act.wait_ge(tile_done, tile.t + 1)
                act.activation(U[:, i, :], PS[:, 2 * tile.slot, :], ACT.Copy).then_inc(slot_free[tile.slot], 1)
                read_out(act, tile)
                act.dma_start(u_dram[i * P:(i + 1) * P, :], U[:, i, :]).then_inc(u_out, 16)

            def columns(b):
                act.wait_ge(c_ps, b + 1)
                if b >= 2:
                    act.wait_ge(w_ready, 2 * (b - 1))
                act.activation(CZ[:, b % 2, :], PA[:, 3, 0:2 * P], ACT.Copy).then_inc(cz_sb, 1)

            def rotations_of(b):
                act.wait_ge(frac_ready, b + 1)
                act.activation(rot_s[:, b % 2, :], rot_c[:, b % 2, :], ACT.Sin, scale=sg2pi[:, 0:1]).then_inc(rot_ready, 1)
                link(act.activation(rot_c[:, b % 2, :], rot_c[:, b % 2, :], ACT.Abs))
                act.activation(rot_c[:, b % 2, :], rot_c[:, b % 2, :], ACT.Sin, scale=-TWO_PI, bias=con[:, C_HPI:C_HPI + 1])\
                    .then_inc(rot_ready, 1)

            def b_rows(b):
                act.wait_ge(b_ps, b + 1)
                if b > 0:
                    act.wait_ge(v_ps, b)
                bt4 = PS[:, 0:2, :].rearrange("p a (g m) -> p a g m", g=4)
                act.activation(WB[:, :, 0:P].rearrange("p (a g) m -> p a g m", a=2), bt4, ACT.Copy)
                act.activation(WB[:, :, P:P + SP_].rearrange("p (a g) m -> p a g m", a=2), bt4[:, :, :, 0:SP_], ACT.Copy)\
                    .then_inc(wb_sb, 1)

            columns(0)
            columns(1)
            rotations_of(0)
            b_rows(0)
            rotations_of(1)
            for b in range(NBATCH):
                if b + 2 < NBATCH:
                    columns(b + 2)
                if b + 1 < NBATCH:
                    b_rows(b + 1)
                act.wait_ge(y_ps, b + 1)
                if b > 0:
                    act.wait_ge(y_out, 16 * TB * b)
                act.activation(YB, PA[:, 0, :], ACT.Copy).then_inc(y_sb, 1)
                act.wait_ge(y_sb, b + 1)
                dst = y_dram[b * P:(b + 1) * P, :].rearrange("(g i) (t n) -> t i g n", g=BG, t=TB)
                for t in range(TB):
                    act.dma_start(dst[t], YB[t * SGRP:(t + 1) * SGRP, :].rearrange("p (g n) -> p g n", g=BG)).then_inc(y_out, 16)
                if b + 2 < NBATCH:
                    rotations_of(b + 2)
            for i in range(KD):
                high("s5z", i, HT[:, i, :], HT6h[:, i, :])
                if i == 0:
                    split_weights(tiles["s5_z"][0].loads[0])
            for b in range(NBATCH):
                act.wait_ge(yd_ready, b + 1)
                act.activation(U[:, b, :], U[:, b, :], ACT.Gelu_apprx_tanh).then_inc(gelu_done, 1)
                if b == 7:
                    split_weights(tiles["s5_z"][0].loads[0] + 1)
            act.wait_ge(gelu_done, NBATCH)
            for i, tile in enumerate(tiles["s5_z"]):
                split_weights(tile.loads[-1] + 1)
                act.wait_ge(tile_done, tile.t + 1)
                act.activation(Z[:, i, :], PS[:, 2 * tile.slot, :], ACT.Silu).then_inc(slot_free[tile.slot], 1)
                high("g", i, U[:, i, :], Uh[:, i, :])
            for i, tile in enumerate(tiles["s5_glu"]):
                split_weights(tile.loads[-1] + 1)
                if i >= 2:
                    act.wait_ge(val_ready, VALS["z"] + i - 1)
                act.wait_ge(tile_done, tile.t + 1)
                act.activation(sq[:, i % 2, 0:T], PS[:, 2 * tile.slot, :], ACT.Sigmoid, bias=pv[:, PV_BGLU + i:PV_BGLU + i + 1])\
                    .then_inc(slot_free[tile.slot], 1)
                if i > 0:
                    high("z", i - 1, Z[:, i - 1, :], Zh[:, i - 1, :])
            high("z", KI - 1, Z[:, KI - 1, :], Zh[:, KI - 1, :])
            for tile in tiles["s5_out"]:
                split_weights(tile.loads[-1] + 1)
                act.wait_ge(tile_done, tile.t + 1)
            for tile in tiles["s5_out"][-2:]:
                read_out(act, tile)
            norm("fin", lambda k: XT[:, k, :], T, D)
            act.wait_ge(mt_ps, 1)
            act.activation(X2[:, :, 0:NM], PA[:, 2, 0:KD * NM].rearrange("p (k m) -> p k m", k=KD), ACT.Copy).then_inc(mt_sb, 1)
            act.wait_ge(mt_sb, 1)
            norm("attn", lambda k: X2[:, k, :], T2, D)
            high_normed("attn", lambda i: U2h[:, i, 0:T2], T2)

            def wide(tile, dst, rows=slice(0, P)):
                split_weights(tile.loads[-1] + 1)
                act.wait_ge(tile_done, tile.t + 1)
                act.activation(dst.rearrange("p (h n) -> p h n", h=2), PS[rows, 2 * tile.slot:2 * tile.slot + 2, 0:HALF], ACT.Copy)\
                    .then_inc(slot_free[tile.slot], 1)

            for i, tile in enumerate(tiles["cq"]):
                evac(tile, CQ[:, i, :])
            wide(tiles["ckv"][0], CK[:, 0:T2])
            wide(tiles["kr"][0], KR[0:MQK, :], slice(0, MQK))
            for i, tile in enumerate(tiles["qs"]):
                evac(tile, QS[:, i, :])
            for tile in (*tiles["cq"], *tiles["ckv"]):
                read_out(act, tile)
            norm("cq", lambda k: CQ[:, k, :], T, MQR)
            high_normed("cq", lambda i: CQh[:, i, :])
            norm("ckv", lambda k: CK[:, 0:T2], T2, MKR)
            high_normed("ckv", lambda i: CKh[:, 0:T2], T2)
            for i, tile in enumerate(tiles["ks"]):
                wide(tile, KS[:, i, :])
            for i, tile in enumerate(tiles["qi"]):
                evac(tile, QI[:, i, :])
            wide(tiles["ki"][0], KI_[:])
            tile = tiles["wi"][0]
            act.wait_ge(tile_done, tile.t + 1)
            act.activation(WI[:], PS[:, 2 * tile.slot, 0:NPAIR * 8].rearrange("p (i h) -> p i h", i=NPAIR), ACT.Copy, scale=8 ** -0.5)\
                .then_inc(slot_free[tile.slot], 1)

            def values(stage, dst):
                for i, tile in enumerate(tiles[stage]):
                    split_weights(tile.loads[-1] + 1)
                    act.wait_ge(tile_done, tile.t + 1)
                    nb = 2 if i < 2 else 1
                    act.activation(dst[:, 2 * i:2 * i + nb, :], PS[:, 2 * tile.slot:2 * tile.slot + nb, :], ACT.Copy)\
                        .then_inc(slot_free[tile.slot], 1)

            values("vs", VS)
            for h, tile in enumerate(tiles["uq"]):
                evac(tile, Qm[0:MQK, h, :], rows=MQK)
            for h, tile in enumerate(tiles["ukn"]):
                wide(tile, Km[0:MNOPE, h, :], slice(0, MNOPE))
            values("ukvv", Vm)
            split_weights(tiles["attn_out"][0].loads[0] + NSLOT - 1)

            n_idx = n_att = 0

            def copy_transposed(m):
                i = ATT_UNITS[m][1]
                act.wait_ge(pT_ps, m + 1)
                if m >= 2:
                    act.wait_ge(pv_out_ps, m - 1)
                act.activation(PT2[:, m % 2, 0:(i + 2) * P],
                               PS[:, 2 * (m % 2):2 * (m % 2) + 2, :].rearrange("p a b -> p (a b)")[:, 0:(i + 2) * P], ACT.Copy)\
                    .then_inc(pT_sb, 1)

            for n, (kind, i, h) in enumerate(UNITS):
                nk = keys(i)
                if kind == "idx":
                    act.wait_ge(score_ps, n + 1)
                    if n_idx >= 2:
                        act.wait_ge(acc_used, n_idx - 1)
                    act.activation(split(RL[:, n_idx % 2, 0:nk], i), scores(n % 2, i), ACT.Relu, scale=64 ** -0.5)\
                        .then_inc(score_free[n % 2], 1)
                    act.wait_ge(score_free[n % 2], n // 2 + 1)
                    act.nop().then_inc(relu_ready, 1)
                    n_idx += 1
                    continue
                scale = (MQK if kind == "mla" else DHD) ** -0.5
                pair = n_att % 2
                act.wait_ge(max_ready, n_att + 1)
                act.activation(PB[:, pair, 0:nk], PB[:, pair, 0:nk], ACT.Exp, scale=scale, bias=mx[:, pair, 1:2],
                               accum_out=mx[:, pair, 2:3]).then_inc(exp_ready, 1)
                if n_att >= 1:
                    copy_transposed(n_att - 1)
                n_att += 1
            copy_transposed(n_att - 1)
            act.wait_ge(oa_ready, 2 * MH * NPAIR)
            for i in range(KD):
                high("oa", i, OA[:, i, :], OAh[:, i, :])
            for tile in tiles["attn_out"]:
                split_weights(tile.loads[-1] + 1)
                act.wait_ge(tile_done, tile.t + 1)
            for tile in tiles["attn_out"][-2:]:
                read_out(act, tile)
            norm("ffn", lambda k: X2[:, k, NM:T2], T, D)
            high_normed("ffn", lambda i: U3h[:, i, :])
            for i, tile in enumerate(tiles["ffn_up"]):
                split_weights(tile.loads[-1] + 1)
                act.wait_ge(tile_done, tile.t + 1)
                if i >= 2:
                    read_out(act, tiles["ffn_up"][i - 2])
                act.activation(SF[:, i % 2, :], PS[:, 2 * tile.slot, :], ACT.Silu).then_inc(silu_ready, 1)
                if i > 0:
                    read_out(act, tiles["ffn_up"][i - 1])
                    high("h", i - 1, HF[:, i - 1, :], HFh[:, i - 1, :])
            read_out(act, tiles["ffn_up"][-1])
            high("h", KF - 1, HF[:, KF - 1, :], HFh[:, KF - 1, :])
            for tile in tiles["ffn_down"]:
                split_weights(tile.loads[-1] + 1)
                act.wait_ge(tile_done, tile.t + 1)
            for tile in tiles["ffn_down"][-2:]:
                read_out(act, tile)
            norm("fin2", lambda k: X2[:, k, NM:T2], T, D)
            for tt in range(NPAIR):
                act.wait_ge(ot_ps, tt + 1)
                act.activation(OT[:, tt, :], PA[:, 2 * (tt % 2):2 * (tt % 2) + 2, :].rearrange("p a b -> p (a b)"), ACT.Copy)\
                    .then_inc(ot_sb, 1)

        def dve_program(dve):
            chain = [0]

            def link(ins):
                chain[0] += 1
                ins.then_inc(dve_chain, 1)
                dve.wait_ge(dve_chain, chain[0])

            def low(name, i, src, hi, lo_):
                dve.wait_ge(xhi_ready, SPLITS[name][0] + i + 1)
                dve.tensor_tensor(lo_, src, hi.bitcast(F32), ALU.subtract).then_inc(xlo_ready, 1)

            def scales(name, width):
                n0 = NORMS[name][1]
                dve.wait_ge(std_ready, n0 + 1)
                dve.reciprocal(rs[:, 0:width], rs[:, 0:width]).then_inc(rstd_ready, 1)
                dve.wait_ge(rstd_ready, n0 + 1)

            def norm(name, src, dst, gain, width):
                scales(name, width)
                for i in range(NORMS[name][2]):
                    dve.scalar_tensor_tensor(out=dst(i), in0=src(i), scalar=pv[:, gain + i:gain + i + 1], in1=rs[:, 0:width],
                                             op0=ALU.mult, op1=ALU.mult).then_inc(normed, 1)

            def norm_split(name, src, hi, lo_, gain, width, r=None):
                r = rs if r is None else r
                k = SPLITS[name][1]
                for i in range(k + 1):
                    if i < k:
                        if i >= 2:
                            dve.wait_ge(xlo_ready, SPLITS[name][0] + i - 1)
                        dve.scalar_tensor_tensor(out=sq[:, i % 2, 0:width], in0=src(i), scalar=pv[:, gain + i:gain + i + 1],
                                                 in1=r[:, 0:width], op0=ALU.mult, op1=ALU.mult).then_inc(val_ready, 1)
                    if i > 0:
                        low(name, i - 1, sq[:, (i - 1) % 2, 0:width], hi(i - 1), lo_(i - 1))

            tt, ts, stt = dve.tensor_tensor, dve.tensor_scalar, dve.scalar_tensor_tensor
            dve.memset(WG[:], 0.0).then_inc(wg_zero, 1)
            dve.wait_ge(con_in, 48)
            dve.wait_ge(pv_sb, 1)
            dve.wait_ge(xT_sb, KD)
            scales("gla", T)
            norm_split("gla", lambda k: XT[:, k, :], lambda k: HTh[:, k, :], lambda k: HTl[:, k, :], PV_GLA, T)
            for i in (-2, -1):
                read_out(dve, tiles["gla_k"][i])
            for h in range(GH):
                dve.wait_ge(gl_ready, h + 1)
                link(dve.scalar_tensor_tensor(out=LA[:, h, :], in0=LA[:, h, :], scalar=0.0, in1=la_e[:],
                                              op0=ALU.min, op1=ALU.subtract))
                dve.tensor_tensor_scan(LA[:, h, :], rst[:], LA[:, h, :], 0.0, ALU.mult, ALU.add)\
                    .then_inc(la_ready, 1)
                dve.wait_ge(la_ready, h + 1)
                la3 = LA[:, h, :].rearrange("p (c t) -> p c t", t=GCH)
                last = la3[:, :, GCH - 1:GCH]
                dve.tensor_tensor(kend[:, h, :].rearrange("p (c t) -> p c t", t=GCH), last.broadcast_to([P, NCH, GCH]), la3,
                                  ALU.subtract).then_inc(de_ready, 1)
                dve.wait_ge(ex_ready, 2 * h + 2)
                link(dve.tensor_copy(dec[:, h, :], ex_p[:].rearrange("p (c t) -> p c t", t=GCH)[:, :, GCH - 1]))
                link(dve.scalar_tensor_tensor(out=QG[:, h, :], in0=QG[:, h, :], scalar=GDK ** -0.5, in1=ex_p[:],
                                              op0=ALU.mult, op1=ALU.mult))
                dve.wait_ge(kx_ready, h + 1)
                dve.tensor_tensor(kend[:, h, :], kend[:, h, :], KG[:, h, :], ALU.mult).then_inc(ke_ready, 1)
                dve.wait_ge(ke_ready, h + 1)
                dve.tensor_tensor(KG[:, h, :], KG[:, h, :], ex_n[:], ALU.mult).then_inc(qkg_ready, 1)
            dve.wait_ge(qkg_ready, GH)
            link(dve.memset(ATT[:].rearrange("p a b -> p (a b)"), 0.0))
            dve.wait_ge(par_in, 16 * 3)

            def mul(o, x, y):
                link(tt(o, x, y, ALU.mult))

            def round_to(o, x):
                link(ts(o, x, ROUND, ROUND, ALU.add, ALU.subtract))

            def expm1(x, n, r, t, p2, ni):
                link(ts(n, x, 1 / math.log(2), None, ALU.mult))
                round_to(n, n)
                ln2_hi = 0.693359375
                link(stt(out=r, in0=n, scalar=-ln2_hi, in1=x, op0=ALU.mult, op1=ALU.add))
                link(stt(out=r, in0=n, scalar=ln2_hi - math.log(2), in1=r, op0=ALU.mult, op1=ALU.add))
                link(ts(t, r, 1 / 8, 1.0, ALU.mult, ALU.add))
                for m in range(7, 1, -1):
                    mul(t, t, r)
                    link(ts(t, t, 1 / m, 1.0, ALU.mult, ALU.add))
                mul(t, t, r)
                link(ts(n, n, 127.0, None, ALU.add))
                link(dve.tensor_copy(ni, n))
                link(dve.tensor_single_scalar(p2.bitcast(I32), ni, 23, ALU.logical_shift_left))

            g = [gt[:, i, :] for i in range(16)]
            d = [gdt[:, i:i + 1] for i in range(8)]
            link(ts(d[1], d[0], -80.0, 80.0, ALU.max, ALU.min))
            expm1(d[1], d[2], d[3], d[4], d[5], gi[:, 0:1])
            mul(d[4], d[4], d[5])
            link(tt(d[6], d[4], d[5], ALU.add))
            link(ts(g[0], glr[:], d[6], A_MIN, ALU.mult, ALU.max))
            link(ts(g[6], gli[:], d[6], 1 / (2 * math.pi), ALU.mult, ALU.mult))
            round_to(g[7], g[6])
            tt(g[7], g[6], g[7], ALU.subtract).then_inc(gx_ready, 1)
            dve.wait_ge(gx_ready, 1)
            expm1(g[0], g[1], g[2], g[3], g[4], gi[:])
            mul(g[3], g[3], g[4])
            link(stt(out=g[5], in0=g[4], scalar=-1.0, in1=g[3], op0=ALU.add, op1=ALU.add))
            link(tt(g[4], g[3], g[4], ALU.add))
            dve.wait_ge(sin_ready, 2)
            mul(g[9], g[9], g[9])
            link(ts(g[9], g[9], 2.0, None, ALU.mult))
            link(ts(g[10], g[9], -1.0, 1.0, ALU.mult, ALU.add))
            tp = [TPg[:, i, 0:SP_] for i in range(8)]
            mul(tp[0], g[4], g[10])
            mul(tp[1], g[4], g[8])
            mul(g[11], g[5], g[10])
            link(tt(g[11], g[11], g[9], ALU.subtract))
            link(dve.reciprocal(g[12], g[4]))
            mul(tp[2], g[12], g[10])
            link(stt(out=tp[3], in0=g[12], scalar=-1.0, in1=g[8], op0=ALU.mult, op1=ALU.mult))
            mul(g[12], glr[:], glr[:])
            mul(g[13], gli[:], gli[:])
            link(tt(g[12], g[12], g[13], ALU.add))
            link(dve.reciprocal(g[12], g[12]))
            mul(g[13], g[11], glr[:])
            mul(g[14], tp[1], gli[:])
            link(tt(g[13], g[13], g[14], ALU.add))
            mul(tp[4], g[13], g[12])
            mul(g[13], tp[1], glr[:])
            mul(g[14], g[11], gli[:])
            link(tt(g[13], g[13], g[14], ALU.subtract))
            mul(tp[5], g[13], g[12])
            mul(g[13], g[4], g[4])
            mul(g[13], g[13], g[13])
            mul(tp[6], g[13], g[13])
            link(ts(g[13], g[7], float(TB), None, ALU.mult))
            round_to(g[14], g[13])
            link(tt(tp[7], g[13], g[14], ALU.subtract))
            dve.tensor_copy(TPg[:, :, SP_:P], TPg[:, :, 0:SP_]).then_inc(tp_ready, 1)

            for h in range(GH):
                dve.wait_ge(att_ps, h + 1)
                dve.copy_predicated(ATT[:, h, :], gmask[:].bitcast(U32), PA[:, h, :]).then_inc(att_sb, 1)
            dve.wait_ge(keT_ps, GH)
            for tile in tiles["gla_v"][-2:]:
                read_out(dve, tile)
            link(dve.tensor_copy(rs2[:], rs[:, 0:T]))
            n = 0
            for c in range(NCH - 1):
                for h in range(GH):
                    dve.wait_ge(kv_ps, n + 1)
                    if c >= 3:
                        dve.wait_ge(o_ps, GH * ((c - 2) // 2) + h + 1)
                    if c > 0:
                        dve.wait_ge(S_ready, n - GH + 1)
                    hs = slice(h * GDV, (h + 1) * GDV)
                    if c == 0:
                        dve.tensor_copy(S[:, 0, hs], PA[:, n % 2, :]).then_inc(S_ready, 1)
                    else:
                        dve.scalar_tensor_tensor(out=S[:, c % 3, hs], in0=S[:, (c - 1) % 3, hs], scalar=dec[:, h, c:c + 1],
                                                 in1=PA[:, n % 2, :], op0=ALU.mult, op1=ALU.add).then_inc(S_ready, 1)
                    n += 1
            dve.wait_ge(o_sb, GH * NPAIR)
            norm_split("gla2", lambda k: XT[:, k, :], lambda k: HT2h[:, k, :], lambda k: HT2l[:, k, :], PV_GLA, T, rs2)
            for h in range(GH):
                norm(f"head{h}", lambda k: O[:, 4 * h + k, :], lambda k: O[:, 4 * h + k, :], PV_HG, T)
            norm_applied(dve, "head3")
            for i, tile in enumerate(tiles["gla_z"]):
                read_out(dve, tile)
                dve.tensor_tensor(O[:, i, :], O[:, i, :], SZ[:, i % 2, :], ALU.mult).then_inc(val_ready, 1)
                if i > 0:
                    low("o", i - 1, O[:, i - 1, :], Oh[:, i - 1, :], Ol[:, i - 1, :])
            low("o", KI - 1, O[:, KI - 1, :], Oh[:, KI - 1, :], Ol[:, KI - 1, :])
            dve.wait_ge(pt_sb, 1)
            L, LI, CO = (PT[:, 0, :], PT[:, 1, :]), (PT[:, 2, :], PT[:, 3, :]), (PT[:, 4, :], PT[:, 5, :])

            def cmul(dst, x, y):
                link(tt(ctmp[:, 0, :], x[1], y[1], ALU.mult))
                link(tt(ctmp[:, 1, :], x[1], y[0], ALU.mult))
                link(tt(dst[0], x[0], y[0], ALU.mult))
                link(tt(dst[1], x[0], y[1], ALU.mult))
                link(tt(dst[0], dst[0], ctmp[:, 0, :], ALU.subtract))
                link(tt(dst[1], dst[1], ctmp[:, 1, :], ALU.add))

            def pw(i, k):
                return PW[:, 2 * i, k, :], PW[:, 2 * i + 1, k, :]

            for c in range(2):
                link(dve.tensor_copy(pw(0, 0)[c], L[c]))
                link(dve.tensor_copy(pw(1, TB - 1)[c], CO[c]))
            cmul(pw(2, 0), CO, LI)
            for i, tile in enumerate(tiles["gla_out"]):
                if i > 0:
                    cmul(pw(0, i), pw(0, i - 1), L)
                    cmul(pw(1, TB - 1 - i), pw(1, TB - i), L)
                    cmul(pw(2, i), pw(2, i - 1), LI)
                dve.wait_ge(tile_done, tile.t + 1)
                dve.tensor_tensor(XT[:, i, :], XT[:, i, :], PS[:, 2 * tile.slot, :], ALU.add).then_inc(slot_free[tile.slot], 1)
            link(dve.tensor_copy(r8f8[:], PT[:, 6:8, :]))
            link(ts(sg2pi[:, 0:1], con[:, C_SG:C_SG + 1], TWO_PI, None, ALU.mult))
            sg, nsg = con[:, C_SG:C_SG + 1], con[:, C_NSG:C_NSG + 1]
            for i, scale in ((0, sg), (1, -1.0), (3, nsg), (5, nsg)):
                v = PW[:, i, :, :].rearrange("p a b -> p (a b)")
                link(ts(v, v, scale, None, ALU.mult))
            dve.nop().then_inc(pw_ready, 1)


            for tile in tiles["gla_out"][-2:]:
                read_out(dve, tile)
            scales("s5", T)
            for i in range(KD + 1):
                if i < KD:
                    stt(out=sn(HT[:, i, :]), in0=by_block(XT[:, i, :]), scalar=pv[:, PV_S5 + i:PV_S5 + i + 1],
                        in1=by_block(rs[:, 0:T]), op0=ALU.mult, op1=ALU.mult).then_inc(val_ready, 1)
                if i > 0:
                    low("s5", i - 1, HT[:, i - 1, :], HT5h[:, i - 1, :], HT5l[:, i - 1, :])
            def factor(i, b):
                return PW[:, i, :, b * BG:(b + 1) * BG].rearrange("p k g -> p g k").unsqueeze(3).broadcast_to([P, BG, TB, SGRP])

            def rows(ap):
                return ap.rearrange("p g j -> p g j").unsqueeze(2).broadcast_to([P, BG, TB, SGRP])

            def four(ap):
                return ap.rearrange("p g (s j) -> p g s j", s=TB)

            def add_skip(b):
                dve.wait_ge(y_in, 16 * (b + 1))
                stt(out=U[:, b, :], in0=U[:, b, :], scalar=pv[:, PV_DS + b:PV_DS + b + 1], in1=YIN, op0=ALU.mult, op1=ALU.add)\
                    .then_inc(yd_ready, 1)

            def b_factors(b, which):
                p, dst, i = b % 2, (Bt, Bn)[which][b % 2], (2, 4)[which]
                dve.wait_ge(small_in[p], 16 * 7 * (b // 2 + 1))
                if b >= 2:
                    dve.wait_ge((b_ps, y_ps)[which], b - 1)
                link(tt(four(dst[:]), factor(i, b), rows(BZ[:, p, 0]), ALU.mult))
                link(tt(four(b_tmp[:]), factor(i + 1, b), rows(BZ[:, p, 1]), ALU.mult))
                tt(dst[:], dst[:], b_tmp[:], ALU.add).then_inc(bt_ready, 1)
                dve.wait_ge(bt_ready, 2 * b + 1 + which)

            def turns(b):
                rc, rk = rot_c[:, b % 2, :], rot_s[:, b % 2, :]
                if b >= 2:
                    dve.wait_ge(m_ready, 2 * (b - 1))
                link(tt(rc.rearrange("p (g n) -> p g n", g=BG),
                        r8f8[:, 1, b * BG:(b + 1) * BG].unsqueeze(2).broadcast_to([P, BG, NB]),
                        con[:, C_NI:C_NI + NB].unsqueeze(1).broadcast_to([P, BG, NB]), ALU.mult))
                round_to(rk, rc)
                tt(rc, rc, rk, ALU.subtract).then_inc(frac_ready, 1)

            def masked(b):
                dve.wait_ge(k_ps, b + 1)
                for h in range(2):
                    tt(KM[b % 2][:, 4 * h:4 * h + 4, :].rearrange("p g m -> p (g m)"), PS[:, 2 + h, :], con[:, C_SM:C_SM + T], ALU.mult)\
                        .then_inc(km_ready, 1)

            def scan(b):
                cos, sin = rot_c[:, b % 2, :], rot_s[:, b % 2, :]
                dve.wait_ge(rot_ready, 2 * b + 2)
                dve.wait_ge(v_ps, b + 1)
                link(tt(M12[:, 0, :], PA[:, 1, :], cos, ALU.mult))
                tt(M12[:, 1, :], PA[:, 2, :], sin, ALU.mult).then_inc(rot_used, 1)
                dve.wait_ge(rot_used, b + 1)
                link(tt(M12[:, 0, :], M12[:, 0, :], M12[:, 1, :], ALU.add))
                dve.wait_ge(dk_ready, b + 1)
                link(dve.tensor_tensor_scan(M12[:, 1, :], dk[:, b % 2, :], M12[:, 0, :], 0.0, ALU.mult, ALU.add))
                tt(M12[:, 0, :], M12[:, 1, :], cos, ALU.mult).then_inc(m_ready, 1)
                dve.wait_ge(m_ready, 2 * b + 1)
                tt(M12[:, 1, :], M12[:, 1, :], sin, ALU.mult).then_inc(m_ready, 1)

            dve.wait_ge(tile_done, tiles["s5_u"][-1].t + 1)
            for b in range(2):
                for which in range(2):
                    b_factors(b, which)
                turns(b)
            masked(0)
            for b in range(NBATCH):
                scan(b)
                if b + 1 < NBATCH:
                    masked(b + 1)
                if b + 2 < NBATCH:
                    turns(b + 2)
                    for which in range(2):
                        b_factors(b + 2, which)
                if b > 0:
                    add_skip(b - 1)
            for i in range(KD):
                low("s5z", i, HT[:, i, :], HT6h[:, i, :], HT6l[:, i, :])
            add_skip(NBATCH - 1)
            for i, tile in enumerate(tiles["s5_z"]):
                dve.wait_ge(gelu_done, NBATCH)
                read_out(dve, tile)
                tt(Z[:, i, :], Z[:, i, :], U[:, i, :], ALU.mult).then_inc(oz_ready, 1)
                low("g", i, U[:, i, :], Uh[:, i, :], Ul[:, i, :])
            for i, tile in enumerate(tiles["s5_glu"]):
                read_out(dve, tile)
                tt(Z[:, i, :], Z[:, i, :], sq[:, i % 2, 0:T], ALU.mult).then_inc(val_ready, 1)
                if i > 0:
                    low("z", i - 1, Z[:, i - 1, :], Zh[:, i - 1, :], Zl[:, i - 1, :])
            low("z", KI - 1, Z[:, KI - 1, :], Zh[:, KI - 1, :], Zl[:, KI - 1, :])
            for i, tile in enumerate(tiles["s5_out"]):
                dve.wait_ge(tile_done, tile.t + 1)
                tt(by_block(XT[:, i, :]), by_block(XT[:, i, :]), sn(PS[:, 2 * tile.slot, :]), ALU.add).then_inc(slot_free[tile.slot], 1)
            for tile in tiles["s5_out"][-2:]:
                read_out(dve, tile)
            norm("fin", lambda k: XT[:, k, :], lambda k: X2[:, k, NM:T2], PV_FIN, T)
            dve.memset(U2h[:, :, T2:TPAD].bitcast(F32), 0.0).then_inc(pad_zero, 1)
            dve.memset(U2l[:, :, T2:TPAD].bitcast(F32), 0.0).then_inc(pad_zero, 1)
            dve.wait_ge(mt_sb, 1)
            norm_applied(dve, "fin")
            scales("attn", T2)
            norm_split("attn", lambda k: X2[:, k, :], lambda k: U2h[:, k, 0:T2], lambda k: U2l[:, k, 0:T2], PV_ATT, T2)
            dve.memset(CKh[:, T2:TPAD].bitcast(F32), 0.0).then_inc(pad_zero, 1)
            dve.memset(CKl[:, T2:TPAD].bitcast(F32), 0.0).then_inc(pad_zero, 1)
            scales("cq", T)
            norm_split("cq", lambda k: CQ[:, k, :], lambda k: CQh[:, k, :], lambda k: CQl[:, k, :], PV_GQ, T)
            scales("ckv", T2)
            norm_split("ckv", lambda k: CK[:, 0:T2], lambda k: CKh[:, 0:T2], lambda k: CKl[:, 0:T2], PV_GKV, T2)
            dve.wait_ge(rt_in, 16)
            for stage in ROT_STAGES:
                for j, (x, lo_row, hi_row, t0, c, tile) in enumerate(rotations(stage)):
                    n = ROT_AT[stage] + j
                    width = T2 - t0
                    r = slice(lo_row, hi_row)
                    sin = c + T2
                    dve.wait_ge(ro_ps, n + 1)
                    tt(halves(ro[r, n % 2, 0:width], 2), PA[r, 2 * (n % 2):2 * (n % 2) + 2, 0:width // 2],
                       halves(rt[r, sin + t0:sin + T2], 2), ALU.mult).then_inc(ro_read, 1)
                    link(tt(x[r, :], x[r, :], rt[r, c + t0:c + T2], ALU.mult))
                    dve.wait_ge(ro_read, n + 1)
                    tt(x[r, :], x[r, :], ro[r, n % 2, 0:width], ALU.add).then_inc(roped, 1)

            n_idx = n_att = 0

            def output(m):
                kind, i, h = ATT_UNITS[m]
                dve.wait_ge(pv_out_ps, m + 1)
                r = slice((h % 2) * 64, (h % 2) * 64 + 64)
                dve.tensor_copy(OA[r, (0 if kind == "mla" else 4) + h // 2, i * P:(i + 1) * P], PS[r, 2 * (m % 2) + 1, 2 * P:3 * P])\
                    .then_inc(oa_ready, 1)

            dve.wait_ge(pb_zero, 1)
            dve.wait_ge(roped, 22)
            for n, (kind, i, h) in enumerate(UNITS):
                nk = keys(i)
                cb = rt[:, C_CB + T2 - nk:C_CB + T2]
                if kind == "idx":
                    dve.wait_ge(relu_ready, n_idx + 1)
                    if n_idx > 0:
                        dve.wait_ge(acc_used, n_idx)
                    wih = WI[:, i, h:h + 1]
                    if h == 0:
                        ts(acc[:, 0:nk], RL[:, n_idx % 2, 0:nk], wih, None, ALU.mult).then_inc(acc_used, 1)
                    else:
                        stt(out=acc[:, 0:nk], in0=RL[:, n_idx % 2, 0:nk], scalar=wih, in1=acc[:, 0:nk], op0=ALU.mult, op1=ALU.add)\
                            .then_inc(acc_used, 1)
                    n_idx += 1
                    if h == 7:
                        dve.wait_ge(acc_used, n_idx)
                        link(tt(acc[:, 0:nk], acc[:, 0:nk], cb, ALU.add))
                    continue
                if n_att >= 3:
                    output(n_att - 3)
                scale = (MQK if kind == "mla" else DHD) ** -0.5
                p = n_att % 2
                dve.wait_ge(score_ps, n + 1)
                if n_att >= 2:
                    dve.wait_ge(pT_ps, n_att - 1)
                bias = cb if kind == "mla" else selb[:, 0:nk]
                dve.tensor_tensor_reduce(split(PB[:, p, 0:nk], i), scores(n % 2, i), split(bias, i), 1.0, TAKEN, ALU.add, ALU.max,
                                         mx[:, p, 0:1]).then_inc(score_free[n % 2], 1)
                dve.wait_ge(score_free[n % 2], n // 2 + 1)
                ts(mx[:, p, 1:2], mx[:, p, 0:1], -scale, None, ALU.mult).then_inc(max_ready, 1)
                if kind == "mla":
                    for _ in range(TOPK // 8 // MH):
                        link(dve.max(top8[:], acc[:, 0:nk]))
                        link(dve.match_replace(out=acc[:, 0:nk], in_to_replace=top8[:], in_values=acc[:, 0:nk], imm_value=TAKEN))
                dve.wait_ge(exp_ready, n_att + 1)
                dve.reciprocal(mx[:, p, 3:4], mx[:, p, 2:3]).then_inc(rsum_ready, 1)
                if kind == "mla" and h == MH - 1:
                    link(ts(selb[:, 0:nk], acc[:, 0:nk], TAKEN, 1.0, ALU.is_equal, ALU.subtract))
                    link(stt(out=selb[:, 0:nk], in0=selb[:, 0:nk], scalar=-LOW, in1=cb, op0=ALU.mult, op1=ALU.add))
                n_att += 1
            for m in range(n_att - 3, n_att):
                output(m)
            for i in range(KD):
                low("oa", i, OA[:, i, :], OAh[:, i, :], OAl[:, i, :])
            for i, tile in enumerate(tiles["attn_out"]):
                dve.wait_ge(tile_done, tile.t + 1)
                tt(X2[:, i, NM:T2], X2[:, i, NM:T2], PS[:, 2 * tile.slot, :], ALU.add).then_inc(slot_free[tile.slot], 1)
            for tile in tiles["attn_out"][-2:]:
                read_out(dve, tile)
            scales("ffn", T)
            norm_split("ffn", lambda k: X2[:, k, NM:T2], lambda k: U3h[:, k, :], lambda k: U3l[:, k, :], PV_FFN, T)
            for i, tile in enumerate(tiles["ffn_up"]):
                dve.wait_ge(silu_ready, i + 1)
                dve.wait_ge(tile_done, tile.t + 1)
                tt(HF[:, i, :], SF[:, i % 2, :], PS[:, 2 * tile.slot + 1, :], ALU.mult).then_inc(slot_free[tile.slot], 1)
                if i > 0:
                    low("h", i - 1, HF[:, i - 1, :], HFh[:, i - 1, :], HFl[:, i - 1, :])
            low("h", KF - 1, HF[:, KF - 1, :], HFh[:, KF - 1, :], HFl[:, KF - 1, :])
            for i, tile in enumerate(tiles["ffn_down"]):
                dve.wait_ge(tile_done, tile.t + 1)
                tt(X2[:, i, NM:T2], X2[:, i, NM:T2], PS[:, 2 * tile.slot, :], ALU.add).then_inc(slot_free[tile.slot], 1)
            for tile in tiles["ffn_down"][-2:]:
                read_out(dve, tile)
            norm("fin2", lambda k: X2[:, k, NM:T2], lambda k: FO[:, k, :], PV_FIN2, T)

        def pool_program(pool):
            def vec(name, row, n, src):
                pool.dma_start(pvr[row:row + n, 0:P], src).then_inc(pv_in, 16)

            def col(x):
                return x.rearrange("(k p) -> k p", p=P)

            pool.dma_start(xtok[:], a["x"][0].rearrange("(t p) d -> p t d", p=P)).then_inc(x_in, 16)
            vec("gla_norm", PV_GLA, KD, col(a["gla_norm"][0]))
            vec("b_gate", PV_BG, 4, col(a["gla_b_gate"][0]))
            vec("head_gain", PV_HG, 4, col(a["gla_head_gain"][0]))
            vec("s5_norm", PV_S5, KD, col(a["s5_norm"][0]))
            vec("b_glu", PV_BGLU, KI, col(a["s5_b_glu"][0]))
            vec("d", PV_DS, KI, col(a["s5_d"][0].rearrange("g i -> (g i)")))
            vec("final_norm", PV_FIN, KD, col(a["final_norm"]))
            vec("attn_norm", PV_ATT, KD, col(a["attn_norm_g_2"][0]))
            vec("q_norm", PV_GQ, 2, col(a["mla_q_norm_g_2"][0]))
            vec("kv_norm", PV_GKV, 1, col(a["mla_kv_norm_g_2"][0]))
            vec("ffn_norm", PV_FFN, KD, col(a["ffn_norm_g_2"][0]))
            vec("final_norm_2", PV_FIN2, KD, col(a["final_norm_g_2"]))
            pool.dma_start(glr[:], a["s5_lam_re"][0]).then_inc(par_in, 16)
            pool.dma_start(gli[:], a["s5_lam_im"][0]).then_inc(par_in, 16)
            pool.dma_start(gdt[:, 0:1], a["s5_log_dt"][0].rearrange("(g o) -> g o", o=1)).then_inc(par_in, 16)
            pool.wait_ge(wg_zero, 1)
            pool.dma_start(WG[P - GRANK:P, :], a["gla_w_gate_up"][0]).then_inc(wg_in, 16)
            done = [0]

            def split_weights(upto):
                while done[0] <= min(upto, len(plan.loads) - 1):
                    n = done[0]
                    done[0] += 1
                    at = slice(0, plan.size[n])
                    pool.wait_ge(whi_ready, n + 1)
                    pool.tensor_tensor(ring_lo[:, n % NSLOT, at], ring[:, n % NSLOT, at], ring_hi[:, n % NSLOT, at].bitcast(F32),
                                       ALU.subtract).then_inc(wlo_ready, 1)
                    pool.wait_ge(wlo_ready, n + 1)

            split_weights(tiles["gla_out"][-1].loads[0])
            split_weights(tiles["s5_u"][-1].loads[0])
            pool.wait_ge(pw_ready, 1)

            def factor(i, b):
                return PW[:, i, :, b * BG:(b + 1) * BG].rearrange("p k g -> p g k").unsqueeze(3).broadcast_to([P, BG, TB, SGRP])

            def rows(ap):
                return ap.rearrange("p (g j) -> p g j", g=BG).unsqueeze(2).broadcast_to([P, BG, TB, SGRP])

            def four(ap):
                return ap.rearrange("p g (s j) -> p g s j", s=TB)

            chain = [0]

            def link(ins):
                chain[0] += 1
                ins.then_inc(pool_chain, 1)
                pool.wait_ge(pool_chain, chain[0])

            def read_back(b):
                pool.wait_ge(y_out, 16 * TB * (b + 1))
                if b > 0:
                    pool.wait_ge(yd_ready, b)
                pool.dma_start(YIN, y_dram[b * P:(b + 1) * P, :]).then_inc(y_in, 16)

            pool.wait_ge(tile_done, tiles["s5_u"][-1].t + 1)
            for b in range(NBATCH):
                p, gs = b % 2, slice(b * BG, (b + 1) * BG)
                if b >= 2:
                    pool.wait_ge(y_ps, b - 1)
                pool.wait_ge(cz_sb, b + 1)
                for dst, i, j, op in ((W1[p], 0, 1, ALU.add), (W2[p], 1, 0, ALU.subtract)):
                    link(pool.tensor_tensor(four(dst[:]), factor(i, b), rows(CZ[:, p, 0:P]), ALU.mult))
                    link(pool.tensor_tensor(four(w_tmp[:]), factor(j, b), rows(CZ[:, p, P:2 * P]), ALU.mult))
                    pool.tensor_tensor(dst[:], dst[:], w_tmp[:], op).then_inc(w_ready, 1)
                    if dst is W1[p]:
                        pool.wait_ge(w_ready, 2 * b + 1)
                        pool.tensor_tensor(dk[:, p, :].rearrange("p (g n) -> p g n", g=BG),
                                           r8f8[:, 0, gs].unsqueeze(2).broadcast_to([P, BG, NB]),
                                           con[:, C_NM:C_NM + NB].unsqueeze(1).broadcast_to([P, BG, NB]), ALU.mult)\
                            .then_inc(dk_ready, 1)
                        if b >= 2:
                            read_back(b - 2)
                pool.wait_ge(w_ready, 2 * b + 2)
            read_back(NBATCH - 2)
            read_back(NBATCH - 1)
            split_weights(tiles["s5_out"][-1].loads[0])
            pool.wait_ge(tile_done, tiles["s5_out"][-1].t + 1)
            pool.dma_start(MT[0:NM, :], a["meta_tokens_2"]).then_inc(mt_in, 16)
            pool.dma_start(rt[:], a["rotary_constants"]).then_inc(rt_in, 16)
            split_weights(tiles["uq"][0].loads[0])
            pool.wait_ge(tile_done, tiles["vs"][-1].t + 1)
            pool.wait_ge(roped, ROT_AT["k1"] + 2)
            for h in range(MH):
                pool.tensor_copy(Km[MNOPE:MQK, h, :], KR[MNOPE:MQK, :]).then_inc(kr_copied, 1)
            pool.wait_ge(kr_copied, MH)
            split_weights(tiles["ukvv"][0].loads[0])
            pool.wait_ge(tile_done, tiles["ukvv"][-1].t + 1)
            split_weights(tiles["attn_out"][0].loads[0] + NSLOT - 1)
            pool.memset(PB[:], 0.0).then_inc(pb_zero, 1)
            for n in range(2 * MH * NPAIR):
                nk = keys(n // (2 * MH))
                p = n % 2
                pool.wait_ge(rsum_ready, n + 1)
                pool.tensor_scalar(PB[:, p, 0:nk], PB[:, p, 0:nk], mx[:, p, 3:4], None, ALU.mult).then_inc(p_ready, 1)
            pool.wait_ge(p_ready, 2 * MH * NPAIR)
            split_weights(len(plan.loads) - 1)

        def sp_program(sp):
            def factor_loads(b):
                gs = slice(b * BG, (b + 1) * BG)
                if b == 0:
                    sp.wait_ge(pw_ready, 1)
                if b >= 2:
                    sp.wait_ge(c_ps, b - 1)
                    sp.wait_ge(bt_ready, 2 * (b - 1))
                here = small_in[b % 2]
                for k, name in enumerate(("s5_c_re", "s5_c_im", "s5_c_re")):
                    sp.dma_start(CN[:, b % 2, k * SP_:(k + 1) * SP_], a[name][0, gs].rearrange("g i p -> (g i) p")).then_inc(here, 16)
                for k in range(2):
                    for r, name in enumerate(("s5_b_re", "s5_b_im")):
                        rows = slice(((r + k) % 2) * SP_, ((r + k) % 2 + 1) * SP_)
                        sp.dma_start(BZ[rows, b % 2, k], a[name][0, gs].rearrange("g p j -> p g j")).then_inc(here, 16)

            def u_loads(b):
                if b + 1 < NBATCH:
                    factor_loads(b + 1)
                if b == 0:
                    sp.wait_ge(u_out, 16 * KI)
                if b >= 2:
                    sp.wait_ge(y_ps, b - 1)
                src = u_dram[b * P:(b + 1) * P, :].rearrange("(g j) (s n) -> s j g n", g=BG, s=TB)
                for s in range(TB):
                    sp.dma_start(UB[s * SGRP:(s + 1) * SGRP, b % 2], src[s]).then_inc(ub_in[b % 2], 16)

            for n, parts in enumerate(plan.loads):
                if n >= NSLOT:
                    sp.wait_ge(tile_done, plan.last_use[n - NSLOT] + 1)
                for src, at, shape, *cols in parts:
                    dst = slot_view(n, shape, at)
                    sp.dma_start(dst[:, :, cols[0]] if cols else dst, src).then_inc(landed[n % NSLOT], 16)
                if n == tiles["s5_z"][0].loads[0] - 1:
                    factor_loads(0)
                    for b in range(2):
                        u_loads(b)
                if n == tiles["s5_z"][0].loads[0] + NSLOT - 1:
                    for b in range(2, NBATCH):
                        u_loads(b)
            for tt in range(NPAIR):
                sp.wait_ge(ot_sb, tt + 1)
                sp.dma_start(out[0, tt * P:(tt + 1) * P, :], OT[:, tt, :]).then_inc(out_done, 16)
            sp.wait_ge(out_done, 16 * NPAIR)

        block = ctx.enter_context(nc.Block())

        @block.tensor
        def _(pe):
            pe_program(pe)

        @block.scalar
        def _(act):
            act_program(act)

        @block.vector
        def _(dve):
            dve_program(dve)

        @block.gpsimd
        def _(pool):
            pool_program(pool)

        @block.sync
        def _(sp):
            sp_program(sp)


def kernel(**inputs):
    import concourse.bacc as bacc
    from concourse.bass_utils import run_bass_kernel_spmd

    nc = bacc.Bacc("TRN2", target_bir_lowering=False, num_devices=1)
    arrays = {f"in_{name}": np.ascontiguousarray(value) for name, value in inputs.items()}
    arrays["in_shape_constants"] = shape_constants()
    arrays["in_chunk_constants"] = chunk_constants()
    arrays["in_rotary_constants"] = rotary_constants()
    a = {name[3:]: nc.dram_tensor(name, value.shape, mybir.dt.from_np(value.dtype), kind="ExternalInput").ap()
         for name, value in arrays.items()}
    out = nc.dram_tensor("out_0_dram", (1, T, D), F32, kind="ExternalOutput").ap()
    build(nc, a, out)
    r = run_bass_kernel_spmd(nc, [arrays], core_ids=[0])
    return r.results[0]["out_0_dram"]
```

```python
import math
from contextlib import ExitStack

import numpy as np

import concourse.bass as bass
from concourse import mybir

F32 = mybir.dt.float32
I32 = mybir.dt.int32
U32 = mybir.dt.uint32
F32R = mybir.dt.float32r
ALU = mybir.AluOpType
ACT = mybir.ActivationFunctionType
AX_X = mybir.AxisListType.X

P = 128
T = 512
D = 1024
KD = D // P
EPS = 1e-6
GH, GDK, GDV, GCH, GRANK, GTAU = 4, 128, 512, 64, 16, 16.0
DI = 2 * D
KI = DI // P
G_Q, G_K, G_V, G_Z, G_R = 0, 512, 1024, 3072, 5120
NPAIR = T // P
NCH = T // GCH
SG, SGRP, SP_ = 128, 16, 64
TB = 8
NB = T // TB
NB1 = NB + 1
BG = 8
NBATCH = SG // BG
NM = 16
T2 = T + NM
HALF = T2 // 2
TPAD = 640
MH, MQR, MKR, MNOPE, MROPE, MV = 8, 256, 128, 64, 32, 64
MQK = MNOPE + MROPE
DH, DHD = 8, 64
TOPK = 128
FF = 2816
KF = FF // P
A_CQ, A_CKV, A_KR, A_QS, A_KS, A_VS, A_QI, A_KI, A_WI, A_END = 0, 256, 384, 416, 928, 1440, 1952, 2464, 2528, 2536
LOW = -1e30
TAKEN = -3e38
ROUND = 12582912.0
A_MIN = -9.0

SLOT = 2048
NSLOT = 3

C_ID, C_ONE, C_SM, C_NM, C_NI, C_SG, C_NSG, C_EPS, C_HPI, C_N = 0, 128, 256, 768, 833, 898, 899, 900, 901, 902
C_GM, C_RST = 0, 512
R_C, R_S, R_MC, R_MS, R_P, R_MP, C_CB, R_N = 0, 528, 1056, 1584, 2112, 2240, 2368, 2896
PV_GLA, PV_BG, PV_HG, PV_S5, PV_BGLU, PV_DS, PV_FIN, PV_ATT, PV_GQ, PV_GKV, PV_FFN, PV_FIN2, PV_N = \
    0, 8, 12, 16, 24, 40, 56, 64, 72, 74, 75, 83, 91


def shape_constants():
    c = np.zeros((P, C_N), np.float32)
    r = np.arange(P)
    c[:, C_ID:C_ID + P] = np.eye(P)
    c[:, C_ONE:C_ONE + P] = 1.0
    m = (r[:, None] // SGRP) <= (r[None, :] // SGRP)
    c[:, C_SM:C_SM + T] = np.tile(m, (1, 4))
    c[:, C_NM:C_NM + NB1] = (np.arange(NB1) != 0)[None, :]
    c[:, C_NI:C_NI + NB1] = np.arange(-1, NB)[None, :]
    c[:, C_SG] = np.where(r < SP_, 1.0, -1.0)
    c[:, C_NSG] = -c[:, C_SG]
    c[:, C_EPS] = EPS
    c[:, C_HPI] = math.pi / 2
    return c


def chunk_constants():
    c = np.zeros((P, 2 * T), np.float32)
    r = np.arange(P)
    m = (r[:, None] <= r[None, :]) & (r[:, None] // GCH == r[None, :] // GCH)
    c[:, C_GM:C_GM + T] = np.tile(m, (1, NPAIR))
    c[:, C_RST:C_RST + T] = (np.arange(T) % GCH != 0)[None, :]
    return c


def rotary_constants():
    c = np.zeros((P, R_N), np.float32)
    r = np.arange(P)
    c[:, C_CB + T2 - P:C_CB + T2] = np.where(r[None, :] <= r[:, None], 0.0, LOW)
    pos = np.arange(T2, dtype=np.float32)
    for width, rows, oc, os, op in ((DHD, range(P), R_C, R_S, R_P), (MROPE, range(MNOPE, MQK), R_MC, R_MS, R_MP)):
        half = width // 2
        inv = np.power(np.float32(10000.0), -np.arange(half, dtype=np.float32) / np.float32(half)).astype(np.float32)
        for r in rows:
            d = r % width if width == DHD else r - MNOPE
            ang = pos * inv[d % half]
            c[r, oc:oc + T2] = np.cos(ang)
            c[r, os:os + T2] = np.sin(ang) * (-1.0 if d < half else 1.0)
            c[r - d + (d + half) % width, op + r] = 1.0
    return c


class Tile:

    def __init__(self, t, loads):
        self.t, self.loads, self.slot = t, loads, t % 2


class Plan:

    def __init__(self):
        self.loads, self.tiles, self.last_use, self.value = [], {}, [], []
        self.n, self.count = 0, [0] * NSLOT
        self.size = []

    def load(self, *parts):
        n = len(self.loads)
        self.size.append(max(at + int(np.prod(shape)) for _, at, shape, *_ in parts))
        self.loads.append(parts)
        self.count[n % NSLOT] += 16 * len(parts)
        self.value.append(self.count[n % NSLOT])
        self.last_use.append(None)
        return n

    def tile(self, stage, *loads):
        t = Tile(self.n, loads)
        self.n += 1
        self.tiles.setdefault(stage, []).append(t)
        for n in loads:
            self.last_use[n] = t.t
        return t


def build(nc, a, out):
    w1 = a["gla_w_in"][0].rearrange("(k p) m -> p k m", p=P)
    wo1 = a["gla_w_out"][0].rearrange("(k p) m -> p k m", p=P)
    w2 = a["s5_w_in"][0].rearrange("(k p) m -> p k m", p=P)
    wg2 = a["s5_w_glu"][0].rearrange("(k p) m -> p k m", p=P)
    wo2 = a["s5_w_out"][0].rearrange("(k p) m -> p k m", p=P)
    w3 = a["w_in_2"][0].rearrange("(k p) m -> p k m", p=P)
    wuq = a["w_uq_2"][0].rearrange("(k p) m -> p k m", p=P)
    wukv = a["w_ukv_2"][0]
    wo3 = a["w_o_2"][0].rearrange("(k p) m -> p k m", p=P)
    wga = a["w_gate_2"][0].rearrange("(k p) m -> p k m", p=P)
    wup = a["w_up_2"][0].rearrange("(k p) m -> p k m", p=P)
    wdn = a["w_down_2"][0].rearrange("(k p) m -> p k m", p=P)

    plan = Plan()

    def pairs(stage, w, c0, n):
        for m in range(0, n, 2):
            ld = plan.load((w[:, :, c0 + m * P:c0 + (m + 2) * P], 0, (KD, 2 * P)))
            plan.tile(stage, ld)
            plan.tile(stage, ld)

    def singles(stage, w, n):
        for m in range(n):
            plan.tile(stage, plan.load((w[:, :, m * P:(m + 1) * P], 0, (KI, P))))

    def token_major(stage, w, c0, n, tiles):
        for m in range(n):
            lds = [plan.load((w[:, 4 * j:4 * j + 4, c0 + m * T:c0 + (m + 1) * T], 0, (4, T))) for j in range(2)]
            for _ in range(tiles):
                plan.tile(stage, *lds)

    pairs("gla_q", w1, G_Q, 4)
    pairs("gla_k", w1, G_K, 4)
    plan.tile("gla_r", plan.load((w1[:, :, G_R + GRANK - P:G_R + GRANK], 0, (KD, P))))
    token_major("gla_v", w1, G_V, 4, 2)
    pairs("gla_z", w1, G_Z, KI)
    singles("gla_out", wo1, KD)
    pairs("s5_u", w2, 0, KI)
    pairs("s5_z", w2, DI, KI)
    singles("s5_glu", wg2, KI)
    singles("s5_out", wo2, KD)
    pairs("cq", w3, A_CQ, 2)
    ld = plan.load((w3[:, :, A_CKV:A_QS], 0, (KD, A_QS - A_CKV)))
    plan.tile("ckv", ld)
    plan.tile("kr", ld)
    pairs("qs", w3, A_QS, 4)
    pairs("ks", w3, A_KS, 4)
    pairs("qi", w3, A_QI, 4)
    ld = plan.load((w3[:, :, A_KI:A_WI], 0, (KD, P), slice(0, 64)), (w3[:, :, A_KI:A_WI], 0, (KD, P), slice(64, P)),
                   (w3[:, :, A_WI:A_END], KD * P, (KD, 8)))
    plan.tile("ki", ld)
    plan.tile("wi", ld)
    token_major("vs", w3, A_VS, 1, 3)
    ld = plan.load((wuq, 0, (2, MH * MQK)))
    for _ in range(MH):
        plan.tile("uq", ld)
    ld = plan.load((wukv, 0, (MH * P,)))
    for _ in range(MH):
        plan.tile("ukn", ld)
    for _ in range(3):
        plan.tile("ukvv", ld)
    pairs("attn_out", wo3, 0, KD)
    for m in range(KF):
        ld = plan.load((wga[:, :, m * P:(m + 1) * P], 0, (KD, P)), (wup[:, :, m * P:(m + 1) * P], KD * P, (KD, P)))
        plan.tile("ffn_up", ld)
    for m in range(KD):
        plan.tile("ffn_down", *[plan.load((wdn[:, 11 * j:11 * j + 11, m * P:(m + 1) * P], 0, (11, P))) for j in range(2)])
    tiles = plan.tiles
    HALVES = [t.loads[0] for stage in ("gla_v", "vs", "ffn_down") for t in tiles[stage] if plan.last_use[t.loads[0]] == t.t]

    NORMS, norm_at = {}, [0, 0]
    for name, k in (("gla", KD), *[(f"head{h}", 4) for h in range(GH)], ("s5", KD), ("fin", KD), ("attn", KD),
                    ("cq", 2), ("ckv", 1), ("ffn", KD), ("fin2", KD)):
        NORMS[name] = (norm_at[0], norm_at[1], k)
        norm_at[0] += k
        norm_at[1] += 1
    SPLITS, VALS, split_at, val_at = {}, {}, 0, 0
    for name, k, counted in (("gla", KD, 1), ("gla2", KD, 1), ("o", KI, 1), ("s5", KD, 1), ("s5z", KD, 0), ("g", KI, 0), ("z", KI, 1),
                             ("attn", KD, 1), ("cq", 2, 1), ("ckv", 1, 1), ("oa", KD, 0), ("ffn", KD, 1), ("h", KF, 0)):
        SPLITS[name] = (split_at, k)
        split_at += k
        if counted:
            VALS[name] = val_at
            val_at += k
    PLAIN, plain_at = {}, 0
    for name in NORMS:
        if name not in SPLITS:
            PLAIN[name] = plain_at
            plain_at += NORMS[name][2]
    BEFORE = dict(zip(list(NORMS)[1:], list(NORMS)))

    with ExitStack() as ctx:
        base = nc.sbuf_base
        base = base() if callable(base) else base
        base = (base + 63) // 64 * 64
        top = [base]
        ends = []

        def place(name, shape, at=None, dt=F32):
            size = int(np.prod(shape[1:])) * 4
            off = (top[0] if at is None else at) + 31 & -32
            t = nc.alloc_sbuf_tensor_at(name, list(shape), dt, offset=off)
            if at is None:
                top[0] = off + size
            ends.append(off + size)
            return t, off + size

        def keep(name, shape, dt=F32):
            return place(name, shape, None, dt)[0]

        ring_off = top[0] + 31 & -32
        ring = keep("ring", [P, NSLOT, SLOT])
        ring_lo, _ = place("ring_lo", [P, NSLOT, SLOT], ring_off, F32R)
        hi_off = top[0] + 31 & -32
        ring_hi = keep("ring_hi", [P, NSLOT, SLOT], F32R)
        con = keep("con", [P, C_N])
        pv = keep("pv", [P, PV_N])
        pvr_off = top[0] + 31 & -32
        pvr = keep("pvr", [P, 2 * P])
        sq = keep("sq", [P, 2, T2])
        rsc = keep("rsc", [P, 8])
        rs1 = keep("rs1", [P, T])
        ssq = keep("ssq", [P, T2])
        sg2pi = keep("sg2pi", [P, 1])
        warm = keep("warm", [P, 1])
        xt_off = top[0] + 31 & -32
        XT = keep("XT", [P, KD, T])
        lo = top[0] + 31 & -32
        K1 = 1024

        HTh, _ = place("HTh", [P, KD, T], lo, F32R)
        HTl, _ = place("HTl", [P, KD, T], lo + 16 * K1, F32R)
        QG, _ = place("QG", [P, GH, T], lo + 32 * K1)
        KG, _ = place("KG", [P, GH, T], lo + 40 * K1)
        LA, _ = place("LA", [P, GH, T], lo + 48 * K1)
        ATT = LA
        KE, _ = place("KE", [P, NPAIR, GH * GDK], lo + 56 * K1)
        V, _ = place("V", [P, NPAIR, DI], lo + 64 * K1)
        xtok, _ = place("xtok", [P, NPAIR, D], lo + 64 * K1)
        o = lo + 96 * K1
        WG, o = place("WG", [P, T], o)
        R16, o = place("R16", [P, T], o)
        la_e, o = place("la_e", [P, T], o)
        ex_p, o = place("ex_p", [P, T], o)
        ex_n, o = place("ex_n", [P, T], o)
        kend, o = place("kend", [P, GH, T], o)
        rst, o = place("rst", [P, T], o)
        S, _ = place("S", [P, 3, GH * GDV], lo)
        O, _ = place("O", [P, KI, T], lo + 96 * K1)
        Ol, _ = place("Ol", [P, KI, T], lo + 96 * K1, F32R)
        Oh, _ = place("Oh", [P, KI, T], lo + 64 * K1, F32R)
        HT2h, _ = place("HT2h", [P, KD, T], lo + 32 * K1, F32R)
        HT2l, _ = place("HT2l", [P, KD, T], lo + 48 * K1, F32R)
        SZ, _ = place("SZ", [P, 2, T], lo)
        gmask, o = place("gmask", [P, T], lo + 128 * K1)
        dec, _ = place("dec", [P, GH, NCH], o)

        o = lo + 116 * K1
        glr, o = place("glr", [P, SP_], o)
        gli, o = place("gli", [P, SP_], o)
        gdt, o = place("gdt", [P, 8], o)
        gt, o = place("gt", [P, 16, SP_], o)
        gi, o = place("gi", [P, SP_], o, I32)
        TPg, o = place("TPg", [P, 8, P], o)
        assert o <= lo + 128 * K1
        PT, o = place("PT", [P, 8, P], lo + 26 * K1)
        ctmp, o = place("ctmp", [P, 2, P], o)
        r8f8, _ = place("r8f8", [P, 2, P], pvr_off)
        PW, o = place("PW", [P, 4, TB, SG], lo + 32 * K1)
        CN, o = place("CN", [P, 2, 3 * SP_], o)
        BZ, o = place("BZ", [P, 2, 2, BG, SGRP], o)
        CZ, o = place("CZ", [P, 2, 2 * P], o)
        dk, o = place("dk", [P, 2, BG, NB1], o)
        UB, o = place("UB", [P, 2, BG, NB], o)
        assert o <= lo + 64 * K1
        HT, _ = place("HT", [P, KD, T], lo)
        U, _ = place("U", [P, KI, T], lo + 64 * K1)
        HT5h, _ = place("HT5h", [P, KD, T], lo + 96 * K1, F32R)
        HT5l, _ = place("HT5l", [P, KD, T], lo + 112 * K1, F32R)

        def factors(name):
            sets = []
            for p_, off in ((0, lo + 16 * K1), (1, lo + 96 * K1)):
                sets.append(place(f"{name}{p_}", [P, BG, TB * SGRP], off + 4 * K1 * ("KM", "Bn", "W1", "W2").index(name))[0])
            return sets

        KM, Bn, W1, W2 = factors("KM"), factors("Bn"), factors("W1"), factors("W2")
        o = lo + 112 * K1
        w_tmp, o = place("w_tmp", [P, BG, TB * SGRP], o)
        b_tmp, o = place("b_tmp", [P, BG, TB * SGRP], o)
        WB, o = place("WB", [P, BG, 3 * SP_], o)
        M12, _ = place("M12", [P, 2, BG, NB1], o)
        free = [n for n in range(NSLOT) if n != tiles["s5_z"][0].loads[0] % NSLOT]
        rot_c, _ = place("rot_c", [P, 2, BG, NB1], hi_off + free[0] * SLOT * 4)
        rot_s, _ = place("rot_s", [P, 2, BG, NB1], hi_off + free[1] * SLOT * 4)
        YB, YIN = sq[:, 0, 0:T], sq[:, 1, 0:T]
        HT6l, _ = place("HT6l", [P, KD, T], lo, F32R)
        HT6h, _ = place("HT6h", [P, KD, T], lo + 16 * K1, F32R)
        Z, _ = place("Z", [P, KI, T], lo + 32 * K1)
        Zl, _ = place("Zl", [P, KI, T], lo + 32 * K1, F32R)
        Ul, _ = place("Ul", [P, KI, T], lo + 64 * K1, F32R)
        Uh, _ = place("Uh", [P, KI, T], lo + 96 * K1, F32R)
        Zh, _ = place("Zh", [P, KI, T], lo, F32R)

        X2, o = place("X2", [P, KD, T2], lo)
        u2_lo = o
        U2h, o = place("U2h", [P, KD, TPAD], o, F32R)
        U2l, att_lo = place("U2l", [P, KD, TPAD], o, F32R)
        o = u2_lo
        Km, o = place("Km", [P, MH, T2], o)
        Qm, o = place("Qm", [P, MH, T], o)
        PB, o = place("PB", [P, 3, TPAD], o)
        assert o <= att_lo
        OAh, _ = place("OAh", [P, KD, T], u2_lo, F32R)
        o = att_lo
        Vm, o = place("Vm", [P, 5, MH * MV], o)
        MT, _ = place("MT", [P, D], att_lo)
        QS, o = place("QS", [P, 4, T], o)
        KS, o = place("KS", [P, 4, T2], o)
        VS, o = place("VS", [P, 5, DH * DHD], o)
        KI_, o = place("KI_", [P, T2], o)
        WI, o = place("WI", [P, NPAIR, 8], o)
        rt, oa_lo = place("rt", [P, R_N], o)
        CQ, o = place("CQ", [P, 2, T], oa_lo)
        CQh, o = place("CQh", [P, 2, T], o, F32R)
        CQl, o = place("CQl", [P, 2, T], o, F32R)
        CKh, o = place("CKh", [P, TPAD], o, F32R)
        CKl, o = place("CKl", [P, TPAD], o, F32R)
        KR, o = place("KR", [P, T2], o)
        ro, o = place("ro", [P, 2, T2], o)
        OA, o = place("OA", [P, KD, T], oa_lo)
        OAl, _ = place("OAl", [P, KD, T], oa_lo, F32R)
        PT2, o = place("PT2", [P, 2, TPAD], o)
        o = xt_off
        QI, o = place("QI", [P, 4, T], o)
        CK, _ = place("CK", [P, T2], o)
        RL, o = place("RL", [P, 2, T2], o)
        acc, o = place("acc", [P, T2], o)
        top8, o = place("top8", [P, 8], o)
        mx, o = place("mx", [P, 3, 8], o)
        assert o <= xt_off + 16 * K1
        selb = ssq
        U3h, _ = place("U3h", [P, KD, T], xt_off, F32R)
        U3l, o = place("U3l", [P, KD, T], u2_lo, F32R)
        HF, _ = place("HF", [P, KF, T], o)
        HFl, o = place("HFl", [P, KF, T], o, F32R)
        HFh, o = place("HFh", [P, KF, T], o, F32R)
        SF, o = place("SF", [P, 2, T], o)
        FO, o = place("FO", [P, KD, T], u2_lo)
        OT, o = place("OT", [P, NPAIR, D], o)

        PS = ctx.enter_context(nc.psum_tensor("PS", [P, 4, 512], F32))
        PA = ctx.enter_context(nc.psum_tensor("PA", [P, 4, 512], F32))

        def sem(name):
            return ctx.enter_context(nc.semaphore(name))

        landed = [sem(f"landed{i}") for i in range(NSLOT)]
        tile_done = sem("tile_done")
        slot_free = [sem("slot_free0"), sem("slot_free1")]
        con_in, pv_in, x_in, wg_in, out_done = sem("con_in"), sem("pv_in"), sem("x_in"), sem("wg_in"), sem("out_done")
        pv_ps, pv_sb = sem("pv_ps"), sem("pv_sb")
        rs_ps = sem("rs_ps")
        squares_summed, half_used = sem("squares_summed"), sem("half_used")
        whi_ready, wlo_ready = sem("whi_ready"), sem("wlo_ready")
        val_ready, xhi_ready, xlo_ready = sem("val_ready"), sem("xhi_ready"), sem("xlo_ready")
        xT_ps, xT_sb = sem("xT_ps"), sem("xT_sb")
        sq_ready, sq_used, std_ready, rstd_ready, normed = (
            sem("sq_ready"), sem("sq_used"), sem("std_ready"), sem("rstd_ready"), sem("normed"))
        act_chain, dve_chain, pool_chain = sem("act_chain"), sem("dve_chain"), sem("pool_chain")
        wg_zero, gate_ps, gate_ev, gl_ready, la_ready, ex_ready, de_ready, kx_ready, qkg_ready, ke_ready = (
            sem("wg_zero"), sem("gate_ps"), sem("gate_ev"), sem("gl_ready"), sem("la_ready"), sem("ex_ready"),
            sem("de_ready"), sem("kx_ready"), sem("qkg_ready"), sem("ke_ready"))
        keT_ps, keT_sb, att_ps, att_sb, kv_ps, S_ready, o_ps, o_sb = (
            sem("keT_ps"), sem("keT_sb"), sem("att_ps"), sem("att_sb"), sem("kv_ps"), sem("S_ready"), sem("o_ps"), sem("o_sb"))
        oz_ready = sem("oz_ready")
        par_in, gx_ready, tp_ready, pt_ps, pt_sb, pw_ready, sin_ready = (
            sem("par_in"), sem("gx_ready"), sem("tp_ready"), sem("pt_ps"), sem("pt_sb"), sem("pw_ready"), sem("sin_ready"))
        u_out, ub_in, y_out, y_in = sem("u_out"), [sem("ub_in_even"), sem("ub_in_odd")], sem("y_out"), sem("y_in")
        small_in = [sem("small_in0"), sem("small_in1")]
        c_ps, cz_sb, bf_ready, b_ps, wb_sb, w_ready, k_ps, km_ready, v_ps, m_ready, y_ps, y_sb = (
            sem("c_ps"), sem("cz_sb"), sem("bf_ready"), sem("b_ps"), sem("wb_sb"), sem("w_ready"), sem("k_ps"),
            sem("km_ready"), sem("v_ps"), sem("m_ready"), sem("y_ps"), sem("y_sb"))
        frac_ready, rot_ready, dk_ready, rot_used, yd_ready, gelu_done = (
            sem("frac_ready"), sem("rot_ready"), sem("dk_ready"), sem("rot_used"), sem("yd_ready"), sem("gelu_done"))

        ident = con[:, C_ID:C_ID + P]
        ones = con[:, C_ONE:C_ONE + P]

        def read_out(eng, tile):
            eng.wait_ge(slot_free[tile.slot], tile.t // 2 + 1)

        mt_in, mt_ps, mt_sb, rt_in, pad_zero = sem("mt_in"), sem("mt_ps"), sem("mt_sb"), sem("rt_in"), sem("pad_zero")
        ro_ps, ro_read, roped, kr_copied, pb_zero = sem("ro_ps"), sem("ro_read"), sem("roped"), sem("kr_copied"), sem("pb_zero")
        score_ps, score_free, relu_ready, acc_used, max_ready, exp_ready, rsum_ready, p_ready = (
            sem("score_ps"), [sem("score_free0"), sem("score_free1")], sem("relu_ready"), sem("acc_used"), sem("max_ready"),
            sem("exp_ready"), sem("rsum_ready"), sem("p_ready"))
        pT_ps, pT_sb, pv_out_ps, oa_ready = sem("pT_ps"), sem("pT_sb"), sem("pv_out_ps"), sem("oa_ready")
        silu_ready, ot_ps, ot_sb = sem("silu_ready"), sem("ot_ps"), sem("ot_sb")

        def keys(i):
            return NM + (i + 1) * P

        def scores(pair, i):
            n = keys(i)
            return PA[:, 2 * pair:2 * pair + 1, 0:n] if n <= 512 else PA[:, 2 * pair:2 * pair + 2, 0:n // 2]

        def split(ap, i):
            n = keys(i)
            return ap.rearrange("p (h n) -> p h n", h=1 if n <= 512 else 2)

        def rotations(stage):
            if stage == "qs":
                return [(QS[:, j, :], 0, P, NM, R_C, tiles["qs"][j]) for j in range(4)]
            if stage == "ks":
                return [(KS[:, j, :], 0, P, 0, R_C, tiles["ks"][j]) for j in range(4)]
            if stage == "qi":
                return [(QI[:, j, :], 0, P, NM, R_C, tiles["qi"][j]) for j in range(4)]
            if stage == "k1":
                return [(KI_[:], 0, P, 0, R_C, tiles["ki"][0]), (KR[:], MNOPE, MQK, 0, R_MC, tiles["kr"][0])]
            return [(Qm[:, h, :], MNOPE, MQK, NM, R_MC, tiles["uq"][h]) for h in range(MH)]

        ROT_STAGES = ("qs", "ks", "qi", "k1", "qm")
        ROT_AT = {"qs": 0, "ks": 4, "qi": 8, "k1": 12, "qm": 14}

        UNITS = [("idx", 0, h) for h in range(8)]
        for i in range(NPAIR):
            UNITS += [("mla", i, h) for h in range(MH)]
            for h in range(0, DH, 2):
                UNITS += [("dsa", i, h), ("dsa", i, h + 1)]
                if i + 1 < NPAIR and h < DH // 2:
                    UNITS += [("idx", i + 1, 2 * h + j) for j in range(4)]

        def selection_rounds(kind, i, h):
            if kind == "mla":
                return i, 2 if i == 0 or h < 2 else 1
            return i + 1, {4: 1, 5: 1, 6: 2, 7: 2}.get(h, 0) if i + 1 < NPAIR else 0

        for i in range(NPAIR):
            assert TOPK // 8 == sum(selection_rounds(*u)[1] for u in UNITS if u[0] != "idx" and selection_rounds(*u)[0] == i)
        ATT_UNITS = [u for u in UNITS if u[0] != "idx"]

        u_dram = nc.dram_tensor("u_by_block", (DI, T), F32, kind="Internal").ap()
        y_dram = nc.dram_tensor("y_by_block", (DI, T), F32, kind="Internal").ap()
        TWO_PI = 6.283185

        def by_block(ap):
            return ap.rearrange("p (n s) -> p s n", s=TB)

        def sn(ap):
            return ap.rearrange("p (s n) -> p s n", s=TB)

        def slot_view(n, shape, at=0, of=None):
            size = int(np.prod(shape))
            v = (ring if of is None else of)[:, n % NSLOT, at:at + size]
            return v.rearrange("p (k m) -> p k m", k=shape[0]) if len(shape) == 2 else v

        def parts_view(n, shape, at=0):
            return slot_view(n, shape, at, ring_hi), slot_view(n, shape, at, ring_lo)

        def both(pair, *index):
            return tuple(x[index] for x in pair)

        WIDE = [name for name in NORMS if NORMS[name][2] >= 4]

        def summed(name, i):
            return sum(NORMS[other][2] - 2 for other in WIDE[:WIDE.index(name)]) + max(i, 1)

        def token_tiles(width):
            return [(j, min(P, width - j * P)) for j in range((width + P - 1) // P)]

        def token_blocks(width):
            full, rest = width // P, width % P
            return [(slice(0, P), slice(0, full))] + ([(slice(0, rest), slice(full, full + 1))] if rest else [])

        def scale_rows(width):
            return PA[:, 0:2, :].rearrange("p a b -> p (a b)")[:, 0:width]

        HEAD_WITH = {0: 0, 2: 1, 6: 2, 10: 3}

        def norm_applied(eng, name):
            if name in SPLITS:
                eng.wait_ge(xlo_ready, sum(SPLITS[name]))
            else:
                eng.wait_ge(normed, PLAIN[name] + NORMS[name][2])

        KV_ORDER = [(c, h) for tt in range(NPAIR) for h in range(GH) for c in (2 * tt, 2 * tt + 1) if c < NCH - 1]
        KV_COUNT = {ch: n + 1 for n, ch in enumerate(KV_ORDER)}

        def halves(ap, width):
            return ap.rearrange("p (h n) -> p h n", h=2)

        def pe_program(pe):
            def weights_in(n):
                pe.wait_ge(wlo_ready, n + 1)

            def open_tile(tile):
                weights_in(tile.loads[0])
                if tile.t >= 2:
                    pe.wait_ge(slot_free[tile.slot], tile.t // 2)

            def product(dst, w, x, start, stop):
                pe.matmul(dst, w[0], x[0], start=start, stop=False)
                pe.matmul(dst, w[0], x[1], start=False, stop=False)
                return pe.matmul(dst, w[1], x[0], start=False, stop=stop)

            def feature_tile(tile, weights, rhs, nk, width=T, rows=P, split=None):
                open_tile(tile)
                for k in range(nk):
                    if split:
                        pe.wait_ge(xlo_ready, SPLITS[split][0] + k + 1)
                    w, x = weights(k), rhs(k)
                    if width == T:
                        m = product(PS[0:rows, 2 * tile.slot, 0:T], w, x, k == 0, k == nk - 1)
                    else:
                        for h in range(2):
                            m = product(PS[0:rows, 2 * tile.slot + h, 0:HALF], w, tuple(y[:, h * HALF:(h + 1) * HALF] for y in x),
                                        k == 0, k == nk - 1)
                m.then_inc(tile_done, 1)

            def pair_stage(stage, rhs, width=T, split=None, then=None):
                first = tiles[stage][:2] if split else []
                for tile in first:
                    open_tile(tile)
                for k in range(KD if split else 0):
                    pe.wait_ge(xlo_ready, SPLITS[split][0] + k + 1)
                    for i, tile in enumerate(first):
                        w = parts_view(tile.loads[0], (KD, 2 * P))
                        m = product(PS[:, 2 * tile.slot, 0:T], both(w, slice(None), k, slice(i * P, (i + 1) * P)), rhs(k),
                                    k == 0, k == KD - 1)
                        if k == KD - 1:
                            m.then_inc(tile_done, 1)
                for i, tile in enumerate(tiles[stage]):
                    if i >= len(first):
                        w = parts_view(tile.loads[0], (KD, 2 * P))
                        feature_tile(tile, lambda k: both(w, slice(None), k, slice((i % 2) * P, (i % 2 + 1) * P)), rhs, KD, width)
                    if then and (i > 0 or not first):
                        for done_i in (0, 1) if first and i == 1 else (i,):
                            then(done_i)

            def single_stage(stage, rhs, split=None):
                for i, tile in enumerate(tiles[stage]):
                    w = parts_view(tile.loads[0], (KI, P))
                    feature_tile(tile, lambda k: both(w, slice(None), k), rhs, KI, split=split if i == 0 else None)

            def half_done(tile, m):
                if plan.last_use[tile.loads[0]] == tile.t:
                    m.then_inc(half_used, 1)

            def token_stage(stage, x, ntiles):
                for i, tile in enumerate(tiles[stage]):
                    first = 2 * (i % ((ntiles + 1) // 2))
                    count = min(2, ntiles - first)
                    for j in range(2):
                        open_tile(tile) if j == 0 else weights_in(tile.loads[1])
                        w = parts_view(tile.loads[j], (4, T))
                        for b in range(count):
                            ts_ = slice((first + b) * P, (first + b + 1) * P)
                            for k in range(4):
                                m = product(PS[:, 2 * tile.slot + b, :], both(x, slice(None), 4 * j + k, ts_), both(w, slice(None), k),
                                            j == 0 and k == 0, j == 1 and k == 3)
                        if j == 0:
                            half_done(tile, m)
                    m.then_inc(tile_done, 1)

            def norm(name, width):
                s0, n0, k = NORMS[name]
                if name in BEFORE:
                    norm_applied(pe, BEFORE[name])
                parts = [sq[:, (s0 + i) % 2, :] for i in range(k)]
                if name in WIDE:
                    pe.wait_ge(squares_summed, summed(name, k - 2))
                    parts = [ssq, parts[-1]]
                pe.wait_ge(sq_ready, s0 + k)
                for j, w in token_tiles(width):
                    for i, part in enumerate(parts):
                        m = pe.matmul(PA[0:w, 3, j:j + 1], part[:, j * P:j * P + w], con[:, C_ONE:C_ONE + 1],
                                      start=i == 0, stop=i == len(parts) - 1)
                m.then_inc(sq_used, k)
                pe.wait_ge(rstd_ready, n0 + 1)
                for j, w in token_tiles(width):
                    m = pe.matmul(scale_rows(width)[:, j * P:j * P + w], rsc[0:w, j:j + 1].broadcast_to([w, P]),
                                  con[0:w, C_ID:C_ID + w], start=True, stop=True)
                m.then_inc(rs_ps, 1)

            pe.wait_ge(con_in, 48)
            pe.wait_ge(x_in, 16 * NPAIR)
            for k in range(KD):
                if k >= 4:
                    pe.wait_ge(xT_sb, k - 3)
                for tt in range(NPAIR):
                    m = pe.transpose(PA[:, k % 4, tt * P:(tt + 1) * P], xtok[:, tt, k * P:(k + 1) * P], ident)
                m.then_inc(xT_ps, 1)
            pe.wait_ge(pv_in, 16 * 12)
            pe.transpose(PS[:, 0, 0:PV_N], pvr[0:PV_N, 0:P], con[0:PV_N, C_ID:C_ID + PV_N]).then_inc(pv_ps, 1)
            pe.wait_ge(xT_sb, KD)
            norm("gla", T)
            HTp = (HTh, HTl)
            pair_stage("gla_q", lambda k: both(HTp, slice(None), k), split="gla")
            pair_stage("gla_k", lambda k: both(HTp, slice(None), k))
            w = parts_view(tiles["gla_r"][0].loads[0], (KD, P))
            feature_tile(tiles["gla_r"][0], lambda k: both(w, slice(None), k), lambda k: both(HTp, slice(None), k), KD)
            pe.wait_ge(wg_in, 16)
            read_out(pe, tiles["gla_r"][0])
            for h in range(GH):
                pe.matmul(PA[:, h, :], WG[:, h * P:(h + 1) * P], R16[:], start=True, stop=True).then_inc(gate_ps, 1)
            token_stage("gla_v", HTp, NPAIR)
            for h in range(GH):
                pe.wait_ge(gate_ev, h + 1)
                pe.wait_ge(ke_ready, h + 1)
                for tt in range(NPAIR):
                    m = pe.transpose(PA[:, h, tt * P:(tt + 1) * P], kend[:, h, tt * P:(tt + 1) * P], ident)
                m.then_inc(keT_ps, 1)
            for h in range(GH):
                pe.wait_ge(qkg_ready, h + 1)
                pe.wait_ge(keT_sb, h + 1)
                for tt in range(NPAIR):
                    s = slice(tt * P, (tt + 1) * P)
                    m = pe.matmul(PA[:, h, s], KG[:, h, s], QG[:, h, s], start=True, stop=True)
                m.then_inc(att_ps, 1)
            read_out(pe, tiles["gla_v"][-1])
            read_out(pe, tiles["gla_v"][-2])
            pe.wait_ge(att_sb, GH)
            pe.wait_ge(tp_ready, 1)
            for i in range(8):
                m = pe.transpose(PA[:, 2 + i // 4, (i % 4) * P:(i % 4 + 1) * P], TPg[:, i, :], ident)
            m.then_inc(pt_ps, 1)

            def additions_of(tt, h):
                for c in (2 * tt, 2 * tt + 1):
                    if c < NCH - 1:
                        n = KV_COUNT[c, h]
                        if n > 2:
                            pe.wait_ge(S_ready, n - 2)
                        r = slice((c % 2) * GCH, (c % 2) * GCH + GCH)
                        pe.matmul(PA[:, (n - 1) % 2, :], KE[r, tt, h * P:(h + 1) * P], V[r, tt, h * GDV:(h + 1) * GDV],
                                  start=True, stop=True).then_inc(kv_ps, 1)

            no = 0
            additions_of(0, 0)
            for tt in range(NPAIR):
                for h in range(GH):
                    if h + 1 < GH:
                        additions_of(tt, h + 1)
                    elif tt + 1 < NPAIR:
                        additions_of(tt + 1, 0)
                    if no >= 2:
                        pe.wait_ge(o_sb, no - 1)
                    if no == 0:
                        pe.wait_ge(pt_sb, 1)
                    pe.wait_ge(S_ready, KV_COUNT[2 * tt, h])
                    for e in range(4):
                        dst = PA[:, 2 + no % 2, e * P:(e + 1) * P]
                        es = slice(h * GDV + e * P, h * GDV + (e + 1) * P)
                        m = pe.matmul(dst, V[:, tt, es], ATT[:, h, tt * P:(tt + 1) * P], start=True, stop=False)
                        for c in range(max(2 * tt, 1), 2 * tt + 2):
                            r = slice((c % 2) * GCH, (c % 2) * GCH + GCH)
                            m = pe.matmul(dst[:, r], S[:, (c - 1) % 3, es], QG[:, h, c * GCH:(c + 1) * GCH],
                                          start=False, stop=c == 2 * tt + 1)
                    m.then_inc(o_ps, 1)
                    no += 1
            pair_stage("gla_z", lambda k: both((HT2h, HT2l), slice(None), k), split="gla2",
                       then=lambda i: norm(f"head{HEAD_WITH[i]}", T) if i in HEAD_WITH else None)
            single_stage("gla_out", lambda k: both((Oh, Ol), slice(None), k), split="o")
            norm("s5", T)
            pair_stage("s5_u", lambda k: both((HT5h, HT5l), slice(None), k), split="s5")
            for tile in tiles["s5_u"][-2:]:
                read_out(pe, tile)

            def c_to_columns(b):
                pe.wait_ge(small_in[b % 2], 16 * 7 * (b // 2 + 1))
                if b > 0:
                    pe.wait_ge(cz_sb, b)
                pe.transpose(PA[:, 3, 0:P], CN[:, b % 2, 0:P], ident)
                pe.transpose(PA[:, 3, P:2 * P], CN[:, b % 2, SP_:SP_ + P], ident).then_inc(c_ps, 1)

            def b_to_rows(b):
                pe.wait_ge(bf_ready, b + 1)
                if b > 0:
                    pe.wait_ge(wb_sb, b)
                for g in range(BG):
                    m = pe.transpose(PS[:, g // 4, (g % 4) * P:(g % 4 + 1) * P], Bn[b % 2][:, g, :], ident)
                m.then_inc(b_ps, 1)

            def inside(b):
                pe.wait_ge(w_ready, 2 * b + 1)
                if b > 0:
                    pe.wait_ge(km_ready, b)
                for g in range(BG):
                    m = pe.matmul(PS[:, 2 + g // 4, (g % 4) * P:(g % 4 + 1) * P], Bn[b % 2][:, g, :], W1[b % 2][:, g, :],
                                  start=True, stop=True)
                m.then_inc(k_ps, 1)

            def additions(b):
                pe.wait_ge(wb_sb, b + 1)
                pe.wait_ge(ub_in[b % 2], 16 * TB * (b // 2 + 1))
                if b > 0:
                    pe.wait_ge(rot_used, b)
                for h in range(2):
                    for g in range(BG):
                        m = pe.matmul(PA[:, 1 + h, g * NB:(g + 1) * NB], WB[:, g, h * SP_:h * SP_ + P], UB[:, b % 2, g, :],
                                      start=True, stop=True)
                m.then_inc(v_ps, 1)

            def outputs(b):
                pe.wait_ge(km_ready, b + 1)
                pe.wait_ge(w_ready, 2 * b + 2)
                pe.wait_ge(m_ready, 2 * b + 2)
                if b > 0:
                    pe.wait_ge(y_sb, b)
                for g in range(BG):
                    dst = PA[:, 0, g * NB:(g + 1) * NB]
                    pe.matmul(dst, KM[b % 2][:, g, :], UB[:, b % 2, g, :], start=True, stop=False)
                    pe.matmul(dst, W1[b % 2][:, g, :], M12[:, 0, g, 0:NB], start=False, stop=False)
                    m = pe.matmul(dst, W2[b % 2][:, g, :], M12[:, 1, g, 0:NB], start=False, stop=True)
                m.then_inc(y_ps, 1)

            c_to_columns(0)
            c_to_columns(1)
            b_to_rows(0)
            inside(0)
            for b in range(NBATCH):
                additions(b)
                if b + 2 < NBATCH:
                    c_to_columns(b + 2)
                if b + 1 < NBATCH:
                    b_to_rows(b + 1)
                    inside(b + 1)
                outputs(b)
            pair_stage("s5_z", lambda k: both((HT6h, HT6l), slice(None), k), split="s5z")
            single_stage("s5_glu", lambda k: both((Uh, Ul), slice(None), k), split="g")
            single_stage("s5_out", lambda k: both((Zh, Zl), slice(None), k), split="z")
            norm("fin", T)
            pe.wait_ge(mt_in, 16)
            for k in range(KD):
                m = pe.transpose(PA[:, 2, k * NM:(k + 1) * NM], MT[0:NM, k * P:(k + 1) * P], con[0:NM, C_ID:C_ID + NM])
            m.then_inc(mt_ps, 1)
            norm("attn", T2)
            U2 = (U2h, U2l)

            def queries(k):
                return both(U2, slice(None), k, slice(NM, T2))

            def keyed(k):
                return both(U2, slice(None), k, slice(0, T2))

            pair_stage("cq", queries, split="attn")
            w = parts_view(tiles["ckv"][0].loads[0], (KD, A_QS - A_CKV))
            feature_tile(tiles["ckv"][0], lambda k: both(w, slice(None), k, slice(0, P)), keyed, KD, T2)
            feature_tile(tiles["kr"][0], lambda k: both(w, slice(None), k, slice(A_KR - A_CKV - MNOPE, A_KR - A_CKV + MROPE)),
                         keyed, KD, T2, MQK)
            pair_stage("qs", queries)
            pe.wait_ge(rt_in, 16)

            def rotate(stage):
                for j, (x, lo_row, hi_row, t0, c, tile) in enumerate(rotations(stage)):
                    n = ROT_AT[stage] + j
                    read_out(pe, tile)
                    if n >= 2:
                        pe.wait_ge(ro_read, n - 1)
                    width = T2 - t0
                    rows = P if hi_row == P else MQK
                    perm = rt[0:rows, (R_P if hi_row == P else R_MP):(R_P if hi_row == P else R_MP) + rows]
                    for h in range(2):
                        m = pe.matmul(PA[0:rows, 2 * (n % 2) + h, 0:width // 2], perm, x[0:rows, h * (width // 2):(h + 1) * (width // 2)],
                                      start=True, stop=True)
                    m.then_inc(ro_ps, 1)

            pair_stage("ks", keyed, T2, then=lambda i: norm("cq", T) if i == 0 else norm("ckv", T2) if i == 2 else None)
            norm_applied(pe, "ckv")
            rotate("qs")
            pair_stage("qi", queries)
            rotate("ks")
            w = parts_view(tiles["ki"][0].loads[0], (KD, P))
            feature_tile(tiles["ki"][0], lambda k: both(w, slice(None), k), keyed, KD, T2)
            tile = tiles["wi"][0]
            open_tile(tile)
            wi = parts_view(tile.loads[0], (KD, 8), KD * P)
            for i in range(NPAIR):
                for k in range(KD):
                    m = product(PS[:, 2 * tile.slot, i * 8:(i + 1) * 8], both(U2, slice(None), k, slice(NM + i * P, NM + (i + 1) * P)),
                                both(wi, slice(None), k), k == 0, k == KD - 1)
            m.then_inc(tile_done, 1)
            rotate("qi")
            pe.wait_ge(pad_zero, 2)
            token_stage("vs", U2, 5)
            rotate("k1")
            pe.wait_ge(xlo_ready, sum(SPLITS["cq"]))
            w = parts_view(tiles["uq"][0].loads[0], (2, MH * MQK))
            for h, tile in enumerate(tiles["uq"]):
                feature_tile(tile, lambda k: both(w, slice(None), k, slice(h * MQK, (h + 1) * MQK)),
                             lambda k: both((CQh, CQl), slice(None), k), 2, T, MQK)
            w = parts_view(tiles["ukn"][0].loads[0], (MH * P,))
            pe.wait_ge(xlo_ready, sum(SPLITS["ckv"]))
            pe.wait_ge(pad_zero, 4)
            for h, tile in enumerate(tiles["ukn"]):
                feature_tile(tile, lambda k: both(w, slice(None), slice(h * P, (h + 1) * P)),
                             lambda k: (CKh[:, 0:T2], CKl[:, 0:T2]), 1, T2)
            wv = tuple(x.rearrange("p (h m) -> p h m", h=MH)[:, :, MNOPE:P] for x in w)
            for i, tile in enumerate(tiles["ukvv"]):
                open_tile(tile)
                for b in range(2 if i < 2 else 1):
                    t0 = (2 * i + b) * P
                    m = product(PS[:, 2 * tile.slot + b, :], (CKh[:, t0:t0 + P], CKl[:, t0:t0 + P]), wv, True, True)
                m.then_inc(tile_done, 1)
            rotate("qm")

            pe.wait_ge(roped, 22)
            pe.wait_ge(kr_copied, MH)
            for tile in tiles["ukvv"][-2:]:
                read_out(pe, tile)
            att_n = 0

            def transposed(m):
                i = ATT_UNITS[m][1]
                pe.wait_ge(p_ready, m + 1)
                if m >= 2:
                    pe.wait_ge(oa_ready, m - 1)
                for j in range(i + 2):
                    ins = pe.transpose(PS[:, 2 * (m % 2) + j // 4, (j % 4) * P:(j % 4 + 1) * P], PB[:, m % 3, j * P:(j + 1) * P], ident)
                ins.then_inc(pT_ps, 1)

            def with_values(m):
                kind, i, h = ATT_UNITS[m]
                pe.wait_ge(pT_sb, m + 1)
                vals = Vm if kind == "mla" else VS
                for j in range(i + 2):
                    ins = pe.matmul(PS[:, 2 * (m % 2) + 1, 2 * P:3 * P], vals[:, j, (h // 2) * P:(h // 2 + 1) * P],
                                    PT2[:, m % 2, j * P:(j + 1) * P], start=j == 0, stop=j == i + 1)
                ins.then_inc(pv_out_ps, 1)

            for n, (kind, i, h) in enumerate(UNITS):
                if n >= 2:
                    pe.wait_ge(score_free[n % 2], n // 2)
                nk = keys(i)
                dst = scores(n % 2, i)
                r = slice((h % 2) * 64, (h % 2) * 64 + 64)
                qs = slice(i * P, (i + 1) * P)
                for b in range(dst.shape[1]):
                    w = nk // dst.shape[1]
                    ks = slice(b * w, (b + 1) * w)
                    if kind == "idx":
                        m = pe.matmul(dst[:, b, :], QI[r, h // 2, qs], KI_[r, ks], start=True, stop=True)
                    elif kind == "mla":
                        m = pe.matmul(dst[:, b, :], Qm[0:MQK, h, qs], Km[0:MQK, h, ks], start=True, stop=True)
                    else:
                        m = pe.matmul(dst[:, b, :], QS[r, h // 2, qs], KS[r, h // 2, ks], start=True, stop=True)
                m.then_inc(score_ps, 1)
                if kind != "idx":
                    if att_n >= 2:
                        transposed(att_n - 2)
                    if att_n >= 3:
                        with_values(att_n - 3)
                    att_n += 1
            for m in (att_n - 2, att_n - 1):
                transposed(m)
                with_values(m - 1)
            with_values(att_n - 1)
            pair_stage("attn_out", lambda k: both((OAh, OAl), slice(None), k), split="oa")
            norm("ffn", T)
            for i, tile in enumerate(tiles["ffn_up"]):
                open_tile(tile)
                w = parts_view(tile.loads[0], (2 * KD, P))
                for k, b in [(k, b) for k in range(KD) for b in range(2)] if i == 0 else [(k, b) for b in range(2) for k in range(KD)]:
                    if i == b == 0:
                        pe.wait_ge(xlo_ready, SPLITS["ffn"][0] + k + 1)
                    m = product(PS[:, 2 * tile.slot + b, :], both(w, slice(None), b * KD + k), both((U3h, U3l), slice(None), k),
                                k == 0, k == KD - 1)
                m.then_inc(tile_done, 1)
            for i, tile in enumerate(tiles["ffn_down"]):
                for j in range(2):
                    open_tile(tile) if j == 0 else weights_in(tile.loads[1])
                    w = parts_view(tile.loads[j], (11, P))
                    for k in range(11 * j, 11 * j + 11):
                        if i == 0:
                            pe.wait_ge(xlo_ready, SPLITS["h"][0] + k + 1)
                        m = product(PS[:, 2 * tile.slot, :], both(w, slice(None), k - 11 * j), both((HFh, HFl), slice(None), k),
                                    k == 0, k == KF - 1)
                    if j == 0:
                        half_done(tile, m)
                m.then_inc(tile_done, 1)
            norm("fin2", T)
            norm_applied(pe, "fin2")
            for tt in range(NPAIR):
                if tt >= 2:
                    pe.wait_ge(ot_sb, tt - 1)
                for k in range(KD):
                    m = pe.transpose(PA[:, 2 * (tt % 2) + k // 4, (k % 4) * P:(k % 4 + 1) * P], FO[:, k, tt * P:(tt + 1) * P], ident)
                m.then_inc(ot_ps, 1)

        def act_program(act):
            chain = [0]

            def link(ins):
                chain[0] += 1
                ins.then_inc(act_chain, 1)
                act.wait_ge(act_chain, chain[0])

            def square(name, i, src, width):
                s0 = NORMS[name][0]
                if i == 0 and name in BEFORE and name != "attn":
                    norm_applied(act, BEFORE[name])
                if i >= 2 and name in WIDE:
                    act.wait_ge(squares_summed, summed(name, i - 2))
                elif s0 > 0 or i >= 2:
                    act.wait_ge(sq_used, s0 if name in WIDE else s0 + i - 1)
                act.activation(sq[:, (s0 + i) % 2, 0:width], src, ACT.Square).then_inc(sq_ready, 1)

            def std(name, width, dim):
                s0, n0, k = NORMS[name]
                if name == "attn":
                    norm_applied(act, "fin")
                link(act.activation(warm[:], con[:, C_EPS:C_EPS + 1], ACT.Sqrt))
                act.wait_ge(sq_used, s0 + k)
                for rows, cols in token_blocks(width):
                    m = act.activation(rsc[rows, cols], PA[rows, 3, cols], ACT.Sqrt, scale=1.0 / dim, bias=con[rows, C_EPS:C_EPS + 1])
                m.then_inc(std_ready, 1)

            def norm(name, src, width, dim):
                for i in range(NORMS[name][2]):
                    square(name, i, src(i), width)
                std(name, width, dim)

            def output_squares(stage, name, src):
                for i, tile in enumerate(tiles[stage]):
                    split_weights(tile.loads[-1] + 1)
                    if i > 0:
                        read_out(act, tiles[stage][i - 1])
                        square(name, i - 1, src(i - 1), T)
                    act.wait_ge(tile_done, tile.t + 1)
                read_out(act, tiles[stage][-1])
                square(name, KD - 1, src(KD - 1), T)
                std(name, T, D)

            done = [0]

            def split_weights(upto):
                while done[0] <= min(upto, len(plan.loads) - 1):
                    n = done[0]
                    done[0] += 1
                    act.wait_ge(landed[n % NSLOT], plan.value[n])
                    act.activation(ring_hi[:, n % NSLOT, 0:plan.size[n]], ring[:, n % NSLOT, 0:plan.size[n]], ACT.Copy)\
                        .then_inc(whi_ready, 1)

            def high(name, i, src, dst):
                if name in VALS:
                    act.wait_ge(val_ready, VALS[name] + i + 1)
                act.activation(dst, src, ACT.Copy).then_inc(xhi_ready, 1)

            def high_normed(name, dst, width=T):
                for i in range(SPLITS[name][1]):
                    high(name, i, sq[:, i % 2, 0:width], dst(i))

            def evac(tile, dst, func=ACT.Copy, rows=P, **kw):
                split_weights(tile.loads[-1] + 1)
                act.wait_ge(tile_done, tile.t + 1)
                return act.activation(dst, PS[0:rows, 2 * tile.slot, 0:T], func, **kw).then_inc(slot_free[tile.slot], 1)

            act.dma_start(con[:], a["shape_constants"]).then_inc(con_in, 16)
            act.dma_start(gmask[:], a["chunk_constants"][:, C_GM:C_GM + T]).then_inc(con_in, 16)
            act.dma_start(rst[:], a["chunk_constants"][:, C_RST:C_RST + T]).then_inc(con_in, 16)

            def vec(name, row, n, src):
                act.dma_start(pvr[row:row + n, 0:P], src).then_inc(pv_in, 16)

            def col(x):
                return x.rearrange("(k p) -> k p", p=P)

            vec("gla_norm", PV_GLA, KD, col(a["gla_norm"][0]))
            vec("b_gate", PV_BG, 4, col(a["gla_b_gate"][0]))
            vec("head_gain", PV_HG, 4, col(a["gla_head_gain"][0]))
            vec("s5_norm", PV_S5, KD, col(a["s5_norm"][0]))
            vec("b_glu", PV_BGLU, KI, col(a["s5_b_glu"][0]))
            vec("d", PV_DS, KI, col(a["s5_d"][0].rearrange("g i -> (g i)")))
            vec("final_norm", PV_FIN, KD, col(a["final_norm"]))
            vec("attn_norm", PV_ATT, KD, col(a["attn_norm_g_2"][0]))
            vec("q_norm", PV_GQ, 2, col(a["mla_q_norm_g_2"][0]))
            vec("kv_norm", PV_GKV, 1, col(a["mla_kv_norm_g_2"][0]))
            vec("ffn_norm", PV_FFN, KD, col(a["ffn_norm_g_2"][0]))
            vec("final_norm_2", PV_FIN2, KD, col(a["final_norm_g_2"]))
            for k in range(KD):
                act.wait_ge(xT_ps, k + 1)
                act.activation(XT[:, k, :], PA[:, k % 4, :], ACT.Copy).then_inc(xT_sb, 1)
                if k > 0:
                    act.wait_ge(xT_sb, k)
                    square("gla", k - 1, XT[:, k - 1, :], T)
            act.wait_ge(xT_sb, KD)
            square("gla", KD - 1, XT[:, KD - 1, :], T)
            std("gla", T, D)
            act.wait_ge(pv_ps, 1)
            act.activation(pv[:], PS[:, 0, 0:PV_N], ACT.Copy).then_inc(pv_sb, 1)
            split_weights(1)
            high_normed("gla", lambda i: HTh[:, i, :])
            for i, tile in enumerate(tiles["gla_q"]):
                evac(tile, QG[:, i, :])
            for i, tile in enumerate(tiles["gla_k"]):
                evac(tile, KG[:, i, :])
            tile = tiles["gla_r"][0]
            evac(tile, R16[:])
            act.wait_ge(pv_sb, 1)
            def value(i):
                tile = tiles["gla_v"][i]
                split_weights(tile.loads[-1] + 1)
                act.wait_ge(tile_done, tile.t + 1)
                tt = (i % 2) * 2
                act.activation(V[:, tt:tt + 2, (i // 2) * T:(i // 2 + 1) * T], PS[:, 2 * tile.slot:2 * tile.slot + 2, :], ACT.Copy)\
                    .then_inc(slot_free[tile.slot], 1)
                if i % 2 == 1:
                    split_weights(tile.loads[-1] + 2)

            split_weights(tiles["gla_v"][0].loads[1])
            for h in range(GH):
                act.wait_ge(gate_ps, h + 1)
                link(act.activation(LA[:, h, :], PA[:, h, :], ACT.Identity, bias=pv[:, PV_BG + h:PV_BG + h + 1]))
                act.nop().then_inc(gate_ev, 1)
                if h > 0:
                    act.wait_ge(la_ready, h)
                link(act.activation(la_e[:], LA[:, h, :], ACT.Abs))
                link(act.activation(la_e[:], la_e[:], ACT.Exp, scale=-1.0))
                act.activation(la_e[:], la_e[:], ACT.Ln, bias=con[:, C_ONE:C_ONE + 1]).then_inc(gl_ready, 1)
                act.wait_ge(la_ready, h + 1)
                if h > 0:
                    act.wait_ge(qkg_ready, h)
                act.activation(ex_p[:], LA[:, h, :], ACT.Exp, scale=1.0 / GTAU).then_inc(ex_ready, 1)
                act.activation(ex_n[:], LA[:, h, :], ACT.Exp, scale=-1.0 / GTAU).then_inc(ex_ready, 1)
                act.wait_ge(de_ready, h + 1)
                act.activation(kend[:, h, :], kend[:, h, :], ACT.Exp, scale=1.0 / GTAU).then_inc(kx_ready, 1)
                value(h)
            for i in range(4, 8):
                value(i)
                if i == 5:
                    act.wait_ge(gx_ready, 1)
                    act.activation(gt[:, 8, :], gt[:, 7, :], ACT.Sin, scale=TWO_PI).then_inc(sin_ready, 1)
                    act.activation(gt[:, 9, :], gt[:, 7, :], ACT.Sin, scale=TWO_PI / 2).then_inc(sin_ready, 1)
            for h in range(GH):
                act.wait_ge(keT_ps, h + 1)
                act.activation(KE[:, :, h * P:(h + 1) * P], PA[:, h, :].rearrange("p (t d) -> p t d", t=NPAIR), ACT.Copy)\
                    .then_inc(keT_sb, 1)
            act.wait_ge(pt_ps, 1)
            act.activation(PT[:].rearrange("p a b -> p (a b)").rearrange("p (a b) -> p a b", a=2), PA[:, 2:4, :], ACT.Copy)\
                .then_inc(pt_sb, 1)
            n = 0
            for tt in range(NPAIR):
                for h in range(GH):
                    act.wait_ge(o_ps, n + 1)
                    act.activation(O[:, 4 * h:4 * h + 4, tt * P:(tt + 1) * P],
                                   PA[:, 2 + n % 2, :].rearrange("p (e c) -> p e c", e=4), ACT.Copy).then_inc(o_sb, 1)
                    n += 1
            act.wait_ge(o_sb, n)
            high_normed("gla2", lambda i: HT2h[:, i, :])
            norm_applied(act, "gla2")
            for i, tile in enumerate(tiles["gla_z"]):
                if i in HEAD_WITH:
                    h = HEAD_WITH[i]
                    norm(f"head{h}", lambda k: O[:, 4 * h + k, :], T, GDV)
                split_weights(tile.loads[-1] + 1)
                if i >= 2:
                    act.wait_ge(val_ready, VALS["o"] + i - 1)
                act.wait_ge(tile_done, tile.t + 1)
                act.activation(SZ[:, i % 2, :], PS[:, 2 * tile.slot, :], ACT.Silu).then_inc(slot_free[tile.slot], 1)
                if i > 0:
                    high("o", i - 1, O[:, i - 1, :], Oh[:, i - 1, :])
            high("o", KI - 1, O[:, KI - 1, :], Oh[:, KI - 1, :])
            output_squares("gla_out", "s5", lambda k: XT[:, k, :])
            for i in range(KD):
                high("s5", i, HT[:, i, :], HT5h[:, i, :])
            for i, tile in enumerate(tiles["s5_u"]):
                split_weights(min(tile.loads[-1] + 1, tiles["s5_u"][-1].loads[0]))
                act.wait_ge(tile_done, tile.t + 1)
                act.activation(U[:, i, :], PS[:, 2 * tile.slot, :], ACT.Copy).then_inc(slot_free[tile.slot], 1)
                read_out(act, tile)
                act.dma_start(u_dram[i * P:(i + 1) * P, :], U[:, i, :]).then_inc(u_out, 16)

            def columns(b):
                act.wait_ge(c_ps, b + 1)
                if b >= 2:
                    act.wait_ge(w_ready, 2 * (b - 1))
                act.activation(CZ[:, b % 2, :], PA[:, 3, 0:2 * P], ACT.Copy).then_inc(cz_sb, 1)

            def rotations_of(b):
                act.wait_ge(frac_ready, b + 1)
                act.activation(rot_s[:, b % 2], rot_c[:, b % 2], ACT.Sin, scale=sg2pi[:, 0:1]).then_inc(rot_ready, 1)
                link(act.activation(rot_c[:, b % 2], rot_c[:, b % 2], ACT.Abs))
                act.activation(rot_c[:, b % 2], rot_c[:, b % 2], ACT.Sin, scale=-TWO_PI, bias=con[:, C_HPI:C_HPI + 1])\
                    .then_inc(rot_ready, 1)

            def b_rows(b):
                act.wait_ge(b_ps, b + 1)
                if b > 0:
                    act.wait_ge(v_ps, b)
                bt4 = PS[:, 0:2, :].rearrange("p a (g m) -> p a g m", g=4)
                act.activation(WB[:, :, 0:P].rearrange("p (a g) m -> p a g m", a=2), bt4, ACT.Copy)
                act.activation(WB[:, :, P:P + SP_].rearrange("p (a g) m -> p a g m", a=2), bt4[:, :, :, 0:SP_], ACT.Copy)\
                    .then_inc(wb_sb, 1)

            def masked(b):
                act.wait_ge(k_ps, b + 1)
                if b >= 2:
                    act.wait_ge(y_ps, b - 1)
                for t in range(TB):
                    cols = slice(t * SGRP, (t + 1) * SGRP)
                    m = act.activation(KM[b % 2][:, :, cols], PS[:, 2:4, :].rearrange("p a (g m) -> p (a g) m", g=4)[:, :, cols], ACT.Copy,
                                       scale=con[:, C_SM + t * SGRP:C_SM + t * SGRP + 1])
                m.then_inc(km_ready, 1)

            columns(0)
            columns(1)
            rotations_of(0)
            b_rows(0)
            masked(0)
            rotations_of(1)
            for b in range(NBATCH):
                if b + 2 < NBATCH:
                    columns(b + 2)
                if b + 1 < NBATCH:
                    b_rows(b + 1)
                    masked(b + 1)
                if b == NBATCH - 1:
                    act.wait_ge(y_ps, b)
                    for i in range(KD):
                        high("s5z", i, HT[:, i, :], HT6h[:, i, :])
                    split_weights(tiles["s5_z"][0].loads[0])
                act.wait_ge(y_ps, b + 1)
                if b > 0:
                    act.wait_ge(y_out, 16 * TB * b)
                act.activation(YB, PA[:, 0, :], ACT.Copy).then_inc(y_sb, 1)
                act.wait_ge(y_sb, b + 1)
                dst = y_dram[b * P:(b + 1) * P, :].rearrange("(g i) (t n) -> t i g n", g=BG, t=TB)
                for t in range(TB):
                    act.dma_start(dst[t], YB[t * SGRP:(t + 1) * SGRP, :].rearrange("p (g n) -> p g n", g=BG)).then_inc(y_out, 16)
                if b + 2 < NBATCH:
                    rotations_of(b + 2)
            for b in range(NBATCH):
                act.wait_ge(yd_ready, b + 1)
                act.activation(U[:, b, :], U[:, b, :], ACT.Gelu_apprx_tanh).then_inc(gelu_done, 1)
                if b == 7:
                    split_weights(tiles["s5_z"][0].loads[0] + 1)
            act.wait_ge(gelu_done, NBATCH)
            for i, tile in enumerate(tiles["s5_z"]):
                split_weights(tile.loads[-1] + 1)
                act.wait_ge(tile_done, tile.t + 1)
                act.activation(Z[:, i, :], PS[:, 2 * tile.slot, :], ACT.Silu).then_inc(slot_free[tile.slot], 1)
                high("g", i, U[:, i, :], Uh[:, i, :])
            for i, tile in enumerate(tiles["s5_glu"]):
                split_weights(tile.loads[-1] + 1)
                if i >= 2:
                    act.wait_ge(val_ready, VALS["z"] + i - 1)
                act.wait_ge(tile_done, tile.t + 1)
                act.activation(sq[:, i % 2, 0:T], PS[:, 2 * tile.slot, :], ACT.Sigmoid, bias=pv[:, PV_BGLU + i:PV_BGLU + i + 1])\
                    .then_inc(slot_free[tile.slot], 1)
                if i > 0:
                    high("z", i - 1, Z[:, i - 1, :], Zh[:, i - 1, :])
            high("z", KI - 1, Z[:, KI - 1, :], Zh[:, KI - 1, :])
            output_squares("s5_out", "fin", lambda k: XT[:, k, :])
            act.wait_ge(mt_ps, 1)
            act.activation(X2[:, :, 0:NM], PA[:, 2, 0:KD * NM].rearrange("p (k m) -> p k m", k=KD), ACT.Copy).then_inc(mt_sb, 1)
            act.wait_ge(mt_sb, 1)
            for i in range(KD):
                act.wait_ge(normed, PLAIN["fin"] + i + 1)
                square("attn", i, X2[:, i, :], T2)
            std("attn", T2, D)
            high_normed("attn", lambda i: U2h[:, i, 0:T2], T2)

            def wide(tile, dst, rows=slice(0, P)):
                split_weights(tile.loads[-1] + 1)
                act.wait_ge(tile_done, tile.t + 1)
                act.activation(dst.rearrange("p (h n) -> p h n", h=2), PS[rows, 2 * tile.slot:2 * tile.slot + 2, 0:HALF], ACT.Copy)\
                    .then_inc(slot_free[tile.slot], 1)

            for i, tile in enumerate(tiles["cq"]):
                evac(tile, CQ[:, i, :])
            wide(tiles["ckv"][0], CK[:, 0:T2])
            wide(tiles["kr"][0], KR[0:MQK, :], slice(0, MQK))
            for i, tile in enumerate(tiles["qs"]):
                evac(tile, QS[:, i, :])
            for tile in (*tiles["cq"], *tiles["ckv"]):
                read_out(act, tile)
            for i, tile in enumerate(tiles["ks"]):
                if i == 0:
                    norm("cq", lambda k: CQ[:, k, :], T, MQR)
                    high_normed("cq", lambda i: CQh[:, i, :])
                if i == 2:
                    norm("ckv", lambda k: CK[:, 0:T2], T2, MKR)
                    high_normed("ckv", lambda i: CKh[:, 0:T2], T2)
                wide(tile, KS[:, i, :])
            for i, tile in enumerate(tiles["qi"]):
                evac(tile, QI[:, i, :])
            wide(tiles["ki"][0], KI_[:])
            tile = tiles["wi"][0]
            act.wait_ge(tile_done, tile.t + 1)
            act.activation(WI[:], PS[:, 2 * tile.slot, 0:NPAIR * 8].rearrange("p (i h) -> p i h", i=NPAIR), ACT.Copy, scale=8 ** -0.5)\
                .then_inc(slot_free[tile.slot], 1)

            def values(stage, dst):
                for i, tile in enumerate(tiles[stage]):
                    split_weights(tile.loads[-1] + 1)
                    act.wait_ge(tile_done, tile.t + 1)
                    nb = 2 if i < 2 else 1
                    act.activation(dst[:, 2 * i:2 * i + nb, :], PS[:, 2 * tile.slot:2 * tile.slot + nb, :], ACT.Copy)\
                        .then_inc(slot_free[tile.slot], 1)

            values("vs", VS)
            for h, tile in enumerate(tiles["uq"]):
                evac(tile, Qm[0:MQK, h, :], rows=MQK)
            for h, tile in enumerate(tiles["ukn"]):
                wide(tile, Km[0:MNOPE, h, :], slice(0, MNOPE))
            values("ukvv", Vm)
            split_weights(tiles["attn_out"][0].loads[0] + NSLOT - 1)

            n_idx = n_att = 0

            def copy_transposed(m):
                i = ATT_UNITS[m][1]
                act.wait_ge(pT_ps, m + 1)
                if m >= 2:
                    act.wait_ge(pv_out_ps, m - 1)
                act.activation(PT2[:, m % 2, 0:(i + 2) * P],
                               PS[:, 2 * (m % 2):2 * (m % 2) + 2, :].rearrange("p a b -> p (a b)")[:, 0:(i + 2) * P], ACT.Copy)\
                    .then_inc(pT_sb, 1)

            for n, (kind, i, h) in enumerate(UNITS):
                nk = keys(i)
                if kind == "idx":
                    act.wait_ge(score_ps, n + 1)
                    if n_idx >= 2:
                        act.wait_ge(acc_used, n_idx - 1)
                    act.activation(split(RL[:, n_idx % 2, 0:nk], i), scores(n % 2, i), ACT.Relu, scale=64 ** -0.5)\
                        .then_inc(score_free[n % 2], 1)
                    act.wait_ge(score_free[n % 2], n // 2 + 1)
                    act.nop().then_inc(relu_ready, 1)
                    n_idx += 1
                    continue
                scale = (MQK if kind == "mla" else DHD) ** -0.5
                p = n_att % 3
                act.wait_ge(max_ready, n_att + 1)
                act.activation(PB[:, p, 0:nk], PB[:, p, 0:nk], ACT.Exp, scale=scale, bias=mx[:, p, 1:2],
                               accum_out=mx[:, p, 2:3]).then_inc(exp_ready, 1)
                if n_att >= 2:
                    copy_transposed(n_att - 2)
                n_att += 1
            for m in (n_att - 2, n_att - 1):
                copy_transposed(m)
            act.wait_ge(oa_ready, 2 * MH * NPAIR)
            for i in range(KD):
                high("oa", i, OA[:, i, :], OAh[:, i, :])
            output_squares("attn_out", "ffn", lambda k: X2[:, k, NM:T2])
            high_normed("ffn", lambda i: U3h[:, i, :])
            for i, tile in enumerate(tiles["ffn_up"]):
                split_weights(tile.loads[-1] + 1)
                act.wait_ge(tile_done, tile.t + 1)
                if i >= 2:
                    read_out(act, tiles["ffn_up"][i - 2])
                act.activation(SF[:, i % 2, :], PS[:, 2 * tile.slot, :], ACT.Silu).then_inc(silu_ready, 1)
                if i > 0:
                    read_out(act, tiles["ffn_up"][i - 1])
                    high("h", i - 1, HF[:, i - 1, :], HFh[:, i - 1, :])
            read_out(act, tiles["ffn_up"][-1])
            high("h", KF - 1, HF[:, KF - 1, :], HFh[:, KF - 1, :])
            output_squares("ffn_down", "fin2", lambda k: X2[:, k, NM:T2])
            for tt in range(NPAIR):
                act.wait_ge(ot_ps, tt + 1)
                act.activation(OT[:, tt, :], PA[:, 2 * (tt % 2):2 * (tt % 2) + 2, :].rearrange("p a b -> p (a b)"), ACT.Copy)\
                    .then_inc(ot_sb, 1)

        def dve_program(dve):
            chain = [0]

            def link(ins):
                chain[0] += 1
                ins.then_inc(dve_chain, 1)
                dve.wait_ge(dve_chain, chain[0])

            def low(name, i, src, hi, lo_):
                dve.wait_ge(xhi_ready, SPLITS[name][0] + i + 1)
                dve.tensor_tensor(lo_, src, hi.bitcast(F32), ALU.subtract).then_inc(xlo_ready, 1)

            def sum_squares(name, i, width=T):
                s0, _, k = NORMS[name]
                if 0 < i < k - 1:
                    dve.wait_ge(sq_ready, s0 + i + 1)
                    if i > 1:
                        dve.wait_ge(squares_summed, summed(name, i - 1))
                    tt(ssq[:, 0:width], sq[:, (s0 + i - 1) % 2, 0:width] if i == 1 else ssq[:, 0:width],
                       sq[:, (s0 + i) % 2, 0:width], ALU.add).then_inc(squares_summed, 1)

            def scales(name, width):
                n0 = NORMS[name][1]
                dve.wait_ge(std_ready, n0 + 1)
                for rows, cols in token_blocks(width):
                    m = dve.reciprocal(rsc[rows, cols], rsc[rows, cols])
                m.then_inc(rstd_ready, 1)
                dve.wait_ge(rs_ps, n0 + 1)

            def norm(name, src, dst, gain, width, then=None):
                scales(name, width)
                for i in range(NORMS[name][2]):
                    dve.scalar_tensor_tensor(out=dst(i), in0=src(i), scalar=pv[:, gain + i:gain + i + 1], in1=scale_rows(width),
                                             op0=ALU.mult, op1=ALU.mult).then_inc(normed, 1)
                    if then:
                        then(i)

            def norm_split(name, src, hi, lo_, gain, width, r=None):
                r = scale_rows(width) if r is None else r
                k = SPLITS[name][1]
                for i in range(k + 1):
                    if i < k:
                        if i >= 2:
                            dve.wait_ge(xlo_ready, SPLITS[name][0] + i - 1)
                        dve.scalar_tensor_tensor(out=sq[:, i % 2, 0:width], in0=src(i), scalar=pv[:, gain + i:gain + i + 1],
                                                 in1=r[:, 0:width], op0=ALU.mult, op1=ALU.mult).then_inc(val_ready, 1)
                    if i > 0:
                        low(name, i - 1, sq[:, (i - 1) % 2, 0:width], hi(i - 1), lo_(i - 1))

            tt, ts, stt = dve.tensor_tensor, dve.tensor_scalar, dve.scalar_tensor_tensor
            dve.memset(WG[:], 0.0).then_inc(wg_zero, 1)
            dve.wait_ge(con_in, 48)
            for i in range(KD):
                sum_squares("gla", i)
            scales("gla", T)
            link(dve.tensor_copy(rs1[:], scale_rows(T)))
            dve.wait_ge(pv_sb, 1)
            norm_split("gla", lambda k: XT[:, k, :], lambda k: HTh[:, k, :], lambda k: HTl[:, k, :], PV_GLA, T)
            for i in (-2, -1):
                read_out(dve, tiles["gla_k"][i])
            for h in range(GH):
                dve.wait_ge(gl_ready, h + 1)
                link(dve.scalar_tensor_tensor(out=LA[:, h, :], in0=LA[:, h, :], scalar=0.0, in1=la_e[:],
                                              op0=ALU.min, op1=ALU.subtract))
                dve.tensor_tensor_scan(LA[:, h, :], rst[:], LA[:, h, :], 0.0, ALU.mult, ALU.add)\
                    .then_inc(la_ready, 1)
                dve.wait_ge(la_ready, h + 1)
                la3 = LA[:, h, :].rearrange("p (c t) -> p c t", t=GCH)
                last = la3[:, :, GCH - 1:GCH]
                dve.tensor_tensor(kend[:, h, :].rearrange("p (c t) -> p c t", t=GCH), last.broadcast_to([P, NCH, GCH]), la3,
                                  ALU.subtract).then_inc(de_ready, 1)
                dve.wait_ge(ex_ready, 2 * h + 2)
                link(dve.tensor_copy(dec[:, h, :], ex_p[:].rearrange("p (c t) -> p c t", t=GCH)[:, :, GCH - 1]))
                link(dve.scalar_tensor_tensor(out=QG[:, h, :], in0=QG[:, h, :], scalar=GDK ** -0.5, in1=ex_p[:],
                                              op0=ALU.mult, op1=ALU.mult))
                dve.wait_ge(kx_ready, h + 1)
                dve.tensor_tensor(kend[:, h, :], kend[:, h, :], KG[:, h, :], ALU.mult).then_inc(ke_ready, 1)
                dve.wait_ge(ke_ready, h + 1)
                dve.tensor_tensor(KG[:, h, :], KG[:, h, :], ex_n[:], ALU.mult).then_inc(qkg_ready, 1)
            dve.wait_ge(qkg_ready, GH)
            link(dve.memset(ATT[:].rearrange("p a b -> p (a b)"), 0.0))
            dve.wait_ge(par_in, 16 * 3)

            def mul(o, x, y):
                link(tt(o, x, y, ALU.mult))

            def round_to(o, x):
                link(ts(o, x, ROUND, ROUND, ALU.add, ALU.subtract))

            def expm1(x, n, r, t, p2, ni):
                link(ts(n, x, 1 / math.log(2), None, ALU.mult))
                round_to(n, n)
                ln2_hi = 0.693359375
                link(stt(out=r, in0=n, scalar=-ln2_hi, in1=x, op0=ALU.mult, op1=ALU.add))
                link(stt(out=r, in0=n, scalar=ln2_hi - math.log(2), in1=r, op0=ALU.mult, op1=ALU.add))
                link(ts(t, r, 1 / 8, 1.0, ALU.mult, ALU.add))
                for m in range(7, 1, -1):
                    mul(t, t, r)
                    link(ts(t, t, 1 / m, 1.0, ALU.mult, ALU.add))
                mul(t, t, r)
                link(ts(n, n, 127.0, None, ALU.add))
                link(dve.tensor_copy(ni, n))
                link(dve.tensor_single_scalar(p2.bitcast(I32), ni, 23, ALU.logical_shift_left))

            g = [gt[:, i, :] for i in range(16)]
            d = [gdt[:, i:i + 1] for i in range(8)]
            link(ts(d[1], d[0], -80.0, 80.0, ALU.max, ALU.min))
            expm1(d[1], d[2], d[3], d[4], d[5], gi[:, 0:1])
            mul(d[4], d[4], d[5])
            link(tt(d[6], d[4], d[5], ALU.add))
            link(ts(g[0], glr[:], d[6], A_MIN, ALU.mult, ALU.max))
            link(ts(g[6], gli[:], d[6], 1 / (2 * math.pi), ALU.mult, ALU.mult))
            round_to(g[7], g[6])
            tt(g[7], g[6], g[7], ALU.subtract).then_inc(gx_ready, 1)
            dve.wait_ge(gx_ready, 1)
            expm1(g[0], g[1], g[2], g[3], g[4], gi[:])
            mul(g[3], g[3], g[4])
            link(stt(out=g[5], in0=g[4], scalar=-1.0, in1=g[3], op0=ALU.add, op1=ALU.add))
            link(tt(g[4], g[3], g[4], ALU.add))
            dve.wait_ge(sin_ready, 2)
            mul(g[9], g[9], g[9])
            link(ts(g[9], g[9], 2.0, None, ALU.mult))
            link(ts(g[10], g[9], -1.0, 1.0, ALU.mult, ALU.add))
            tp = [TPg[:, i, 0:SP_] for i in range(8)]
            mul(tp[0], g[4], g[10])
            mul(tp[1], g[4], g[8])
            mul(g[11], g[5], g[10])
            link(tt(g[11], g[11], g[9], ALU.subtract))
            link(dve.reciprocal(g[12], g[4]))
            mul(tp[2], g[12], g[10])
            link(stt(out=tp[3], in0=g[12], scalar=-1.0, in1=g[8], op0=ALU.mult, op1=ALU.mult))
            mul(g[12], glr[:], glr[:])
            mul(g[13], gli[:], gli[:])
            link(tt(g[12], g[12], g[13], ALU.add))
            link(dve.reciprocal(g[12], g[12]))
            mul(g[13], g[11], glr[:])
            mul(g[14], tp[1], gli[:])
            link(tt(g[13], g[13], g[14], ALU.add))
            mul(tp[4], g[13], g[12])
            mul(g[13], tp[1], glr[:])
            mul(g[14], g[11], gli[:])
            link(tt(g[13], g[13], g[14], ALU.subtract))
            mul(tp[5], g[13], g[12])
            mul(g[13], g[4], g[4])
            mul(g[13], g[13], g[13])
            mul(tp[6], g[13], g[13])
            link(ts(g[13], g[7], float(TB), None, ALU.mult))
            round_to(g[14], g[13])
            link(tt(tp[7], g[13], g[14], ALU.subtract))
            dve.tensor_copy(TPg[:, :, SP_:P], TPg[:, :, 0:SP_]).then_inc(tp_ready, 1)

            for h in range(GH):
                dve.wait_ge(att_ps, h + 1)
                dve.copy_predicated(ATT[:, h, :], gmask[:].bitcast(U32), PA[:, h, :]).then_inc(att_sb, 1)
            dve.wait_ge(keT_ps, GH)
            for tile in tiles["gla_v"][-2:]:
                read_out(dve, tile)
            for n, (c, h) in enumerate(KV_ORDER):
                dve.wait_ge(kv_ps, n + 1)
                if c >= 3:
                    dve.wait_ge(o_ps, GH * ((c - 2) // 2) + h + 1)
                if c > 0:
                    dve.wait_ge(S_ready, KV_COUNT[c - 1, h])
                hs = slice(h * GDV, (h + 1) * GDV)
                if c == 0:
                    dve.tensor_copy(S[:, 0, hs], PA[:, n % 2, :]).then_inc(S_ready, 1)
                else:
                    dve.scalar_tensor_tensor(out=S[:, c % 3, hs], in0=S[:, (c - 1) % 3, hs], scalar=dec[:, h, c:c + 1],
                                             in1=PA[:, n % 2, :], op0=ALU.mult, op1=ALU.add).then_inc(S_ready, 1)
            dve.wait_ge(o_sb, GH * NPAIR)
            norm_split("gla2", lambda k: XT[:, k, :], lambda k: HT2h[:, k, :], lambda k: HT2l[:, k, :], PV_GLA, T, rs1)
            for i, tile in enumerate(tiles["gla_z"]):
                if i in HEAD_WITH:
                    h = HEAD_WITH[i]
                    for k in range(4):
                        sum_squares(f"head{h}", k)
                    norm(f"head{h}", lambda k: O[:, 4 * h + k, :], lambda k: O[:, 4 * h + k, :], PV_HG, T)
                    norm_applied(dve, f"head{h}")
                read_out(dve, tile)
                dve.tensor_tensor(O[:, i, :], O[:, i, :], SZ[:, i % 2, :], ALU.mult).then_inc(val_ready, 1)
                if i > 0:
                    low("o", i - 1, O[:, i - 1, :], Oh[:, i - 1, :], Ol[:, i - 1, :])
            low("o", KI - 1, O[:, KI - 1, :], Oh[:, KI - 1, :], Ol[:, KI - 1, :])
            dve.wait_ge(pt_sb, 1)
            L, LI, CO = (PT[:, 0, :], PT[:, 1, :]), (PT[:, 2, :], PT[:, 3, :]), (PT[:, 4, :], PT[:, 5, :])

            def cmul(dst, x, y):
                link(tt(ctmp[:, 0, :], x[1], y[1], ALU.mult))
                link(tt(ctmp[:, 1, :], x[1], y[0], ALU.mult))
                link(tt(dst[0], x[0], y[0], ALU.mult))
                link(tt(dst[1], x[0], y[1], ALU.mult))
                link(tt(dst[0], dst[0], ctmp[:, 0, :], ALU.subtract))
                link(tt(dst[1], dst[1], ctmp[:, 1, :], ALU.add))

            def pw(i, k):
                return PW[:, 2 * i, k, :], PW[:, 2 * i + 1, k, :]

            for c in range(2):
                link(dve.tensor_copy(pw(0, 0)[c], L[c]))
            cmul(pw(1, 0), CO, LI)
            for i, tile in enumerate(tiles["gla_out"]):
                if i > 0:
                    cmul(pw(0, i), pw(0, i - 1), L)
                    cmul(pw(1, i), pw(1, i - 1), LI)
                dve.wait_ge(tile_done, tile.t + 1)
                dve.tensor_tensor(XT[:, i, :], XT[:, i, :], PS[:, 2 * tile.slot, :], ALU.add).then_inc(slot_free[tile.slot], 1)
                sum_squares("s5", i - 1)
            link(dve.tensor_copy(r8f8[:], PT[:, 6:8, :]))
            link(ts(sg2pi[:, 0:1], con[:, C_SG:C_SG + 1], TWO_PI, None, ALU.mult))
            sg, nsg = con[:, C_SG:C_SG + 1], con[:, C_NSG:C_NSG + 1]
            for i, scale in ((0, sg), (1, -1.0), (3, nsg)):
                v = PW[:, i, :, :].rearrange("p a b -> p (a b)")
                link(ts(v, v, scale, None, ALU.mult))
            dve.nop().then_inc(pw_ready, 1)


            for tile in tiles["gla_out"][-2:]:
                read_out(dve, tile)
            scales("s5", T)
            for i in range(KD + 1):
                if i < KD:
                    stt(out=sn(HT[:, i, :]), in0=by_block(XT[:, i, :]), scalar=pv[:, PV_S5 + i:PV_S5 + i + 1],
                        in1=by_block(scale_rows(T)), op0=ALU.mult, op1=ALU.mult).then_inc(val_ready, 1)
                if i > 0:
                    low("s5", i - 1, HT[:, i - 1, :], HT5h[:, i - 1, :], HT5l[:, i - 1, :])
            def factor(i, b):
                return PW[:, i, :, b * BG:(b + 1) * BG].rearrange("p k g -> p g k").unsqueeze(3).broadcast_to([P, BG, TB, SGRP])

            def rows(ap):
                return ap.rearrange("p g j -> p g j").unsqueeze(2).broadcast_to([P, BG, TB, SGRP])

            def four(ap):
                return ap.rearrange("p g (s j) -> p g s j", s=TB)

            def add_skip(b):
                dve.wait_ge(y_in, 16 * (b + 1))
                stt(out=U[:, b, :], in0=U[:, b, :], scalar=pv[:, PV_DS + b:PV_DS + b + 1], in1=YIN, op0=ALU.mult, op1=ALU.add)\
                    .then_inc(yd_ready, 1)

            def b_factors(b):
                p = b % 2
                dve.wait_ge(small_in[p], 16 * 7 * (b // 2 + 1))
                if b >= 2:
                    dve.wait_ge(k_ps, b - 1)
                link(tt(four(Bn[p][:]), factor(2, b), rows(BZ[:, p, 0]), ALU.mult))
                link(tt(four(b_tmp[:]), factor(3, b), rows(BZ[:, p, 1]), ALU.mult))
                tt(Bn[p][:], Bn[p][:], b_tmp[:], ALU.add).then_inc(bf_ready, 1)
                dve.wait_ge(bf_ready, b + 1)

            def turns(b):
                rc, rk = rot_c[:, b % 2], rot_s[:, b % 2]
                if b >= 2:
                    dve.wait_ge(m_ready, 2 * (b - 1))
                link(tt(rc, r8f8[:, 1, b * BG:(b + 1) * BG].unsqueeze(2).broadcast_to([P, BG, NB1]),
                        con[:, C_NI:C_NI + NB1].unsqueeze(1).broadcast_to([P, BG, NB1]), ALU.mult))
                round_to(rk, rc)
                tt(rc, rc, rk, ALU.subtract).then_inc(frac_ready, 1)
                tt(dk[:, b % 2], r8f8[:, 0, b * BG:(b + 1) * BG].unsqueeze(2).broadcast_to([P, BG, NB1]),
                   con[:, C_NM:C_NM + NB1].unsqueeze(1).broadcast_to([P, BG, NB1]), ALU.mult).then_inc(dk_ready, 1)

            def scan(b):
                cos, sin = rot_c[:, b % 2], rot_s[:, b % 2]
                dve.wait_ge(rot_ready, 2 * b + 2)
                dve.wait_ge(v_ps, b + 1)
                own = [M12[:, i, :, 1:NB1] for i in range(2)]
                v = [PA[:, 1 + i, :].rearrange("p (g n) -> p g n", g=BG) for i in range(2)]
                link(tt(own[0], v[0], cos[:, :, 0:NB], ALU.mult))
                tt(own[1], v[1], sin[:, :, 0:NB], ALU.mult).then_inc(rot_used, 1)
                dve.wait_ge(rot_used, b + 1)
                link(tt(own[0], own[0], own[1], ALU.add))
                dve.wait_ge(dk_ready, b + 1)
                link(dve.tensor_tensor_scan(M12[:, 1].rearrange("p g n -> p (g n)"), M12[:, 0].rearrange("p g n -> p (g n)"),
                                            dk[:, b % 2].rearrange("p g n -> p (g n)"), 0.0, ALU.add, ALU.mult))
                tt(M12[:, 0], M12[:, 1], cos, ALU.mult).then_inc(m_ready, 1)
                dve.wait_ge(m_ready, 2 * b + 1)
                tt(M12[:, 1], M12[:, 1], sin, ALU.mult).then_inc(m_ready, 1)

            dve.wait_ge(tile_done, tiles["s5_u"][-1].t + 1)
            link(dve.memset(M12[:].rearrange("p a g n -> p (a g n)"), 0.0))
            for b in range(2):
                b_factors(b)
                turns(b)
            for b in range(NBATCH):
                scan(b)
                if b + 2 < NBATCH:
                    turns(b + 2)
                    b_factors(b + 2)
                if b == NBATCH - 1:
                    for i in range(KD):
                        low("s5z", i, HT[:, i, :], HT6h[:, i, :], HT6l[:, i, :])
                if b > 0:
                    add_skip(b - 1)
            add_skip(NBATCH - 1)
            for i, tile in enumerate(tiles["s5_z"]):
                dve.wait_ge(gelu_done, NBATCH)
                read_out(dve, tile)
                tt(Z[:, i, :], Z[:, i, :], U[:, i, :], ALU.mult).then_inc(oz_ready, 1)
                low("g", i, U[:, i, :], Uh[:, i, :], Ul[:, i, :])
            for i, tile in enumerate(tiles["s5_glu"]):
                read_out(dve, tile)
                tt(Z[:, i, :], Z[:, i, :], sq[:, i % 2, 0:T], ALU.mult).then_inc(val_ready, 1)
                if i > 0:
                    low("z", i - 1, Z[:, i - 1, :], Zh[:, i - 1, :], Zl[:, i - 1, :])
            low("z", KI - 1, Z[:, KI - 1, :], Zh[:, KI - 1, :], Zl[:, KI - 1, :])
            for i, tile in enumerate(tiles["s5_out"]):
                dve.wait_ge(tile_done, tile.t + 1)
                tt(by_block(XT[:, i, :]), by_block(XT[:, i, :]), sn(PS[:, 2 * tile.slot, :]), ALU.add).then_inc(slot_free[tile.slot], 1)
                sum_squares("fin", i - 1)
            for tile in tiles["s5_out"][-2:]:
                read_out(dve, tile)
            norm("fin", lambda k: XT[:, k, :], lambda k: X2[:, k, NM:T2], PV_FIN, T, then=lambda k: sum_squares("attn", k - 1, T2))
            dve.memset(U2h[:, :, T2:TPAD].bitcast(F32), 0.0).then_inc(pad_zero, 1)
            dve.memset(U2l[:, :, T2:TPAD].bitcast(F32), 0.0).then_inc(pad_zero, 1)
            dve.wait_ge(mt_sb, 1)
            norm_applied(dve, "fin")
            scales("attn", T2)
            norm_split("attn", lambda k: X2[:, k, :], lambda k: U2h[:, k, 0:T2], lambda k: U2l[:, k, 0:T2], PV_ATT, T2)
            dve.memset(CKh[:, T2:TPAD].bitcast(F32), 0.0).then_inc(pad_zero, 1)
            dve.memset(CKl[:, T2:TPAD].bitcast(F32), 0.0).then_inc(pad_zero, 1)
            scales("cq", T)
            norm_split("cq", lambda k: CQ[:, k, :], lambda k: CQh[:, k, :], lambda k: CQl[:, k, :], PV_GQ, T)
            scales("ckv", T2)
            norm_split("ckv", lambda k: CK[:, 0:T2], lambda k: CKh[:, 0:T2], lambda k: CKl[:, 0:T2], PV_GKV, T2)
            dve.wait_ge(rt_in, 16)
            for stage in ROT_STAGES:
                if stage == "qm":
                    dve.wait_ge(tile_done, tiles["vs"][-1].t + 1)
                    dve.wait_ge(roped, ROT_AT["qm"])
                    for h in range(MH):
                        dve.tensor_copy(Km[MNOPE:MQK, h, :], KR[MNOPE:MQK, :]).then_inc(kr_copied, 1)
                for j, (x, lo_row, hi_row, t0, c, tile) in enumerate(rotations(stage)):
                    n = ROT_AT[stage] + j
                    width = T2 - t0
                    r = slice(lo_row, hi_row)
                    sin = c + T2
                    dve.wait_ge(ro_ps, n + 1)
                    tt(halves(ro[r, n % 2, 0:width], 2), PA[r, 2 * (n % 2):2 * (n % 2) + 2, 0:width // 2],
                       halves(rt[r, sin + t0:sin + T2], 2), ALU.mult).then_inc(ro_read, 1)
                    link(tt(x[r, :], x[r, :], rt[r, c + t0:c + T2], ALU.mult))
                    dve.wait_ge(ro_read, n + 1)
                    tt(x[r, :], x[r, :], ro[r, n % 2, 0:width], ALU.add).then_inc(roped, 1)

            n_idx = n_att = 0

            def output(m):
                kind, i, h = ATT_UNITS[m]
                dve.wait_ge(pv_out_ps, m + 1)
                r = slice((h % 2) * 64, (h % 2) * 64 + 64)
                dve.tensor_copy(OA[r, (0 if kind == "mla" else 4) + h // 2, i * P:(i + 1) * P], PS[r, 2 * (m % 2) + 1, 2 * P:3 * P])\
                    .then_inc(oa_ready, 1)

            dve.wait_ge(pb_zero, 1)
            dve.wait_ge(roped, 22)
            for n, (kind, i, h) in enumerate(UNITS):
                nk = keys(i)
                cb = rt[:, C_CB + T2 - nk:C_CB + T2]
                if kind == "idx":
                    dve.wait_ge(relu_ready, n_idx + 1)
                    if n_idx > 0:
                        dve.wait_ge(acc_used, n_idx)
                    wih = WI[:, i, h:h + 1]
                    if h == 0:
                        ts(acc[:, 0:nk], RL[:, n_idx % 2, 0:nk], wih, None, ALU.mult).then_inc(acc_used, 1)
                    else:
                        stt(out=acc[:, 0:nk], in0=RL[:, n_idx % 2, 0:nk], scalar=wih, in1=acc[:, 0:nk], op0=ALU.mult, op1=ALU.add)\
                            .then_inc(acc_used, 1)
                    n_idx += 1
                    if h == 7:
                        dve.wait_ge(acc_used, n_idx)
                        link(tt(acc[:, 0:nk], acc[:, 0:nk], cb, ALU.add))
                    continue
                if n_att >= 4:
                    output(n_att - 4)
                scale = (MQK if kind == "mla" else DHD) ** -0.5
                p = n_att % 3
                dve.wait_ge(score_ps, n + 1)
                if n_att >= 3:
                    dve.wait_ge(pT_ps, n_att - 2)
                bias = cb if kind == "mla" else selb[:, 0:nk]
                dve.tensor_tensor_reduce(split(PB[:, p, 0:nk], i), scores(n % 2, i), split(bias, i), 1.0, TAKEN, ALU.add, ALU.max,
                                         mx[:, p, 0:1]).then_inc(score_free[n % 2], 1)
                dve.wait_ge(score_free[n % 2], n // 2 + 1)
                ts(mx[:, p, 1:2], mx[:, p, 0:1], -scale, None, ALU.mult).then_inc(max_ready, 1)
                tile_i, rounds = selection_rounds(kind, i, h)
                for _ in range(rounds):
                    nks = keys(tile_i)
                    link(dve.max(top8[:], acc[:, 0:nks]))
                    link(dve.match_replace(out=acc[:, 0:nks], in_to_replace=top8[:], in_values=acc[:, 0:nks], imm_value=TAKEN))
                dve.wait_ge(exp_ready, n_att + 1)
                dve.reciprocal(mx[:, p, 3:4], mx[:, p, 2:3]).then_inc(rsum_ready, 1)
                if kind == "mla" and h == MH - 1:
                    link(ts(selb[:, 0:nk], acc[:, 0:nk], TAKEN, 1.0, ALU.is_equal, ALU.subtract))
                    link(stt(out=selb[:, 0:nk], in0=selb[:, 0:nk], scalar=-LOW, in1=cb, op0=ALU.mult, op1=ALU.add))
                n_att += 1
            for m in range(n_att - 4, n_att):
                output(m)
            for i in range(KD):
                low("oa", i, OA[:, i, :], OAh[:, i, :], OAl[:, i, :])
            for i, tile in enumerate(tiles["attn_out"]):
                dve.wait_ge(tile_done, tile.t + 1)
                tt(X2[:, i, NM:T2], X2[:, i, NM:T2], PS[:, 2 * tile.slot, :], ALU.add).then_inc(slot_free[tile.slot], 1)
                sum_squares("ffn", i - 1)
            for tile in tiles["attn_out"][-2:]:
                read_out(dve, tile)
            scales("ffn", T)
            norm_split("ffn", lambda k: X2[:, k, NM:T2], lambda k: U3h[:, k, :], lambda k: U3l[:, k, :], PV_FFN, T)
            for i, tile in enumerate(tiles["ffn_up"]):
                dve.wait_ge(silu_ready, i + 1)
                dve.wait_ge(tile_done, tile.t + 1)
                tt(HF[:, i, :], SF[:, i % 2, :], PS[:, 2 * tile.slot + 1, :], ALU.mult).then_inc(slot_free[tile.slot], 1)
                if i > 0:
                    low("h", i - 1, HF[:, i - 1, :], HFh[:, i - 1, :], HFl[:, i - 1, :])
            low("h", KF - 1, HF[:, KF - 1, :], HFh[:, KF - 1, :], HFl[:, KF - 1, :])
            for i, tile in enumerate(tiles["ffn_down"]):
                dve.wait_ge(tile_done, tile.t + 1)
                tt(X2[:, i, NM:T2], X2[:, i, NM:T2], PS[:, 2 * tile.slot, :], ALU.add).then_inc(slot_free[tile.slot], 1)
                sum_squares("fin2", i - 1)
            for tile in tiles["ffn_down"][-2:]:
                read_out(dve, tile)
            norm("fin2", lambda k: X2[:, k, NM:T2], lambda k: FO[:, k, :], PV_FIN2, T)

        def pool_program(pool):
            pool.dma_start(glr[:], a["s5_lam_re"][0]).then_inc(par_in, 16)
            pool.dma_start(gli[:], a["s5_lam_im"][0]).then_inc(par_in, 16)
            pool.dma_start(gdt[:, 0:1], a["s5_log_dt"][0].rearrange("(g o) -> g o", o=1)).then_inc(par_in, 16)
            pool.wait_ge(wg_zero, 1)
            pool.dma_start(WG[P - GRANK:P, :], a["gla_w_gate_up"][0]).then_inc(wg_in, 16)
            done = [0]

            def split_weights(upto):
                while done[0] <= min(upto, len(plan.loads) - 1):
                    n = done[0]
                    done[0] += 1
                    at = slice(0, plan.size[n])
                    pool.wait_ge(whi_ready, n + 1)
                    pool.tensor_tensor(ring_lo[:, n % NSLOT, at], ring[:, n % NSLOT, at], ring_hi[:, n % NSLOT, at].bitcast(F32),
                                       ALU.subtract).then_inc(wlo_ready, 1)
                    pool.wait_ge(wlo_ready, n + 1)

            split_weights(tiles["gla_out"][-1].loads[0])
            split_weights(tiles["s5_u"][-1].loads[0])
            pool.wait_ge(pw_ready, 1)

            def factor(i, b):
                return PW[:, i, :, b * BG:(b + 1) * BG].rearrange("p k g -> p g k").unsqueeze(3).broadcast_to([P, BG, TB, SGRP])

            def rows(ap):
                return ap.rearrange("p (g j) -> p g j", g=BG).unsqueeze(2).broadcast_to([P, BG, TB, SGRP])

            def four(ap):
                return ap.rearrange("p g (s j) -> p g s j", s=TB)

            chain = [0]

            def link(ins):
                chain[0] += 1
                ins.then_inc(pool_chain, 1)
                pool.wait_ge(pool_chain, chain[0])

            pool.wait_ge(tile_done, tiles["s5_u"][-1].t + 1)
            for b in range(NBATCH):
                p = b % 2
                if b >= 2:
                    pool.wait_ge(y_ps, b - 1)
                pool.wait_ge(cz_sb, b + 1)
                for dst, i, j, op in ((W1[p], 0, 1, ALU.add), (W2[p], 1, 0, ALU.subtract)):
                    link(pool.tensor_tensor(four(dst[:]), factor(i, b), rows(CZ[:, p, 0:P]), ALU.mult))
                    link(pool.tensor_tensor(four(w_tmp[:]), factor(j, b), rows(CZ[:, p, P:2 * P]), ALU.mult))
                    pool.tensor_tensor(dst[:], dst[:], w_tmp[:], op).then_inc(w_ready, 1)
                    if dst is W1[p]:
                        pool.wait_ge(w_ready, 2 * b + 1)
                pool.wait_ge(w_ready, 2 * b + 2)
            split_weights(tiles["s5_out"][-1].loads[0])
            pool.wait_ge(tile_done, tiles["s5_out"][-1].t + 1)
            pool.dma_start(MT[0:NM, :], a["meta_tokens_2"]).then_inc(mt_in, 16)
            pool.dma_start(rt[:], a["rotary_constants"]).then_inc(rt_in, 16)
            split_weights(tiles["ukvv"][0].loads[0])
            pool.wait_ge(tile_done, tiles["ukvv"][-1].t + 1)
            pool.memset(PB[:], 0.0).then_inc(pb_zero, 1)
            split_weights(tiles["attn_out"][0].loads[0] + NSLOT - 1)
            for n in range(2 * MH * NPAIR):
                nk = keys(n // (2 * MH))
                p = n % 3
                pool.wait_ge(rsum_ready, n + 1)
                pool.tensor_scalar(PB[:, p, 0:nk], PB[:, p, 0:nk], mx[:, p, 3:4], None, ALU.mult).then_inc(p_ready, 1)
            pool.wait_ge(p_ready, 2 * MH * NPAIR)
            split_weights(len(plan.loads) - 1)

        def sp_program(sp):
            def factor_loads(b):
                gs = slice(b * BG, (b + 1) * BG)
                if b == 0:
                    sp.wait_ge(pw_ready, 1)
                if b >= 2:
                    sp.wait_ge(c_ps, b - 1)
                    sp.wait_ge(bf_ready, b - 1)
                here = small_in[b % 2]
                for k, name in enumerate(("s5_c_re", "s5_c_im", "s5_c_re")):
                    sp.dma_start(CN[:, b % 2, k * SP_:(k + 1) * SP_], a[name][0, gs].rearrange("g i p -> (g i) p")).then_inc(here, 16)
                for k in range(2):
                    for r, name in enumerate(("s5_b_re", "s5_b_im")):
                        rows = slice(((r + k) % 2) * SP_, ((r + k) % 2 + 1) * SP_)
                        sp.dma_start(BZ[rows, b % 2, k], a[name][0, gs].rearrange("g p j -> p g j")).then_inc(here, 16)

            def read_back(b):
                sp.wait_ge(y_out, 16 * TB * (b + 1))
                if b > 0:
                    sp.wait_ge(yd_ready, b)
                sp.dma_start(YIN, y_dram[b * P:(b + 1) * P, :]).then_inc(y_in, 16)

            def u_loads(b):
                if b + 1 < NBATCH:
                    factor_loads(b + 1)
                if b == 0:
                    sp.wait_ge(u_out, 16 * KI)
                if b >= 2:
                    sp.wait_ge(y_ps, b - 1)
                src = u_dram[b * P:(b + 1) * P, :].rearrange("(g j) (s n) -> s j g n", g=BG, s=TB)
                for s in range(TB):
                    sp.dma_start(UB[s * SGRP:(s + 1) * SGRP, b % 2], src[s]).then_inc(ub_in[b % 2], 16)
                if b >= 2:
                    read_back(b - 2)

            for tt in range(NPAIR):
                sp.dma_start(xtok[:, tt, :], a["x"][0, tt * P:(tt + 1) * P, :]).then_inc(x_in, 16)
            for n, parts in enumerate(plan.loads):
                if n >= NSLOT:
                    if n - NSLOT in HALVES:
                        sp.wait_ge(half_used, HALVES.index(n - NSLOT) + 1)
                    else:
                        sp.wait_ge(tile_done, plan.last_use[n - NSLOT] + 1)
                for src, at, shape, *cols in parts:
                    dst = slot_view(n, shape, at)
                    sp.dma_start(dst[:, :, cols[0]] if cols else dst, src).then_inc(landed[n % NSLOT], 16)
                if n == tiles["s5_z"][0].loads[0] - 1:
                    factor_loads(0)
                    for b in range(2):
                        u_loads(b)
                if n == tiles["s5_z"][0].loads[0] + NSLOT - 1:
                    for b in range(2, NBATCH):
                        u_loads(b)
                    read_back(NBATCH - 2)
                    read_back(NBATCH - 1)
            for tt in range(NPAIR):
                sp.wait_ge(ot_sb, tt + 1)
                sp.dma_start(out[0, tt * P:(tt + 1) * P, :], OT[:, tt, :]).then_inc(out_done, 16)
            sp.wait_ge(out_done, 16 * NPAIR)

        block = ctx.enter_context(nc.Block())

        @block.tensor
        def _(pe):
            pe_program(pe)

        @block.scalar
        def _(act):
            act_program(act)

        @block.vector
        def _(dve):
            dve_program(dve)

        @block.gpsimd
        def _(pool):
            pool_program(pool)

        @block.sync
        def _(sp):
            sp_program(sp)


def kernel(**inputs):
    import concourse.bacc as bacc
    from concourse.bass_utils import run_bass_kernel_spmd

    nc = bacc.Bacc("TRN2", target_bir_lowering=False, num_devices=1)
    arrays = {f"in_{name}": np.ascontiguousarray(value) for name, value in inputs.items()}
    arrays["in_shape_constants"] = shape_constants()
    arrays["in_chunk_constants"] = chunk_constants()
    arrays["in_rotary_constants"] = rotary_constants()
    a = {name[3:]: nc.dram_tensor(name, value.shape, mybir.dt.from_np(value.dtype), kind="ExternalInput").ap()
         for name, value in arrays.items()}
    out = nc.dram_tensor("out_0_dram", (1, T, D), F32, kind="ExternalOutput").ap()
    build(nc, a, out)
    r = run_bass_kernel_spmd(nc, [arrays], core_ids=[0])
    return r.results[0]["out_0_dram"]
```
